# Optimizing a Trainium2 kernel written in Bass

```python
import jax, jax.numpy as jnp
from jax import lax
import numpy as np

D_MODEL = 2048
BATCH = 1
SEQ = 256
DEPTH = 1
DEC_BATCH = 8
DEC_SEQ = 8
PAST_LEN = 2048
PAGE_SIZE = 128

N_HEADS = 16
N_KV = 4
HPG = N_HEADS // N_KV
HEAD_DIM = 64
ROPE_DIM = HEAD_DIM // 4
ROPE_THETA = 500000.0
BLOCK = 64
N_SEL = 16
WINDOW = 512
Q_BLOCK = 16
RW_HEADS = 16
RW_HEAD = 64
RW_DIM = RW_HEADS * RW_HEAD
LORA_W = 64
LORA_A = 64
LN_X_EPS = 64e-5
D_FF = 5632
CONV_W = 3
NORM_EPS = 1e-6

ATT_DIM = N_HEADS * HEAD_DIM
KV_COLS = 2 * N_KV * HEAD_DIM
SHIFT_COLS = 3 * RW_DIM + LORA_W + LORA_A
PROJ_SIZES = (ATT_DIM, KV_COLS, KV_COLS, KV_COLS, 3 * N_HEADS, SHIFT_COLS, 2 * D_MODEL)
RWKV_SIZES = (RW_DIM, RW_DIM, RW_DIM, LORA_W, LORA_A)
PROJ_COLS = ATT_DIM + 3 * KV_COLS + 3 * N_HEADS + SHIFT_COLS + 2 * D_MODEL
NEG = -1e30

kernel_name = 'nsa_rwkv7_convffn_hybrid_step'

def _splits(sizes):
    return [int(v) for v in np.cumsum(np.array(sizes))[:-1]]

def rms_norm(x, gain):
    xf = x.astype(jnp.float32)
    y = xf * lax.rsqrt(jnp.mean(xf * xf, axis=-1, keepdims=True) + NORM_EPS)
    return (y * gain.astype(jnp.float32)).astype(x.dtype)

def partial_rope(x, pos):
    half = ROPE_DIM // 2
    inv = ROPE_THETA ** (-jnp.arange(half, dtype=jnp.float32) * 2.0 / ROPE_DIM)
    ang = pos.astype(jnp.float32)[:, None] * inv[None, :]
    cos = jnp.cos(ang)[None, :, None, :]
    sin = jnp.sin(ang)[None, :, None, :]
    xf = x[..., :ROPE_DIM].astype(jnp.float32)
    x1, x2 = xf[..., :half], xf[..., half:]
    rot = jnp.concatenate([x1 * cos - x2 * sin, x2 * cos + x1 * sin], axis=-1).astype(x.dtype)
    return jnp.concatenate([rot, x[..., ROPE_DIM:]], axis=-1)

def masked_softmax(s, mask, axes):
    s = jnp.where(mask, s.astype(jnp.float32), NEG)
    m = jnp.max(s, axis=axes, keepdims=True)
    e = jnp.where(mask, jnp.exp(s - m), 0.0)
    return e / jnp.maximum(jnp.sum(e, axis=axes, keepdims=True), 1e-30)

def kv_rows(p, gain_k, pos):
    B, T = p.shape[:2]
    kv = p.reshape(B, T, 2, N_KV, HEAD_DIM)
    k = partial_rope(rms_norm(kv[:, :, 0], gain_k), pos)
    return jnp.stack([k, kv[:, :, 1]], axis=2)

def compress(kv_blocks, w_cmp):
    return jnp.einsum('bnlcgd,cld->bncgd', kv_blocks, w_cmp.astype(kv_blocks.dtype))

def mixer_inputs(x, pos, norm_g, w_in, q_gain, k_gains):
    B, T = x.shape[:2]
    p = rms_norm(x, norm_g) @ w_in
    p_q, p_cmp, p_sel, p_win, p_gate, p_shift, p_merge = jnp.split(p, _splits(PROJ_SIZES), axis=-1)
    q = partial_rope(rms_norm(p_q.reshape(B, T, N_HEADS, HEAD_DIM), q_gain), pos)
    kv_cmp = kv_rows(p_cmp, k_gains[0], pos)
    kv_sel = kv_rows(p_sel, k_gains[1], pos)
    kv_win = kv_rows(p_win, k_gains[2], pos)
    gates = jax.nn.sigmoid(p_gate.reshape(B, T, N_HEADS, 3))
    return q, kv_cmp, kv_sel, kv_win, gates, p_shift, p_merge

def nsa_core(q, pos_q, kc, vc, gather_sel, kw, vw, pos_kw, gates):
    B, Q = q.shape[:2]
    scale = HEAD_DIM ** -0.5
    qg = q.reshape(B, Q, N_KV, HPG, HEAD_DIM)
    nb = kc.shape[1]
    blk = jnp.arange(nb, dtype=jnp.int32)
    s_c = jnp.einsum('bqghd,bngd->bqghn', qg, kc) * scale
    vis = ((blk + 1) * BLOCK - 1)[None, :] <= pos_q[:, None]
    p_c = masked_softmax(s_c, vis[None, :, None, None, :], (-1,))
    o_c = jnp.einsum('bqghn,bngd->bqghd', p_c.astype(vc.dtype), vc)
    cur = pos_q // BLOCK
    cand = (blk[None, :] < cur[:, None])[None, :, None, :]
    imp = jnp.where(cand, jnp.sum(p_c, axis=3), -1.0)
    _, top = lax.top_k(imp, min(N_SEL - 1, nb))
    cur_b = jnp.broadcast_to(cur[None, :, None, None], (B, Q, N_KV, 1))
    idx = jnp.concatenate([top.astype(jnp.int32), cur_b], axis=-1)
    valid = jnp.concatenate([top < cur_b, jnp.ones(cur_b.shape, dtype=bool)], axis=-1)
    ks, vs = gather_sel(idx)
    kpos = idx[..., None] * BLOCK + jnp.arange(BLOCK, dtype=jnp.int32)
    m_s = valid[..., None] & (kpos <= pos_q[None, :, None, None, None])
    s_s = jnp.einsum('bqghd,bqgkld->bqghkl', qg, ks) * scale
    p_s = masked_softmax(s_s, m_s[:, :, :, None], (-2, -1))
    o_s = jnp.einsum('bqghkl,bqgkld->bqghd', p_s.astype(vs.dtype), vs)
    dist = pos_q[:, None] - pos_kw[None, :]
    m_w = (dist >= 0) & (dist <= WINDOW) & (pos_kw >= 0)[None, :]
    s_w = jnp.einsum('bqghd,bkgd->bqghk', qg, kw) * scale
    p_w = masked_softmax(s_w, m_w[None, :, None, None, :], (-1,))
    o_w = jnp.einsum('bqghk,bkgd->bqghd', p_w.astype(vw.dtype), vw)
    g = gates.reshape(B, Q, N_KV, HPG, 3)
    o = g[..., 0:1] * o_c + g[..., 1:2] * o_s + g[..., 2:3] * o_w
    return o.reshape(B, Q, ATT_DIM)

def nsa_prompt(q, kv_cmp, kv_sel, kv_win, gates, w_cmp):
    B, T = q.shape[:2]
    nb = T // BLOCK
    blk_shape = (B, nb, BLOCK, 2, N_KV, HEAD_DIM)
    summ = compress(kv_cmp.reshape(blk_shape), w_cmp)
    sel_blocks = kv_sel.reshape(blk_shape)
    bi = jnp.arange(B)[:, None, None, None]
    gi = jnp.arange(N_KV)[None, None, :, None]

    def gather_sel(idx):
        kv = sel_blocks[bi, idx, :, :, gi, :]
        return kv[..., 0, :], kv[..., 1, :]

    win_pad = jnp.pad(kv_win, ((0, 0), (WINDOW, 0), (0, 0), (0, 0), (0, 0)))

    def chunk(c):
        q0 = c * Q_BLOCK
        qc = lax.dynamic_slice_in_dim(q, q0, Q_BLOCK, axis=1)
        gc = lax.dynamic_slice_in_dim(gates, q0, Q_BLOCK, axis=1)
        kwc = lax.dynamic_slice_in_dim(win_pad, q0, WINDOW + Q_BLOCK, axis=1)
        pos_q = q0 + jnp.arange(Q_BLOCK, dtype=jnp.int32)
        pos_kw = q0 - WINDOW + jnp.arange(WINDOW + Q_BLOCK, dtype=jnp.int32)
        return nsa_core(qc, pos_q, summ[:, :, 0], summ[:, :, 1], gather_sel,
                        kwc[:, :, 0], kwc[:, :, 1], pos_kw, gc)

    out = lax.map(chunk, jnp.arange(T // Q_BLOCK, dtype=jnp.int32))
    y = jnp.transpose(out, (1, 0, 2, 3)).reshape(B, T, ATT_DIM)
    return y, kv_win[:, T - min(WINDOW, T):]

def nsa_sample(q, kv_cmp, kv_sel, kv_win, gates, pos, pool_cmp, pool_sel, page_table, win_buf, w_cmp, layer):
    DB, T = q.shape[:2]
    nbp = PAST_LEN // BLOCK
    bpp = PAGE_SIZE // BLOCK
    past_c = pool_cmp[layer, page_table].reshape(DB, nbp, BLOCK, 2, N_KV, HEAD_DIM)
    nfull = T // BLOCK
    new_c = kv_cmp[:, :nfull * BLOCK].reshape(DB, nfull, BLOCK, 2, N_KV, HEAD_DIM)
    summ = jnp.concatenate([compress(past_c, w_cmp), compress(new_c.astype(past_c.dtype), w_cmp)], axis=1)
    nbn = -(-T // BLOCK)
    new_s = jnp.pad(kv_sel, ((0, 0), (0, nbn * BLOCK - T), (0, 0), (0, 0), (0, 0)))
    new_s = new_s.reshape(DB, nbn, BLOCK, 2, N_KV, HEAD_DIM)
    pool = pool_sel.reshape(pool_sel.shape[0], pool_sel.shape[1], bpp, BLOCK, 2, N_KV, HEAD_DIM)
    bi = jnp.arange(DB)[:, None, None, None]
    gi = jnp.arange(N_KV)[None, None, :, None]

    def gather_sel(idx):
        pidx = jnp.minimum(idx, nbp - 1)
        phys = page_table[bi, pidx // bpp]
        past = pool[layer, phys, pidx % bpp, :, :, gi, :]
        new = new_s[bi, jnp.clip(idx - nbp, 0, nbn - 1), :, :, gi, :]
        kv = jnp.where((idx < nbp)[..., None, None, None], past, new.astype(past.dtype))
        return kv[..., 0, :], kv[..., 1, :]

    keep = win_buf.shape[1]
    kw = jnp.concatenate([win_buf.astype(kv_win.dtype), kv_win], axis=1)
    pos_kw = PAST_LEN - keep + jnp.arange(keep + T, dtype=jnp.int32)
    y = nsa_core(q, pos, summ[:, :, 0], summ[:, :, 1], gather_sel, kw[:, :, 0], kw[:, :, 1], pos_kw, gates)
    return y, kw[:, T:]

def wkv_scan(r, decay, k, v, kk, a, s0):
    def step(S, inp):
        r_t, w_t, k_t, v_t, kk_t, a_t = inp
        sa = jnp.einsum('bhvk,bhk->bhv', S, kk_t)
        S = (S * w_t[:, :, None, :] - sa[..., None] * (kk_t * a_t)[:, :, None, :]
             + v_t[..., None] * k_t[:, :, None, :])
        return S, jnp.einsum('bhvk,bhk->bhv', S, r_t)
    xs = tuple(jnp.swapaxes(t, 0, 1) for t in (r, decay, k, v, kk, a))
    S, ys = lax.scan(step, s0, xs)
    return jnp.swapaxes(ys, 0, 1), S

def rwkv_branch(p_shift, shift_prev, s0, mu, w0, w_lora_w, a0, w_lora_a, k_k, k_a, r_k, ln_w, ln_b):
    B, T = p_shift.shape[:2]
    f32 = jnp.float32
    prev = jnp.concatenate([shift_prev[:, None].astype(p_shift.dtype), p_shift[:, :-1]], axis=1)
    z = p_shift + (prev - p_shift) * mu
    r, k, v, xw, xa = jnp.split(z, _splits(RWKV_SIZES), axis=-1)
    wl = -jax.nn.softplus(-(w0 + jnp.tanh(xw) @ w_lora_w).astype(f32)) - 0.5
    decay = jnp.exp(-jnp.exp(wl))
    a = jax.nn.sigmoid((a0 + xa @ w_lora_a).astype(f32))

    def heads(t):
        return t.astype(f32).reshape(t.shape[:-1] + (RW_HEADS, RW_HEAD))

    r, k, v, decay, a = heads(r), heads(k), heads(v), heads(decay), heads(a)
    kk = k * heads(k_k)
    kk = kk * lax.rsqrt(jnp.maximum(jnp.sum(kk * kk, axis=-1, keepdims=True), 1e-24))
    k = k * (1.0 + (a - 1.0) * heads(k_a))
    y, s_new = wkv_scan(r, decay, k, v, kk, a, s0.astype(f32))
    mean = jnp.mean(y, axis=-1, keepdims=True)
    var = jnp.mean(jnp.square(y - mean), axis=-1, keepdims=True)
    y = (y - mean) * lax.rsqrt(var + LN_X_EPS) * heads(ln_w) + heads(ln_b)
    y = y + jnp.sum(r * k * heads(r_k), axis=-1, keepdims=True) * v
    return y.reshape(B, T, RW_DIM).astype(p_shift.dtype), s_new.astype(s0.dtype), p_shift[:, -1]

def merge_out(x, o_att, y_rw, p_merge, w_a, w_b, w_o):
    g_a, g_b = jnp.split(p_merge, 2, axis=-1)
    m = jax.nn.sigmoid(g_a) * (o_att @ w_a) + jax.nn.sigmoid(g_b) * (y_rw @ w_b)
    return x + m @ w_o

def conv_ffn(h, conv_prev, norm_g, w_up, conv_w, conv_b, w_down):
    T = h.shape[1]
    u = rms_norm(h, norm_g) @ w_up
    up = jnp.concatenate([conv_prev.astype(u.dtype), u], axis=1)
    c = conv_b
    for j in range(CONV_W):
        c = c + conv_w[j] * up[:, j:j + T]
    gate, val = jnp.split(c, 2, axis=-1)
    return h + (jax.nn.silu(gate) * val) @ w_down, up[:, T:]

def setup_inputs(seed: int = 0) -> dict:
    key = jax.random.key(seed)
    ks = jax.random.split(key, 40)
    f32 = jnp.float32

    def nrm(i, shape, scale):
        return jax.random.normal(ks[i], shape, f32) * scale

    def gain(i, shape):
        return 1.0 + 0.1 * jax.random.normal(ks[i], shape, f32)

    n_pages = PAST_LEN // PAGE_SIZE
    n_used = DEC_BATCH * n_pages
    n_pool = n_used + (n_used + 3) // 4
    page_table = jax.random.permutation(ks[4], n_pool)[:n_used].reshape(DEC_BATCH, n_pages).astype(jnp.int32)
    win_keep = min(WINDOW, PAST_LEN)
    pool_shape = (DEPTH, n_pool, PAGE_SIZE, 2, N_KV, HEAD_DIM)
    L = (DEPTH,)
    return {
        'x_prompt': nrm(0, (BATCH, SEQ, D_MODEL), 1.0),
        'x_sample': nrm(1, (DEC_BATCH, DEC_SEQ, D_MODEL), 1.0),
        'cache_kv_cmp': nrm(2, pool_shape, 1.0),
        'cache_kv_sel': nrm(3, pool_shape, 1.0),
        'page_table': page_table,
        'cache_kv_win': nrm(5, L + (DEC_BATCH, win_keep, 2, N_KV, HEAD_DIM), 1.0),
        'state_wkv': nrm(6, L + (DEC_BATCH, RW_HEADS, RW_HEAD, RW_HEAD), 0.3),
        'state_shift': nrm(7, L + (DEC_BATCH, SHIFT_COLS), 1.0),
        'state_conv': nrm(8, L + (DEC_BATCH, CONV_W - 1, 2 * D_FF), 1.0),
        'norm1_g': gain(9, L + (D_MODEL,)),
        'w_in': nrm(10, L + (D_MODEL, PROJ_COLS), D_MODEL ** -0.5),
        'q_gain': gain(11, L + (HEAD_DIM,)),
        'k_gains': gain(12, L + (3, HEAD_DIM)),
        'w_cmp': (1.0 + nrm(13, L + (2, BLOCK, HEAD_DIM), 0.2)) * BLOCK ** -0.5,
        'mu_shift': jax.random.uniform(ks[14], L + (SHIFT_COLS,), f32),
        'w0': -2.5 + nrm(15, L + (RW_DIM,), 1.5),
        'w_lora_w': nrm(16, L + (LORA_W, RW_DIM), 0.5 * LORA_W ** -0.5),
        'a0': nrm(17, L + (RW_DIM,), 0.1),
        'w_lora_a': nrm(18, L + (LORA_A, RW_DIM), 0.5 * LORA_A ** -0.5),
        'k_k': 0.85 + nrm(19, L + (RW_DIM,), 0.05),
        'k_a': 1.0 + nrm(20, L + (RW_DIM,), 0.05),
        'r_k': nrm(21, L + (RW_DIM,), 0.1),
        'ln_x_w': gain(22, L + (RW_DIM,)),
        'ln_x_b': nrm(23, L + (RW_DIM,), 0.02),
        'w_branch_a': nrm(24, L + (ATT_DIM, D_MODEL), ATT_DIM ** -0.5),
        'w_branch_b': nrm(25, L + (RW_DIM, D_MODEL), RW_DIM ** -0.5),
        'w_out': nrm(26, L + (D_MODEL, D_MODEL), D_MODEL ** -0.5),
        'norm2_g': gain(27, L + (D_MODEL,)),
        'w_up': nrm(28, L + (D_MODEL, 2 * D_FF), D_MODEL ** -0.5),
        'conv_w': nrm(29, L + (CONV_W, 2 * D_FF), CONV_W ** -0.5),
        'conv_b': nrm(30, L + (2 * D_FF,), 0.02),
        'w_down': nrm(31, L + (D_FF, D_MODEL), D_FF ** -0.5),
    }

def reference(x_prompt, x_sample, cache_kv_cmp, cache_kv_sel, page_table, cache_kv_win, state_wkv,
              state_shift, state_conv, norm1_g, w_in, q_gain, k_gains, w_cmp, mu_shift, w0, w_lora_w,
              a0, w_lora_a, k_k, k_a, r_k, ln_x_w, ln_x_b, w_branch_a, w_branch_b, w_out, norm2_g,
              w_up, conv_w, conv_b, w_down):
    B, T = x_prompt.shape[:2]
    DB, TS = x_sample.shape[:2]
    pos_p = jnp.arange(T, dtype=jnp.int32)
    pos_s = PAST_LEN + jnp.arange(TS, dtype=jnp.int32)
    h_p, h_s = x_prompt, x_sample
    kvc_p, kvc_s, kvs_p, kvs_s, kvw_p, kvw_s = [], [], [], [], [], []
    wkv_p, wkv_s, sh_p, sh_s, cv_p, cv_s = [], [], [], [], [], []
    for l in range(DEPTH):
        rw = (mu_shift[l], w0[l], w_lora_w[l], a0[l], w_lora_a[l], k_k[l], k_a[l], r_k[l], ln_x_w[l], ln_x_b[l])
        q, kv_cmp, kv_sel, kv_win, gates, p_shift, p_merge = mixer_inputs(h_p, pos_p, norm1_g[l], w_in[l], q_gain[l], k_gains[l])
        o_att, win_new = nsa_prompt(q, kv_cmp, kv_sel, kv_win, gates, w_cmp[l])
        y_rw, s_new, sh_new = rwkv_branch(p_shift, jnp.zeros((B, SHIFT_COLS), p_shift.dtype),
                                          jnp.zeros((B, RW_HEADS, RW_HEAD, RW_HEAD), jnp.float32), *rw)
        h_p = merge_out(h_p, o_att, y_rw, p_merge, w_branch_a[l], w_branch_b[l], w_out[l])
        h_p, cv_new = conv_ffn(h_p, jnp.zeros((B, CONV_W - 1, 2 * D_FF), h_p.dtype), norm2_g[l],
                               w_up[l], conv_w[l], conv_b[l], w_down[l])
        kvc_p.append(kv_cmp)
        kvs_p.append(kv_sel)
        kvw_p.append(win_new)
        wkv_p.append(s_new)
        sh_p.append(sh_new)
        cv_p.append(cv_new)
        q, kv_cmp, kv_sel, kv_win, gates, p_shift, p_merge = mixer_inputs(h_s, pos_s, norm1_g[l], w_in[l], q_gain[l], k_gains[l])
        o_att, win_new = nsa_sample(q, kv_cmp, kv_sel, kv_win, gates, pos_s, cache_kv_cmp, cache_kv_sel,
                                    page_table, cache_kv_win[l], w_cmp[l], l)
        y_rw, s_new, sh_new = rwkv_branch(p_shift, state_shift[l], state_wkv[l], *rw)
        h_s = merge_out(h_s, o_att, y_rw, p_merge, w_branch_a[l], w_branch_b[l], w_out[l])
        h_s, cv_new = conv_ffn(h_s, state_conv[l], norm2_g[l], w_up[l], conv_w[l], conv_b[l], w_down[l])
        kvc_s.append(kv_cmp)
        kvs_s.append(kv_sel)
        kvw_s.append(win_new)
        wkv_s.append(s_new)
        sh_s.append(sh_new)
        cv_s.append(cv_new)
    return (h_p, h_s, jnp.stack(kvc_p), jnp.stack(kvc_s), jnp.stack(kvs_p), jnp.stack(kvs_s),
            jnp.stack(kvw_p), jnp.stack(kvw_s), jnp.stack(wkv_p), jnp.stack(wkv_s),
            jnp.stack(sh_p), jnp.stack(sh_s), jnp.stack(cv_p), jnp.stack(cv_s))


_drawn_inputs = setup_inputs


def setup_inputs(seed=0):
    import zlib

    import numpy as np

    out = dict(_drawn_inputs(seed))
    spreads = {}
    factors = {'cache_kv_sel': 3.957, 'q_gain': 4.654, 'ln_x_b': 5.828, 'conv_b': 4.249}
    for name, (base, spread) in spreads.items():
        noise = np.random.default_rng([zlib.crc32(name.encode()), seed]).standard_normal(out[name].shape)
        drawn = base * np.exp(spread * noise) if base else spread * noise
        out[name] = __import__('jax').numpy.asarray(drawn.astype(out[name].dtype))
    for name, factor in factors.items():
        out[name] = (out[name] * factor).astype(out[name].dtype)
    return out
```

```python
from contextlib import ExitStack

import numpy as np

import concourse.bass as bass
from concourse import mybir

F32 = mybir.dt.float32
I32 = mybir.dt.int32
ALU = mybir.AluOpType
ACT = mybir.ActivationFunctionType
AX = mybir.AxisListType
ds = bass.ds

DM = 2048
T = 256
DB = 8
TS = 8
PAST = 2048
PAGE = 128
NH = 16
NKV = 4
HPG = NH // NKV
HD = 64
ROPE = HD // 4
THETA = 500000.0
BLOCK = 64
NSEL = 16
WIN = 512
RW = 1024
LORA = 64
LNX_EPS = 64e-5
DFF = 5632
EPS = 1e-6
NEG = -1e30

P = 128
NS = DB * TS
NT = T + NS
ATT = NH * HD
KVC = 2 * NKV * HD
SHIFT = 3 * RW + 2 * LORA
C_GATE = ATT + 3 * KVC
C_SHIFT = C_GATE + 3 * NH
C_MERGE = C_SHIFT + SHIFT
KD = DM // P
NPG = PAST // PAGE
NBLK = PAST // BLOCK
TOK = [(0, 128), (128, 128), (256, 64)]
NP_BLK = T // BLOCK
CH = 16
NEW0 = PAST

CONST = {}


def _const_layout():
    at = 0
    for name, n in (("ident", 128), ("halves", 128), ("group", 128), ("blocksum", 62), ("rope", 48),
                    ("causal", 256), ("newmask", 8), ("winmask", 8), ("earlier", 1024), ("vis", 16),
                    ("gram", 1024), ("nmask", 256), ("chunk", 16), ("reset", 320), ("eps", 4), ("ones", 128)):
        CONST[name] = (at, n)
        at += n
    return at


NCONST = _const_layout()


def shape_constants():
    c = np.zeros((P, NCONST), np.float32)

    def put(name, v):
        a, n = CONST[name]
        v = np.asarray(v, np.float32)
        c[:, a:a + n] = v.reshape(v.shape[0], n)

    p = np.arange(P)
    put("ident", np.eye(P))
    put("halves", (p[:, None] // 64 == p[None, :] // 64))
    g, q = p // 32, p % 8
    put("group", (g[:, None] == g[None, :]) & (q[:, None] == q[None, :]))
    put("blocksum", np.arange(62)[None, :] == 30 + p[:, None] // BLOCK)
    inv = np.float32(THETA) ** (-np.arange(ROPE // 2, dtype=np.float32) * np.float32(2.0) / np.float32(ROPE))
    pos = np.zeros((P, 3), np.float32)
    pos[:, 0], pos[:, 1] = p, 128 + p
    pos[:, 2] = PAST + p % TS
    ang = (pos[:, :, None] * inv.astype(np.float32)).astype(np.float32)
    put("rope", np.stack([np.cos(ang.astype(np.float64)), np.sin(ang.astype(np.float64))], 2))
    m = np.zeros((P, 256))
    m[:, 128:] = np.where(p[None, :] <= p[:, None], 0, NEG)
    put("causal", m)
    put("newmask", np.where(np.arange(8)[None, :] <= q[:, None], 0, NEG))
    put("winmask", np.where(np.arange(8)[None, :] >= q[:, None], 0, NEG))
    i = np.arange(NBLK)
    put("earlier", np.broadcast_to(i[None, :] < i[:, None], (P, NBLK, NBLK)))
    b4 = np.arange(NP_BLK)
    vis = np.stack([((b4[None, :] + 1) * BLOCK - 1 <= p[:, None] + 128 * t) for t in range(2)], 1)
    put("vis", np.stack([vis, np.where(vis, 0, NEG)], 2))
    s, t = p[:, None], p[None, :]
    sets, nm = [], []
    for size, top in ((CH, 128), (TS, 64)):
        same = (s // size == t // size) & (s < top) & (t < top)
        strict, incl = same & (s < t), same & (s <= t)
        sets.append(np.stack([-1.0 * strict, -1.0 * incl, strict, incl], 1))
        nm.append(-1.0 * (same & (t < s)))
    put("gram", np.stack(sets, 1))
    put("nmask", np.stack(nm, 1))
    put("chunk", np.stack([p[:, None] // CH == np.arange(8)[None], p[:, None] // TS == np.arange(8)[None]], 1))
    r = np.ones(320)
    r[0:256:CH] = 0
    r[256::TS] = 0
    put("reset", np.broadcast_to(r, (P, 320)))
    put("eps", np.broadcast_to([EPS, LNX_EPS, 0, 0], (P, 4)))
    put("ones", np.ones((P, 128)))
    return c


VEC = {}
_at = 0
for _n, _r in (("norm1_g", 16), ("norm2_g", 16), ("mu_shift", 25), ("w0", 8), ("a0", 8), ("k_k", 8), ("k_a", 8),
               ("r_k", 8), ("ln_x_w", 8), ("ln_x_b", 8)):
    VEC[_n] = (_at, _r)
    _at += _r
NVEC = _at


class Steps:

    def __init__(self, sem, names):
        self.sem, self.names, self.cursor = sem, list(names), 0

    def done(self, name, ins):
        assert self.names[self.cursor] == name, (self.names[self.cursor], name)
        self.cursor += 1
        ins.then_inc(self.sem, 1)

    def turn(self):
        assert self.cursor == len(self.names), self.names[self.cursor:]
        self.cursor = 0

    def start(self, eng):
        eng.sem_inc(self.sem, 1)

    def at(self, name, turn=0):
        return turn * len(self.names) + (self.names.index(name) + 2)

    def before(self, turn):
        return turn * len(self.names) + 1


class Chain:

    def __init__(self, eng, sem):
        self.eng, self.sem, self.n, self.base = eng, sem, 0, 0

    def __call__(self, ins):
        self.n += 1
        ins.then_inc(self.sem, 1)
        self.eng.wait_ge(self.sem, self.base + self.n)

    def body(self, turn, per_turn):
        self.start, self.base, self.per = (self.n, 0, per_turn) if False else (self.n, turn * per_turn, per_turn)

    def end(self, turns):
        assert self.n - self.start == self.per, (self.n - self.start, self.per)
        self.n = self.start + self.per * turns
        self.base = 0


def build_layer(nc, a, o):
    top = ExitStack()
    with top:
        _layer(nc, a, o, top)


def _layer(nc, a, o, top):
    def sb(name, shape, dt=F32):
        return top.enter_context(nc.sbuf_tensor(name, shape, dt))

    def sem(name):
        return top.enter_context(nc.semaphore(name))

    def settled(eng):
        eng.sem_inc(passed, 1)

    const_in = sem("const_in")
    passed = sem("passed")

    cst = sb("cst", [P, NCONST])
    vecs = sb("vecs", [P, NVEC])
    conv = sb("conv", [P, 4, 88])
    gains = sb("gains", [P, 4, HD])
    xT = sb("xT", [P, KD, NT])
    nT = sb("nT", [P, KD, NT])
    ring = sb("ring", [P, 4, 4096])
    work = sb("work", [P, 19680])
    oT = sb("oT", [P, 8, NT])
    bank = [top.enter_context(nc.psum_tensor(f"bank{i}", [P, 512], F32)) for i in range(8)]

    def const(name, *shape):
        at, n = CONST[name]
        v = cst[:, at:at + n]
        if len(shape) == 2:
            v = v.rearrange("p (a b) -> p a b", b=shape[1])
        if len(shape) == 3:
            v = v.rearrange("p (a b c) -> p a b c", b=shape[1], c=shape[2])
        return v

    def vec(name, t):
        return vecs[:, VEC[name][0] + t:VEC[name][0] + t + 1]

    class Carve:
        def __init__(self, region, at=0):
            self.region, self.at = region, at

        def __call__(self, *shape, dt=F32):
            n = int(np.prod(shape))
            v = self.region[:, self.at:self.at + n]
            self.at += n
            assert self.at <= self.region.shape[1], (self.at, self.region.shape)
            if len(shape) == 2:
                v = v.rearrange("p (a b) -> p a b", b=shape[1])
            if len(shape) == 3:
                v = v.rearrange("p (a b c) -> p a b c", b=shape[1], c=shape[2])
            if len(shape) == 4:
                v = v.rearrange("p (a b c d) -> p a b c d", b=shape[1], c=shape[2], d=shape[3])
            return v

    ringflat = ring[:, :, :].rearrange("p a b -> p (a b)")
    ident = const("ident")
    win_stores = sem("win_stores")

    def load_and_norm():
        w = Carve(work)
        xin = w(3, DM)
        vrow = w(P)
        crow = w(4, P)
        sq = w(2, NT)
        rms = w(NT)
        rstd = w(NT)
        grow = w(4 * HD)
        vec_in, x_in = sem("vec_in"), sem("x_in")
        vec_t, vec_got, x_t, x_got = sem("vec_t"), sem("vec_got"), sem("x_t"), sem("x_got")
        squared, summed, rooted, inverted, normed = (sem(f"n1_{n}") for n in "abcde")
        with nc.Block() as block:
            @block.sync
            def _(sp):
                sp.dma_start(cst[:, :], a["shape_constants"]).then_inc(const_in, 16)
                for t, (t0, n) in enumerate(TOK):
                    src = a["x_prompt"][0, t0:t0 + n, :] if t < 2 else a["x_sample"].rearrange("b t d -> (b t) d")
                    sp.dma_start(xin[0:n, t, :], src).then_inc(x_in, 16)

            @block.scalar
            def _(act):
                for name, (r0, n) in VEC.items():
                    act.dma_start(vrow[r0:r0 + n, :], a[name].rearrange("l (t p) -> (l t) p", p=P)).then_inc(vec_in, 16)
                cw = a["conv_w"].rearrange("l w (t p) -> (l w) t p", p=P)
                for j in range(3):
                    act.dma_start(crow[0:88, j, :], cw[j]).then_inc(vec_in, 16)
                act.dma_start(crow[0:88, 3, :], a["conv_b"].rearrange("l (t p) -> (l t) p", p=P)).then_inc(vec_in, 16)
                act.dma_start(grow[0:1, 0:HD], a["q_gain"]).then_inc(vec_in, 16)
                act.dma_start(grow[0:1, HD:4 * HD], a["k_gains"].rearrange("l a d -> l (a d)")).then_inc(vec_in, 16)
                act.wait_ge(vec_t, 1)
                nc.scalar.copy(vecs[:, :], bank[7][:, 0:NVEC]).then_inc(vec_got, 1)
                nc.scalar.copy(conv[:, :, :], bank[6][:, 0:352].rearrange("p (a b) -> p a b", b=88)).then_inc(vec_got, 1)
                nc.scalar.copy(gains[:, :, :], bank[5][:, 0:256].rearrange("p (a b) -> p a b", b=HD)).then_inc(vec_got, 1)
                for k in range(KD):
                    act.wait_ge(x_t, k + 1)
                    nc.scalar.copy(xT[:, k, :], bank[k % 4][:, 0:NT]).then_inc(x_got, 1)
                act.wait_ge(summed, 1)
                nc.scalar.activation(rms, bank[4][:, 0:NT], ACT.Sqrt, bias=const("eps")[:, 0:1], scale=1.0 / DM).then_inc(rooted, 1)

            @block.tensor
            def _(pe):
                pe.wait_ge(const_in, 16)
                pe.wait_ge(vec_in, 16 * (len(VEC) + 6))
                nc.tensor.transpose(bank[7][:, 0:NVEC], vrow[0:NVEC, :], ident[0:NVEC, 0:NVEC])
                for j in range(4):
                    nc.tensor.transpose(bank[6][:, 88 * j:88 * j + 88], crow[0:88, j, :], ident[0:88, 0:88])
                nc.tensor.matmul(bank[5][:, 0:256], const("ones")[0:1, :], grow[0:1, :], start=True, stop=True).then_inc(vec_t, 1)
                pe.wait_ge(x_in, 48)
                for k in range(KD):
                    if k >= 4:
                        pe.wait_ge(x_got, k - 3)
                    for t, (t0, n) in enumerate(TOK):
                        last = nc.tensor.transpose(bank[k % 4][:, t0:t0 + n], xin[0:n, t, k * P:(k + 1) * P], ident[0:n, 0:n])
                    last.then_inc(x_t, 1)
                for k in range(KD):
                    pe.wait_ge(squared, k + 1)
                    last = nc.tensor.matmul(bank[4][:, 0:NT], const("ones"), sq[:, k % 2, :], start=k == 0, stop=k == KD - 1)
                    last.then_inc(summed_each, 1)
                pe.wait_ge(summed_each, KD)
                pe.sem_inc(summed, 1)

            @block.vector
            def _(dve):
                for k in range(KD):
                    dve.wait_ge(x_got, k + 1)
                    if k >= 2:
                        dve.wait_ge(summed_each, k - 1)
                    nc.vector.tensor_tensor(sq[:, k % 2, :], xT[:, k, :], xT[:, k, :], ALU.mult).then_inc(squared, 1)
                dve.wait_ge(rooted, 1)
                nc.vector.reciprocal(rstd, rms).then_inc(inverted, 1)
                dve.wait_ge(inverted, 1)
                dve.wait_ge(vec_got, 3)
                for k in range(KD):
                    nc.vector.scalar_tensor_tensor(out=nT[:, k, :], in0=xT[:, k, :], scalar=vec("norm1_g", k), in1=rstd,
                                                   op0=ALU.mult, op1=ALU.mult).then_inc(normed, 1)

    summed_each = sem("summed_each")
    load_and_norm()

    w = Carve(work)
    pkv = w(3, ATT + 3 * KVC)
    gates = w(3, 48)
    chunk_in = [sem(f"chunk_in{i}") for i in range(4)]

    def project_qkv():
        sqr = ringflat[:, 0:1792].rearrange("p (a b) -> p a b", b=HD)
        rr = Carve(ringflat, 1792)
        ss = rr(28)
        rt = rr(28)
        rs = rr(28)
        rope = rr(4, 16, 8)
        used, made, taken = sem("qkv_used"), sem("qkv_made"), sem("qkv_taken")
        norm_sq, rooted, ready, stored = sem("qkv_sq"), sem("qkv_root"), sem("qkv_ready"), sem("qkv_stored")
        wv = a["w_in"].rearrange("l (k p) c -> p (l k) c", p=P)
        NCH = 11
        with nc.Block() as block:
            @block.sync
            def _(sp):
                for c in range(NCH):
                    if c >= 4:
                        sp.wait_ge(used, c - 3)
                    n = 256 if c < 10 else 48
                    dst = ring[:, c % 4, 0:KD * n].rearrange("p (k n) -> p k n", n=n)
                    sp.dma_start(dst, wv[:, :, c * 256:c * 256 + n]).then_inc(chunk_in[c % 4], 16)
                names = ("cmp", "sel", "win")
                for t, (t0, n) in enumerate(TOK):
                    sp.wait_ge(ready, t + 1)
                    for j, name in enumerate(names):
                        src = pkv[0:n, t, ATT + j * KVC:ATT + (j + 1) * KVC]
                        if t < 2:
                            dst = o["kv_%s_prompt" % name][0, 0, t0:t0 + n].rearrange("t c g d -> t (c g d)")
                            sp.dma_start(dst, src).then_inc(stored, 16)
                        elif name != "win":
                            dst = o["kv_%s_sample" % name].rearrange("l b t c g d -> (l b t) (c g d)")
                            sp.dma_start(dst, src).then_inc(stored, 16)
                        else:
                            for b in range(DB):
                                dst = o["kv_win_sample"][0, b, WIN - TS:WIN].rearrange("t c g d -> t (c g d)")
                                sp.dma_start(dst, src[b * TS:(b + 1) * TS, :]).then_inc(stored, 16)
                for b in range(DB):
                    sp.dma_start(o["kv_win_sample"][0, b, 0:WIN - TS].rearrange("t c g d -> t (c g d)"),
                                 a["cache_kv_win"][0, b, TS:WIN].rearrange("t c g d -> t (c g d)")).then_inc(win_stores, 16)
                sp.wait_ge(stored, 16 * (3 * 2 + 2 + DB))
                sp.wait_ge(win_stores, 16 * DB)

            @block.tensor
            def _(pe):
                for c in range(NCH):
                    n = 256 if c < 10 else 48
                    wt = ring[:, c % 4, 0:KD * n].rearrange("p (k n) -> p k n", n=n)
                    pe.wait_ge(chunk_in[c % 4], 16 * (c // 4 + 1))
                    for t, (t0, m) in enumerate(TOK):
                        g = 3 * c + t
                        if g >= 6:
                            pe.wait_ge(taken, g - 5)
                        for k in range(KD):
                            last = nc.tensor.matmul(bank[g % 6][0:m, 0:n], nT[:, k, t0:t0 + m], wt[:, k, :], start=k == 0, stop=k == KD - 1)
                        last.then_inc(made, 1)
                    pe.wait_ge(made, 3 * c + 3)
                    pe.sem_inc(used, 1)

            @block.scalar
            def _(act):
                for c in range(NCH):
                    n = 256 if c < 10 else 48
                    for t, (t0, m) in enumerate(TOK):
                        g = 3 * c + t
                        act.wait_ge(made, g + 1)
                        if c < 10:
                            nc.scalar.copy(pkv[0:m, t, c * 256:c * 256 + n], bank[g % 6][0:m, 0:n]).then_inc(taken, 1)
                        else:
                            nc.scalar.activation(gates[0:m, t, :], bank[g % 6][0:m, 0:n], ACT.Sigmoid).then_inc(taken, 1)
                for t, (t0, m) in enumerate(TOK):
                    act.wait_ge(norm_sq, t + 1)
                    nc.scalar.activation(rt[0:m, :], ss[0:m, :], ACT.Sqrt, bias=const("eps")[0:m, 0:1], scale=1.0 / HD).then_inc(rooted, 1)

            @block.vector
            def _(dve):
                own = Chain(dve, sem("qkv_dve"))
                dve.wait_ge(taken, 3 * NCH)
                for t, (t0, m) in enumerate(TOK):
                    q = pkv[0:m, t, 0:ATT].rearrange("p (h d) -> p h d", d=HD)
                    ks = pkv[0:m, t, ATT:ATT + 3 * KVC].rearrange("p (j c g d) -> p j c g d", j=3, c=2, d=HD)[:, :, 0]
                    cos = const("rope", 3, 2, 8)[0:m, t, 0, :]
                    sin = const("rope", 3, 2, 8)[0:m, t, 1, :]
                    sk = sqr[0:m, 16:28, :].rearrange("p (j g) d -> p j g d", j=3)
                    own(nc.vector.tensor_tensor(sqr[0:m, 0:16, :], q, q, ALU.mult))
                    own(nc.vector.tensor_tensor(sk, ks, ks, ALU.mult))
                    nc.vector.tensor_reduce(ss[0:m, :], sqr[0:m, :, :], AX.X, ALU.add).then_inc(norm_sq, 1)
                    dve.wait_ge(rooted, t + 1)
                    own(nc.vector.reciprocal(rs[0:m, :], rt[0:m, :]))
                    own(nc.vector.tensor_tensor(q, q, rs[0:m, 0:16].unsqueeze(2).to_broadcast([m, 16, HD]), ALU.mult))
                    own(nc.vector.tensor_tensor(ks, ks, rs[0:m, 16:28].rearrange("p (j g) -> p j g", j=3).unsqueeze(3).to_broadcast([m, 3, 4, HD]), ALU.mult))
                    own(nc.vector.tensor_tensor(q, q, gains[0:m, 0:1, :].to_broadcast([m, 16, HD]), ALU.mult))
                    own(nc.vector.tensor_tensor(ks, ks, gains[0:m, 1:4, :].unsqueeze(2).to_broadcast([m, 3, 4, HD]), ALU.mult))
                    for x, shape in ((q, [m, 16, 8]), (ks, [m, 3, 4, 8])):
                        if len(shape) == 3:
                            x1, x2 = x[:, :, 0:8], x[:, :, 8:16]
                            c_, s_ = (v.unsqueeze(1).to_broadcast(shape) for v in (cos, sin))
                            tmp = [rope[0:m, j] for j in range(4)]
                        else:
                            x1, x2 = x[:, :, :, 0:8], x[:, :, :, 8:16]
                            c_, s_ = (v.unsqueeze(1).unsqueeze(1).to_broadcast(shape) for v in (cos, sin))
                            tmp = [rope[0:m, j, 0:12].rearrange("p (j g) d -> p j g d", j=3) for j in range(4)]
                        own(nc.vector.tensor_tensor(tmp[0], x1, c_, ALU.mult))
                        own(nc.vector.tensor_tensor(tmp[1], x2, s_, ALU.mult))
                        own(nc.vector.tensor_tensor(tmp[2], x2, c_, ALU.mult))
                        own(nc.vector.tensor_tensor(tmp[3], x1, s_, ALU.mult))
                        own(nc.vector.tensor_tensor(x1, tmp[0], tmp[1], ALU.subtract))
                        own(nc.vector.tensor_tensor(x2, tmp[2], tmp[3], ALU.add))
                    dve.sem_inc(ready, 1)

    project_qkv()
    ATTENTION_HERE = None
    pages = [ringflat[:, 2048 * i:2048 * (i + 1)].rearrange("p (j c) -> p j c", c=KVC) for i in range(6)]
    wcmp = w(2, HD)
    qrows = w(DB, 2, P)
    kT = w(2, 2, NT)
    qT = w(2, HPG, T)
    table = w(NPG * DB)
    gcol = w(DB, 3)
    gates_dram = nc.dram_tensor("gates_rows", (NS, 48), F32, kind="Internal").ap()
    att_w = w.at
    SCALE = HD ** -0.5

    def prompt_setup():
        v = Carve(ringflat)
        prod = v(2, KVC)
        qp = v(3, ATT)
        permuted = sem("ps_permuted")
        summ = vsum
        kc_in, table_in, gd_out, gd_in = sem("ps_wcmp"), sem("ps_table"), sem("ps_gd_out"), sem("ps_gd_in")
        zeroed, q_t, q_got, multiplied, sum_made, sum_got, kct, kcgot = (
            sem(f"ps_{n}") for n in ("zeroed", "q_t", "q_got", "mult", "sum_made", "sum_got", "kct", "kcgot"))
        with nc.Block() as block:
            @block.sync
            def _(sp):
                for half in range(2):
                    sp.dma_start(wcmp[64 * half:64 * half + 64], a["w_cmp"][0].rearrange("c l d -> l c d")).then_inc(kc_in, 16)
                sp.dma_start(table[0:1, :].bitcast(I32), a["page_table"].rearrange("b n -> (b n)").unsqueeze(0)).then_inc(table_in, 16)
                sp.wait_ge(table_in, 16)
                sp.dma_start(gates_dram, gates[0:NS, 2, :]).then_inc(gd_out, 16)
                sp.wait_ge(gd_out, 16)
                for h in range(NH):
                    sp.dma_start(gcol[8 * h:8 * h + 8], gates_dram[:, 3 * h:3 * h + 3].rearrange("(b q) c -> q b c", q=TS)).then_inc(gd_in, 16)
                sp.wait_ge(gd_in, 16 * NH)

            @block.tensor
            def _(pe):
                for u in range(8):
                    gp, h = u // 4, u % 4
                    if u >= 6:
                        pe.wait_ge(q_got, 3 * (u - 5))
                    for t, (t0, n) in enumerate(TOK):
                        if u == 0:
                            pe.wait_ge(permuted, 2 * t + 2)
                        src = qp[0:n, t, u * P:(u + 1) * P]
                        last = nc.tensor.transpose(bank[u % 6][:, t0:t0 + n], src, ident[0:n, 0:n])
                    last.then_inc(q_t, 1)
                for u in range(4):
                    kind, gp = u // 2, u % 2
                    pe.wait_ge(q_got, 3 * (u + 3) if u + 3 <= 8 else 24 + (u + 3 - 8))
                    for t, (t0, n) in enumerate(TOK):
                        c0 = ATT + (1 + kind) * KVC + gp * P
                        last = nc.tensor.transpose(bank[(8 + u) % 6][:, t0:t0 + n], pkv[0:n, t, c0:c0 + P], ident[0:n, 0:n])
                    last.then_inc(q_t, 1)
                pe.wait_ge(multiplied, 2)
                for t in range(2):
                    last = nc.tensor.matmul(bank[6][0:NP_BLK, :], const("blocksum")[:, 30 - 2 * t:34 - 2 * t], prod[:, t, :], start=t == 0, stop=t == 1)
                last.then_inc(sum_made, 1)
                pe.wait_ge(sum_got, 1)
                for gp in range(2):
                    last = nc.tensor.transpose(bank[7][:, 4 * gp:4 * gp + 4], summ[0:NP_BLK, gp * P:(gp + 1) * P], ident[0:NP_BLK, 0:NP_BLK])
                last.then_inc(kct, 1)

            @block.scalar
            def _(act):
                act.wait_ge(zeroed, 1)
                for u in range(8):
                    gp, h = u // 4, u % 4
                    act.wait_ge(q_t, u + 1)
                    nc.scalar.mul(qT[:, gp, h, :], bank[u % 6][:, 0:T], SCALE).then_inc(q_got, 1)
                    for e in range(2):
                        row = 32 * (2 * gp + e) + 8 * h
                        nc.scalar.mul(qrows[64 * e:64 * e + 64, :, gp, row:row + 8],
                                      bank[u % 6][64 * e:64 * e + 64, T:NT].rearrange("p (b q) -> p b q", q=TS), SCALE).then_inc(q_got, 1)
                for u in range(4):
                    act.wait_ge(q_t, 9 + u)
                    nc.scalar.copy(kT[:, u // 2, u % 2, :], bank[(8 + u) % 6][:, 0:NT]).then_inc(q_got, 1)
                act.wait_ge(sum_made, 1)
                nc.scalar.copy(summ[0:NP_BLK, :], bank[6][0:NP_BLK, :]).then_inc(sum_got, 1)
                act.wait_ge(kct, 1)
                nc.scalar.copy(kcT[:, :, 0:NP_BLK], bank[7][:, 0:8].rearrange("p (a b) -> p a b", b=4)).then_inc(kcgot, 1)

            @block.gpsimd
            def _(pool):
                for t, (t0, n) in enumerate(TOK):
                    for gp in range(2):
                        src = pkv[0:n, t, gp * 512:gp * 512 + 512].rearrange("p (e h d) -> p h e d", e=2, d=HD)
                        dst = qp[0:n, t, gp * 512:gp * 512 + 512].rearrange("p (h e d) -> p h e d", e=2, d=HD)
                        nc.gpsimd.tensor_copy(dst, src).then_inc(permuted, 1)
                nc.gpsimd.memset(qrows[:, :, :, :], 0.0).then_inc(zeroed, 1)

            @block.vector
            def _(dve):
                dve.wait_ge(kc_in, 32)
                for t in range(2):
                    shape = [P, 2, NKV, HD]
                    nc.vector.tensor_tensor(prod[:, t, :].rearrange("p (c g d) -> p c g d", c=2, d=HD),
                                            pkv[:, t, ATT:ATT + KVC].rearrange("p (c g d) -> p c g d", c=2, d=HD),
                                            wcmp.unsqueeze(2).to_broadcast(shape), ALU.mult).then_inc(multiplied, 1)

    vsum = w(KVC)
    kcT = w(2, NBLK)
    att_w = w.at
    prompt_setup()

    def prompt_attention():
        v = Carve(ringflat)
        orow = v(2, ATT)
        qs = v(2, T)
        gs = v(2, 4, 3)
        sc, ec = v(8, NP_BLK), v(8, NP_BLK)
        mc, lc, rc = v(8), v(8), v(8)
        pcT = v(8, P)
        S = v(2, 2, T)
        PT = v(2, 512)
        nm, sm, rc2, cf = v(2, 2), v(2, 2), v(2, 2), v(2, 2)
        ccf = v(8)
        ob = v(2, 2, HD)
        U = range(8)
        PE = Steps(sem("pa_pe"), ["cmp"] + ["s0", "s1", "ctrans"] + [x for u in U for x in ([f"s{u + 1}"] if 2 <= u + 1 < 8 and u else []) + [f"t{u}", f"o{u}"]])
        DV = Steps(sem("pa_dve"), ["gates", "cbias", "cp"] + [f"{x}{u}" for u in U for x in ("soft",)] + [f"o{u}" for u in U])
        names = ["gates", "csub", "cp"]
        for u in U:
            names.append(f"soft{u}")
            if u >= 1:
                names.append(f"o{u - 1}")
        names.append("o7")
        DV.names = names
        AC = Steps(sem("pa_act"), ["q0", "q1", "cexp", "cpT"] + [x for u in U for x in (f"exp0_{u}", f"exp1_{u}", f"pt{u}")])
        turned, copied = sem("pa_turned"), sem("pa_copied")

        def unit(u):
            gp, e, qi = u // 4, u // 2 % 2, u % 2
            return gp, e, qi, slice(64 * e, 64 * e + 64), P * (qi + 1)

        with nc.Block() as block:
            @block.tensor
            def _(pe):
                PE.start(pe)
                mm = nc.tensor.matmul

                def scores(u, h):
                    gp, e, qi, hs, nk = unit(u)
                    if u >= 2:
                        pe.wait_ge(DV.sem, DV.at(f"soft{u - 2}", h))
                    for kind in range(2):
                        last = mm(bank[u % 2][:, kind * nk:(kind + 1) * nk], qs[hs, gp, qi * P:(qi + 1) * P], kT[hs, kind, gp, 0:nk], start=True, stop=True)
                    PE.done(f"s{u}", last)

                with pe.Fori(0, HPG) as h:
                    pe.wait_ge(AC.sem, AC.at("q1", h))
                    pe.wait_ge(DV.sem, DV.before(h))
                    settled(pe)
                    for u in U:
                        gp, e, qi, hs, nk = unit(u)
                        last = mm(bank[2 + e][:, u * 4:u * 4 + 4], qs[hs, gp, qi * P:(qi + 1) * P], kcT[hs, gp, 0:NP_BLK], start=True, stop=True)
                    PE.done("cmp", last)
                    scores(0, h)
                    scores(1, h)
                    pe.wait_ge(DV.sem, DV.at("cp", h))
                    for u in U:
                        last = nc.tensor.transpose(bank[4 + u // 4][0:NP_BLK, (u % 4) * P:(u % 4 + 1) * P], ec[:, u, :], ident)
                    PE.done("ctrans", last)
                    for u in U:
                        gp, e, qi, hs, nk = unit(u)
                        if 2 <= u + 1 < 8:
                            scores(u + 1, h)
                        pe.wait_ge(AC.sem, AC.at(f"exp1_{u}", h))
                        n = 0
                        for kind in range(2):
                            for j in range(qi + 1):
                                last = nc.tensor.transpose(bank[4 + u % 2][:, n * P:(n + 1) * P], S[:, u % 2, kind, j * P:(j + 1) * P], ident)
                                n += 1
                        PE.done(f"t{u}", last)
                        pe.wait_ge(AC.sem, AC.at(f"pt{u}", h))
                        if u >= 2:
                            pe.wait_ge(DV.sem, DV.at(f"o{u - 2}", h))
                        ps = bank[6 + u % 2]
                        c0 = HD * (2 * gp + e)
                        mm(ps[:, 128:192], pcT[0:NP_BLK, u, :], vsum[0:NP_BLK, 256 + c0:256 + c0 + HD], start=True, stop=True)
                        n = 0
                        for kind in range(2):
                            for j in range(qi + 1):
                                vv = pkv[:, j, ATT + (1 + kind) * KVC + 256 + c0:ATT + (1 + kind) * KVC + 256 + c0 + HD]
                                last = mm(ps[:, kind * HD:(kind + 1) * HD], PT[:, u % 2, n * P:(n + 1) * P], vv, start=j == 0, stop=j == qi)
                                n += 1
                        PE.done(f"o{u}", last)
                    PE.turn()
                pe.wait_ge(DV.sem, DV.before(HPG))
                for j in range(8):
                    if j >= 4:
                        pe.wait_ge(copied, j - 3)
                    for qi in range(2):
                        last = nc.tensor.transpose(bank[j % 4][:, qi * P:(qi + 1) * P], orow[:, qi, j * P:(j + 1) * P], ident)
                    last.then_inc(turned, 1)

            @block.scalar
            def _(act):
                AC.start(act)
                with act.Fori(0, HPG) as h:
                    act.wait_ge(PE.sem, PE.before(h))
                    for gp in range(2):
                        AC.done(f"q{gp}", nc.scalar.copy(qs[:, gp:gp + 1, :], qT[:, gp, ds(h, 1), :]))
                    act.wait_ge(DV.sem, DV.at("csub", h))
                    AC.done("cexp", nc.scalar.activation(ec, sc, ACT.Exp))

                    def exps(u):
                        gp, e, qi, hs, nk = unit(u)
                        act.wait_ge(DV.sem, DV.at(f"soft{u}", h))
                        for kind in range(2):
                            x = S[:, u % 2, kind, 0:nk]
                            AC.done(f"exp{kind}_{u}", nc.scalar.activation(x, x, ACT.Exp, bias=nm[:, u % 2, kind:kind + 1], accum_out=sm[:, u % 2, kind:kind + 1]))

                    act.wait_ge(PE.sem, PE.at("ctrans", h))
                    for s in range(2):
                        ins = nc.scalar.copy(pcT[0:NP_BLK, 4 * s:4 * s + 4, :], bank[4 + s][0:NP_BLK, :].rearrange("p (a b) -> p a b", b=P))
                        if s:
                            AC.done("cpT", ins)
                    for u in U:
                        gp, e, qi, hs, nk = unit(u)
                        exps(u)
                        act.wait_ge(PE.sem, PE.at(f"t{u}", h))
                        AC.done(f"pt{u}", nc.scalar.copy(PT[:, u % 2, 0:2 * nk], bank[4 + u % 2][:, 0:2 * nk]))
                    AC.turn()
                for j in range(8):
                    act.wait_ge(turned, j + 1)
                    nc.scalar.copy(oT[:, j, 0:T], bank[j % 4][:, 0:T]).then_inc(copied, 1)

            @block.vector
            def _(dve):
                DV.start(dve)
                own = Chain(dve, sem("pa_own"))
                tt = nc.vector.tensor_tensor
                vis = const("vis", 2, 2, 4)
                with dve.Fori(0, HPG) as h:
                    own.body(h, OWN)
                    dve.wait_ge(PE.sem, PE.before(h))
                    dve.wait_ge(AC.sem, AC.before(h))
                    dve.wait_ge(DV.sem, DV.before(h))
                    gv = gates[:, 0:2, :].rearrange("p t (g h c) -> p t g h c", h=HPG, c=3)[:, :, :, ds(h, 1), :].rearrange("p t g a c -> p t g (a c)")
                    DV.done("gates", nc.vector.tensor_copy(gs, gv))
                    dve.wait_ge(PE.sem, PE.at("cmp", h))
                    s4 = sc.rearrange("p (a b) c -> p a b c", b=2)
                    e4 = ec.rearrange("p (a b) c -> p a b c", b=2)
                    for e in range(2):
                        ps = bank[2 + e][:, 0:32].rearrange("p (a e b c) -> p a e b c", a=2, e=2, b=2)[:, :, e]
                        dst = sc.rearrange("p (a e b) c -> p a e b c", e=2, b=2)[:, :, e]
                        own(tt(dst, ps, vis[:, :, 1, :].unsqueeze(1).to_broadcast([P, 2, 2, 4]), ALU.add))
                    own(nc.vector.tensor_reduce(mc, sc, AX.X, ALU.max))
                    DV.done("csub", tt(sc, sc, mc.unsqueeze(2).to_broadcast([P, 8, 4]), ALU.subtract))
                    dve.wait_ge(AC.sem, AC.at("cexp", h))
                    own(tt(e4, e4, vis[:, :, 0, :].unsqueeze(1).to_broadcast([P, 4, 2, 4]), ALU.mult))
                    own(nc.vector.tensor_reduce(lc, ec, AX.X, ALU.add))
                    own(nc.vector.tensor_scalar(lc, lc, 1e-30, None, ALU.max))
                    own(nc.vector.reciprocal(rc, lc))
                    DV.done("cp", tt(ec, ec, rc.unsqueeze(2).to_broadcast([P, 8, 4]), ALU.mult))

                    def soft(u):
                        gp, e, qi, hs, nk = unit(u)
                        dve.wait_ge(PE.sem, PE.at(f"s{u}", h))
                        if u >= 2:
                            dve.wait_ge(PE.sem, PE.at(f"t{u - 2}", h))
                        m = const("causal")[:, 0:T] if qi else const("causal")[:, P:T]
                        own(tt(S[:, u % 2, :, 0:nk], bank[u % 2][:, 0:2 * nk].rearrange("p (a b) -> p a b", b=nk), m.unsqueeze(1).to_broadcast([P, 2, nk]), ALU.add))
                        DV.done(f"soft{u}", nc.vector.tensor_reduce(nm[:, u % 2, :], S[:, u % 2, :, 0:nk], AX.X, ALU.max, negate=True))

                    def out(u):
                        gp, e, qi, hs, nk = unit(u)
                        b = u % 2
                        dve.wait_ge(AC.sem, AC.at(f"exp1_{u}", h))
                        own(nc.vector.reciprocal(rc2[:, b, :], sm[:, b, :]))
                        own(tt(cf[:, b, :], rc2[:, b, :], gs[:, qi, 2 * gp + e, 1:3], ALU.mult))
                        dve.wait_ge(PE.sem, PE.at(f"o{u}", h))
                        ps = bank[6 + u % 2]
                        own(nc.vector.tensor_scalar(ob[:, b, 0, :], ps[:, 128:192], gs[:, qi, 2 * gp + e, 0:1], None, ALU.mult))
                        own(nc.vector.scalar_tensor_tensor(out=ob[:, b, 1, :], in0=ps[:, 0:HD], scalar=cf[:, b, 0:1], in1=ob[:, b, 0, :], op0=ALU.mult, op1=ALU.add))
                        dst = orow[:, qi, :].rearrange("p (g h d) -> p g h d", h=HPG, d=HD)[:, 2 * gp + e, ds(h, 1), :].rearrange("p a d -> p (a d)")
                        DV.done(f"o{u}", nc.vector.scalar_tensor_tensor(out=dst, in0=ps[:, HD:2 * HD], scalar=cf[:, b, 1:2], in1=ob[:, b, 1, :], op0=ALU.mult, op1=ALU.add))

                    soft(0)
                    for u in U:
                        if u + 1 < 8:
                            soft(u + 1)
                        out(u)
                    DV.turn()
                own.end(HPG)

    OWN = 47
    prompt_attention()

    def sample_attention():
        v = Carve(ringflat, 6 * 2048)
        Kq = v(2, 512)
        Sw = v(WIN + TS)
        PTn = v(2, P)
        imp, rank, bias, sc, pc = v(NBLK), v(NBLK), v(NBLK), v(NBLK), v(NBLK)
        pcT = v(P)
        vnew = v(2, 256)
        small = v(16)
        v2 = Carve(work, att_w)
        S = v2(PAST + TS)
        PT = v2(3, 512)
        gt = v2(NBLK, NBLK)
        eq = Carve(ringflat, v.at)(NBLK, NBLK) if v.at + 1024 <= 16384 else v2(NBLK, NBLK)
        v3 = Carve(work, 0)
        ob = v3(3, HD)
        qb = v3(2, P)
        more = [v3(4, KVC) for _ in range(3)]
        slot = dict(s0=pages[0], s1=pages[1], s2=pages[2], s3=pages[3], w=pages[4], c0=pages[5], c1=more[0], c2=more[1], c3=more[2])
        landed = {n: sem(f"sa_landed_{n}") for n in slot}
        summed, sums_got = sem("sa_summed"), sem("sa_sums_got")
        v_in = sem("sa_v_in")
        Q = range(4)
        PE = Steps(sem("sa_pe"), ["k0", "kc", "sc", "s0", "k1", "imp", "s1", "k2", "ocmp", "s2", "k3", "s3", "snew", "kw", "sw", "swnew",
                                  "tp0", "tp1", "pv0", "tp2", "pv1", "tp3", "pv2", "tpn", "pv3", "tpw", "tpwn", "pvn", "pvw", "fin"])
        AC = Steps(sem("sa_act"), ["q", "k0", "kc", "cexp", "k1", "pct", "k2", "k3", "kw", "exps", "expw", "pt0", "pt1", "pt2", "pt3", "ptn", "ptw", "ptwn", "out0", "out1"])
        DV = Steps(sem("sa_dve"), ["cmax", "pc", "bias", "s0", "s1", "s2", "s3", "snew", "smax", "wmax", "o"])
        PL = Steps(sem("sa_pool"), ["m0", "m1", "m2", "m3"])

        def arrived(eng, name, b):
            eng.wait_ge(landed[name], b * 64 + 64)

        LAST = DB - 1

        with nc.Block() as block:
            @block.sync
            def _(sp):
                cmp_, sel_ = (a[n][0].rearrange("n t c g d -> n t (c g d)") for n in ("cache_kv_cmp", "cache_kv_sel"))

                def load(name, cache, b):
                    for j in range(4):
                        page = sp.value_load(table[0:1, ds(b * NPG + (4 * int(name[1]) + j), 1)].bitcast(I32), min_val=0, max_val=cache.shape[0] - 1)
                        sp.dma_start(slot[name][:, j:j + 1, :], cache[ds(page, 1), :, :].rearrange("n t c -> t n c")).then_inc(landed[name], 16)

                def load_rest(b):
                    for j in range(4):
                        sp.dma_start(slot["w"][:, j:j + 1, :], a["cache_kv_win"][0, ds(b, 1), j * P:(j + 1) * P].rearrange("b t c g d -> t b (c g d)")).then_inc(landed["w"], 16)
                    sp.dma_start(vnew[0:TS, 0:1, :], o["kv_sel_sample"][0, ds(b, 1), :, 1].rearrange("b t g d -> t b (g d)")).then_inc(v_in, 16)
                    sp.dma_start(vnew[0:TS, 1:2, :], o["kv_win_sample"][0, ds(b, 1), WIN - TS:WIN, 1].rearrange("b t g d -> t b (g d)")).then_inc(v_in, 16)

                for q in Q:
                    load(f"c{q}", cmp_, 0)
                for q in Q:
                    load(f"s{q}", sel_, 0)
                load_rest(0)
                with sp.Fori(0, LAST) as b:
                    sp.wait_ge(summed, b * 1 + 1)
                    settled(sp)
                    for q in Q:
                        load(f"c{q}", cmp_, b + 1)
                    for q in Q:
                        sp.wait_ge(PE.sem, PE.at(f"pv{q}", b))
                        settled(sp)
                        load(f"s{q}", sel_, b + 1)
                    sp.wait_ge(PE.sem, PE.at("pvw", b))
                    settled(sp)
                    load_rest(b + 1)

            @block.gpsimd
            def _(pool):
                PL.start(pool)
                with pool.Fori(0, DB) as b:
                    for n in Q:
                        arrived(pool, f"c{n}", b)
                        pg = slot[f"c{n}"]
                        for j in range(4):
                            x = pg[:, j, :].rearrange("p (c g d) -> p c g d", c=2, d=HD)
                            last = nc.gpsimd.tensor_tensor(x, x, wcmp.unsqueeze(2).to_broadcast([P, 2, NKV, HD]), ALU.mult)
                        PL.done(f"m{n}", last)
                    PL.turn()

            @block.tensor
            def _(pe):
                PE.start(pe)
                mm, tr = nc.tensor.matmul, nc.tensor.transpose

                def block_sums(b):
                    for n in Q:
                        pe.wait_ge(PL.sem, PL.at(f"m{n}", b))
                        for j in range(4):
                            pg = 4 * n + j
                            last = mm(bank[0][0:NBLK, :], const("blocksum")[:, 30 - 2 * pg:62 - 2 * pg], slot[f"c{n}"][:, j, :], start=pg == 0, stop=pg == NPG - 1)
                    last.then_inc(summed, 1)

                def turn(b, last_one):
                    def ktrans(name, src):
                        arrived(pe, src, b)
                        for gp in range(2):
                            for j in range(4):
                                last = tr(bank[1 + gp][:, j * P:(j + 1) * P], slot[src][:, j, gp * P:(gp + 1) * P], ident)
                        PE.done(name, last)

                    def score(name, bk, src, n):
                        for gp in range(2):
                            last = mm(bank[bk][:, 0:n] if not isinstance(bk, tuple) else bank[bk[0]][:, bk[1]:bk[1] + n], qb[:, gp, :], src(gp), start=gp == 0, stop=gp == 1)
                        PE.done(name, last)

                    ktrans("k0", "s0")
                    pe.wait_ge(sums_got, b * 1 + 1)
                    settled(pe)
                    for gp in range(2):
                        last = tr(bank[7][:, 32 * gp:32 * gp + 32], vsum[0:NBLK, gp * P:(gp + 1) * P], ident[0:NBLK, 0:NBLK])
                    PE.done("kc", last)
                    pe.wait_ge(AC.sem, AC.at("kc", b))
                    score("sc", (7, 64), lambda gp: kcT[:, gp, :], NBLK)
                    score("s0", 3, lambda gp: Kq[:, gp, :], 512)
                    ktrans("k1", "s1")
                    pe.wait_ge(DV.sem, DV.at("pc", b))
                    mm(bank[7][:, 96:128], const("group"), pc, start=True, stop=True)
                    last = tr(bank[6][0:NBLK, 0:P], pc, ident)
                    PE.done("imp", last)
                    pe.wait_ge(AC.sem, AC.at("k1", b))
                    score("s1", 4, lambda gp: Kq[:, gp, :], 512)
                    ktrans("k2", "s2")
                    pe.wait_ge(AC.sem, AC.at("pct", b))
                    PE.done("ocmp", mm(bank[6][:, 256:512], pcT[0:NBLK, :], vsum[0:NBLK, 256:512], start=True, stop=True))
                    pe.wait_ge(AC.sem, AC.at("k2", b))
                    pe.wait_ge(DV.sem, DV.at("s0", b))
                    score("s2", 3, lambda gp: Kq[:, gp, :], 512)
                    ktrans("k3", "s3")
                    pe.wait_ge(AC.sem, AC.at("k3", b))
                    pe.wait_ge(DV.sem, DV.at("s1", b))
                    score("s3", 4, lambda gp: Kq[:, gp, :], 512)
                    new = ds(b * TS + T, TS)
                    score("snew", (0, 0), lambda gp: kT[:, 0, gp, new], TS)
                    ktrans("kw", "w")
                    pe.wait_ge(AC.sem, AC.at("kw", b))
                    score("sw", 5, lambda gp: Kq[:, gp, :], 512)
                    score("swnew", (7, 128), lambda gp: kT[:, 1, gp, new], TS)
                    if not last_one:
                        pe.wait_ge(DV.sem, DV.at("snew", b))
                        block_sums(b + 1)

                    def tp(q, bk):
                        for j in range(4):
                            last = tr(bank[bk][:, j * P:(j + 1) * P], S[:, (4 * q + j) * P:(4 * q + j + 1) * P], ident)
                        PE.done(f"tp{q}", last)

                    def pv(q):
                        pe.wait_ge(AC.sem, AC.at(f"pt{q}", b))
                        for j in range(4):
                            last = mm(bank[6][:, 0:256], PT[:, q % 3, j * P:(j + 1) * P], slot[f"s{q}"][:, j, 256:512], start=q == 0 and j == 0, stop=False)
                        PE.done(f"pv{q}", last)

                    pe.wait_ge(AC.sem, AC.at("exps", b))
                    tp(0, 1)
                    tp(1, 2)
                    pv(0)
                    tp(2, 3)
                    pv(1)
                    pe.wait_ge(AC.sem, AC.at("pt0", b))
                    tp(3, 1)
                    pv(2)
                    pe.wait_ge(AC.sem, AC.at("pt1", b))
                    PE.done("tpn", tr(bank[2][0:TS, 0:P], S[:, PAST:PAST + TS], ident))
                    pv(3)
                    pe.wait_ge(AC.sem, AC.at("expw", b))
                    for j in range(4):
                        last = tr(bank[3][:, j * P:(j + 1) * P], Sw[:, j * P:(j + 1) * P], ident)
                    PE.done("tpw", last)
                    PE.done("tpwn", tr(bank[4][0:TS, 0:P], Sw[:, WIN:WIN + TS], ident))
                    pe.wait_ge(v_in, b * 32 + 32)
                    pe.wait_ge(AC.sem, AC.at("ptn", b))
                    settled(pe)
                    PE.done("pvn", mm(bank[6][:, 0:256], PTn[0:TS, 0, :], vnew[0:TS, 0, :], start=False, stop=True))
                    pe.wait_ge(AC.sem, AC.at("ptwn", b))
                    for j in range(4):
                        mm(bank[7][:, 256:512], PT[:, 1, j * P:(j + 1) * P], slot["w"][:, j, 256:512], start=j == 0, stop=False)
                    PE.done("pvw", mm(bank[7][:, 256:512], PTn[0:TS, 1, :], vnew[0:TS, 1, :], start=False, stop=True))
                    pe.wait_ge(DV.sem, DV.at("o", b))
                    if not last_one:
                        pe.wait_ge(sums_got, b * 1 + 2)
                    settled(pe)
                    PE.done("fin", tr(bank[0][0:HD, 128:256], ob[:, 0, :], ident))
                    PE.turn()

                block_sums(0)
                with pe.Fori(0, LAST) as b:
                    turn(b, False)
                turn(LAST, True)

            @block.scalar
            def _(act):
                AC.start(act)

                def take_sums(b):
                    act.wait_ge(summed, b * 1 + 1)
                    nc.scalar.copy(vsum[0:NBLK, :], bank[0][0:NBLK, :]).then_inc(sums_got, 1)

                def turn(b, last_one):
                    act.wait_ge(PE.sem, PE.before(b))
                    AC.done("q", nc.scalar.copy(qb.unsqueeze(1), qrows[:, ds(b, 1), :, :]))

                    def keys(n):
                        act.wait_ge(PE.sem, PE.at(n, b))
                        nc.scalar.copy(Kq[:, 0, :], bank[1][:, :])
                        AC.done(n, nc.scalar.copy(Kq[:, 1, :], bank[2][:, :]))

                    keys("k0")
                    act.wait_ge(PE.sem, PE.at("kc", b))
                    AC.done("kc", nc.scalar.copy(kcT, bank[7][:, 0:64].rearrange("p (a b) -> p a b", b=NBLK)))
                    act.wait_ge(DV.sem, DV.at("cmax", b))
                    AC.done("cexp", nc.scalar.activation(sc, sc, ACT.Exp, bias=small[:, 0:1], accum_out=small[:, 1:2]))
                    keys("k1")
                    act.wait_ge(PE.sem, PE.at("imp", b))
                    AC.done("pct", nc.scalar.copy(pcT[0:NBLK, :], bank[6][0:NBLK, 0:P]))
                    keys("k2")
                    keys("k3")
                    keys("kw")
                    act.wait_ge(DV.sem, DV.at("smax", b))
                    AC.done("exps", nc.scalar.activation(S, S, ACT.Exp, bias=small[:, 2:3], accum_out=small[:, 3:4]))
                    act.wait_ge(DV.sem, DV.at("wmax", b))
                    AC.done("expw", nc.scalar.activation(Sw, Sw, ACT.Exp, bias=small[:, 4:5], accum_out=small[:, 5:6]))
                    if not last_one:
                        take_sums(b + 1)
                    for q, bk in ((0, 1), (1, 2), (2, 3)):
                        act.wait_ge(PE.sem, PE.at(f"tp{q}", b))
                        AC.done(f"pt{q}", nc.scalar.copy(PT[:, q, :], bank[bk][:, :]))
                    act.wait_ge(PE.sem, PE.at("tp3", b))
                    AC.done("pt3", nc.scalar.copy(PT[:, 0, :], bank[1][:, :]))
                    act.wait_ge(PE.sem, PE.at("tpn", b))
                    AC.done("ptn", nc.scalar.copy(PTn[0:TS, 0, :], bank[2][0:TS, 0:P]))
                    act.wait_ge(PE.sem, PE.at("tpw", b))
                    AC.done("ptw", nc.scalar.copy(PT[:, 1, :], bank[3][:, :]))
                    act.wait_ge(PE.sem, PE.at("tpwn", b))
                    AC.done("ptwn", nc.scalar.copy(PTn[0:TS, 1, :], bank[4][0:TS, 0:P]))
                    act.wait_ge(PE.sem, PE.at("fin", b))
                    for e in range(2):
                        src = bank[0][0:HD, 128:256].rearrange("p (j e q) -> p j e q", e=2, q=TS)[:, :, e, :]
                        AC.done(f"out{e}", nc.scalar.copy(oT[64 * e:64 * e + 64, :, ds(b * TS + T, TS)], src))
                    AC.turn()

                take_sums(0)
                with act.Fori(0, LAST) as b:
                    turn(b, False)
                turn(LAST, True)

            @block.vector
            def _(dve):
                DV.start(dve)
                own = Chain(dve, sem("sa_own"))
                tt = nc.vector.tensor_tensor

                def turn(b):
                    dve.wait_ge(PE.sem, PE.at("sc", b))
                    dve.wait_ge(AC.sem, AC.before(b))
                    dve.wait_ge(DV.sem, DV.before(b))
                    own(nc.vector.tensor_copy(sc, bank[7][:, 64:96]))
                    DV.done("cmax", nc.vector.tensor_reduce(small[:, 0:1], sc, AX.X, ALU.max, negate=True))
                    dve.wait_ge(AC.sem, AC.at("cexp", b))
                    own(nc.vector.reciprocal(small[:, 6:7], small[:, 1:2]))
                    DV.done("pc", nc.vector.tensor_scalar(pc, sc, small[:, 6:7], None, ALU.mult))
                    dve.wait_ge(PE.sem, PE.at("imp", b))
                    own(nc.vector.tensor_copy(imp, bank[7][:, 96:128]))
                    each, other = imp.unsqueeze(2).to_broadcast([P, NBLK, NBLK]), imp.unsqueeze(1).to_broadcast([P, NBLK, NBLK])
                    own(tt(gt, other, each, ALU.is_gt))
                    own(tt(eq, other, each, ALU.is_equal))
                    own(tt(eq, eq, const("earlier", NBLK, NBLK), ALU.mult))
                    own(tt(gt, gt, eq, ALU.add))
                    own(nc.vector.tensor_reduce(rank, gt, AX.X, ALU.add))
                    DV.done("bias", nc.vector.tensor_scalar(bias, rank, NSEL - 1.5, NEG, ALU.is_gt, ALU.mult))
                    dve.wait_ge(DV.sem, DV.at("bias", b))
                    for q in Q:
                        dve.wait_ge(PE.sem, PE.at(f"s{q}", b))
                        dst = S[:, q * 512:(q + 1) * 512].rearrange("p (n l) -> p n l", l=BLOCK)
                        src = bank[3 + q % 2][:, :].rearrange("p (n l) -> p n l", l=BLOCK)
                        DV.done(f"s{q}", tt(dst, src, bias[:, 8 * q:8 * q + 8].unsqueeze(2).to_broadcast([P, 8, BLOCK]), ALU.add))
                    dve.wait_ge(PE.sem, PE.at("snew", b))
                    DV.done("snew", tt(S[:, PAST:], bank[0][:, 0:TS], const("newmask"), ALU.add))
                    dve.wait_ge(DV.sem, DV.at("snew", b))
                    DV.done("smax", nc.vector.tensor_reduce(small[:, 2:3], S, AX.X, ALU.max, negate=True))
                    dve.wait_ge(PE.sem, PE.at("swnew", b))
                    own(nc.vector.tensor_copy(Sw[:, TS:WIN], bank[5][:, TS:WIN]))
                    own(tt(Sw[:, 0:TS], bank[5][:, 0:TS], const("winmask"), ALU.add))
                    own(tt(Sw[:, WIN:], bank[7][:, 128:136], const("newmask"), ALU.add))
                    DV.done("wmax", nc.vector.tensor_reduce(small[:, 4:5], Sw, AX.X, ALU.max, negate=True))
                    dve.wait_ge(AC.sem, AC.at("expw", b))
                    own(nc.vector.reciprocal(small[:, 7:8], small[:, 3:4]))
                    own(nc.vector.reciprocal(small[:, 8:9], small[:, 5:6]))
                    gb = gcol[:, ds(b, 1), :].rearrange("p a c -> p (a c)")
                    own(nc.vector.tensor_copy(small[:, 12:15], gb))
                    own(tt(small[:, 9:11], small[:, 7:9], small[:, 13:15], ALU.mult))
                    dve.wait_ge(PE.sem, PE.at("pvw", b))
                    for g in range(NKV):
                        r, c = slice(32 * g, 32 * g + 32), slice(HD * g, HD * g + HD)
                        own(nc.vector.tensor_scalar(ob[r, 2, :], bank[6][r, 256 + HD * g:256 + HD * g + HD], small[r, 12:13], None, ALU.mult))
                    for g in range(NKV):
                        r, c = slice(32 * g, 32 * g + 32), slice(HD * g, HD * g + HD)
                        own(nc.vector.scalar_tensor_tensor(out=ob[r, 1, :], in0=bank[6][r, c], scalar=small[r, 9:10], in1=ob[r, 2, :], op0=ALU.mult, op1=ALU.add))
                    for g in range(NKV):
                        r, c = slice(32 * g, 32 * g + 32), slice(256 + HD * g, 256 + HD * g + HD)
                        ins = nc.vector.scalar_tensor_tensor(out=ob[r, 0, :], in0=bank[7][r, c], scalar=small[r, 10:11], in1=ob[r, 1, :], op0=ALU.mult, op1=ALU.add)
                        if g < NKV - 1:
                            own(ins)
                        else:
                            DV.done("o", ins)
                    DV.turn()

                with dve.Fori(0, LAST) as b:
                    own.body(b, OWN2)
                    turn(b)
                own.end(LAST)
                turn(LAST)

    OWN2 = 26
    sample_attention()

    w = Carve(work)
    z = w(25, NT)
    yT = z[:, 0:8, :]
    decay_in = w(8, NT)
    rate = w(8, NT)
    rwkv_work = w.at

    def project_shift():
        v = Carve(work, 8000)
        srow = v(SHIFT)
        v.at = rwkv_work
        prevT = v(25, DB)
        lastT = v(25, 1 + DB)
        ub = v(4, 1 + T + DB * (TS + 1))
        used, made, taken = sem("sh_used"), sem("sh_made"), sem("sh_taken")
        prev_in, prev_t, prev_got = sem("sh_prev_in"), sem("sh_prev_t"), sem("sh_prev_got")
        mixed, kept, zeroed = sem("sh_mixed"), sem("sh_kept"), sem("sh_zeroed")
        last_t, last_got, last_out = sem("sh_last_t"), sem("sh_last_got"), sem("sh_last_out")
        landed = [sem(f"sh_landed{i}") for i in range(4)]
        wv = a["w_in"].rearrange("l (k p) c -> p (l k) c", p=P)[:, :, C_SHIFT:C_MERGE]
        slot = [ring[:, i, :].rearrange("p (k n) -> p k n", n=256) for i in range(4)]
        with nc.Block() as block:
            @block.sync
            def _(sp):
                sp.dma_start(srow[0:DB, :], a["state_shift"][0]).then_inc(prev_in, 16)
                with sp.Fori(0, 3) as i:
                    for c in range(4):
                        sp.wait_ge(used, i * 4 + (c + 1))
                        sp.dma_start(slot[c], wv[:, :, ds(i * 1024 + c * 256, 256)]).then_inc(landed[c], 16)
                sp.wait_ge(used, 12 + 1)
                sp.dma_start(slot[0][:, :, 0:P], wv[:, :, 3072:3200]).then_inc(landed[0], 16)
                sp.wait_ge(last_got, 7)
                sp.dma_start(o["shift_prompt"][0], srow[0:1, :]).then_inc(last_out, 16)
                sp.dma_start(o["shift_sample"][0], srow[1:1 + DB, :]).then_inc(last_out, 16)
                sp.wait_ge(last_out, 32)

            @block.tensor
            def _(pe):
                pe.sem_inc(used, 4)
                pe.wait_ge(prev_in, 16)
                for t in range(25):
                    last = nc.tensor.transpose(bank[7][:, 8 * t:8 * t + 8], srow[0:DB, t * P:(t + 1) * P], ident[0:DB, 0:DB])
                last.then_inc(prev_t, 1)

                def tile(k0, b, sl, col, signal):
                    for k in range(KD):
                        last = nc.tensor.matmul(bank[b][:, 0:NT], sl[:, k, col:col + P], nT[:, k, :], start=k == 0, stop=k == KD - 1)
                    last.then_inc(made, 1)

                with pe.Fori(0, 3) as i:
                    for c in range(4):
                        pe.wait_ge(landed[c], i * 16 + 16)
                        for h in range(2):
                            g = 2 * c + h
                            pe.wait_ge(taken, i * 8 + (g + 1))
                            tile(0, g % 4, slot[c], h * P, made)
                        pe.wait_ge(made, i * 8 + 2 * c + 2)
                        pe.sem_inc(used, 1)
                pe.wait_ge(landed[0], 64)
                pe.wait_ge(taken, 24 + 1)
                tile(0, 0, slot[0], 0, made)
                pe.wait_ge(kept, 25 + 4)
                for q in range(7):
                    n = 4 if q < 6 else 1
                    if q >= 2:
                        pe.wait_ge(last_got, q - 1)
                    for j in range(n):
                        last = nc.tensor.transpose(bank[5 + q % 2][0:9, j * P:(j + 1) * P], lastT[:, 4 * q + j, :], ident)
                    last.then_inc(last_t, 1)

            @block.scalar
            def _(act):
                act.sem_inc(taken, 4)
                act.wait_ge(prev_t, 1)
                nc.scalar.copy(prevT, bank[7][:, 0:200].rearrange("p (a b) -> p a b", b=DB)).then_inc(prev_got, 1)
                act.wait_ge(prev_got, 1)
                act.wait_ge(zeroed, 1)

                def take(n, b, u, prev):
                    act.wait_ge(made, n + 1)
                    s = ub[:, u, 1 + T:].rearrange("p (b t) -> p b t", t=TS + 1)
                    nc.scalar.copy(s[:, :, 0:1], prev)
                    nc.scalar.copy(s[:, :, 1:], bank[b][:, T:NT].rearrange("p (b t) -> p b t", t=TS))
                    nc.scalar.copy(ub[:, u, 1:1 + T], bank[b][:, 0:T]).then_inc(taken, 1)

                with act.Fori(0, 3) as i:
                    for g in range(8):
                        act.wait_ge(mixed, i * 8 + (g + 1))
                        act.wait_ge(kept, i * 8 + (g + 1))
                        take(i * 8 + g, g % 4, g % 4, prevT[:, ds(i * 8 + g, 1), :].rearrange("p a b -> p b a"))
                act.wait_ge(mixed, 24 + 1)
                act.wait_ge(kept, 24 + 1)
                take(24, 0, 0, prevT[:, 24:25, :].rearrange("p a b -> p b a"))
                for q in range(7):
                    n = 4 if q < 6 else 1
                    act.wait_ge(last_t, q + 1)
                    nc.scalar.copy(srow[0:9, 4 * q * P:(4 * q + n) * P], bank[5 + q % 2][0:9, 0:n * P]).then_inc(last_got, 1)

            @block.gpsimd
            def _(pool):
                pool.sem_inc(kept, 4)
                nc.gpsimd.memset(ub[:, :, 0:1], 0.0).then_inc(zeroed, 1)

                def keep(n, u, dst):
                    pool.wait_ge(taken, n + (1 + 4))
                    s = ub[:, u, 1 + T:].rearrange("p (b t) -> p b t", t=TS + 1)
                    nc.gpsimd.tensor_copy(dst[:, :, 0:1], ub[:, u:u + 1, T:T + 1])
                    nc.gpsimd.tensor_copy(dst[:, :, 1:].rearrange("p a b -> p b a"), s[:, :, TS:TS + 1]).then_inc(kept, 1)

                with pool.Fori(0, 3) as i:
                    for g in range(8):
                        keep(i * 8 + g, g % 4, lastT[:, ds(i * 8 + g, 1), :])
                keep(24, 0, lastT[:, 24:25, :])

            @block.vector
            def _(dve):
                dve.sem_inc(mixed, 4)
                own = Chain(dve, sem("sh_dve"))
                dve.wait_ge(zeroed, 1)

                def mix(n, u, zt, mu):
                    dve.wait_ge(taken, n + (1 + 4))
                    s = ub[:, u, 1 + T:].rearrange("p (b t) -> p b t", t=TS + 1)
                    zp = zt[:, :, 0:T].rearrange("p a t -> p (a t)")
                    zs = zt[:, :, T:NT].rearrange("p a (b t) -> p (a b) t", t=TS)
                    nc.vector.tensor_tensor(zp, ub[:, u, 0:T], ub[:, u, 1:1 + T], ALU.subtract)
                    own(nc.vector.tensor_tensor(zs, s[:, :, 0:TS], s[:, :, 1:], ALU.subtract))
                    nc.vector.scalar_tensor_tensor(out=zs, in0=zs, scalar=mu, in1=s[:, :, 1:], op0=ALU.mult, op1=ALU.add)
                    nc.vector.scalar_tensor_tensor(out=zp, in0=zp, scalar=mu, in1=ub[:, u, 1:1 + T], op0=ALU.mult, op1=ALU.add).then_inc(mixed, 1)

                at = VEC["mu_shift"][0]
                with dve.Fori(0, 3) as i:
                    own.body(i, 8)
                    for g in range(8):
                        mix(i * 8 + g, g % 4, z[:, ds(i * 8 + g, 1), :], vecs[:, ds(i * 8 + (g + at), 1)])
                own.end(3)
                mix(24, 0, z[:, 24:25, :], vec("mu_shift", 24))

    project_shift()

    def low_rank():
        v = Carve(ringflat)
        lora = v(RW)
        th = v(NT)
        lora_in, tanhed, made, taken = sem("lr_in"), sem("lr_tanh"), sem("lr_made"), sem("lr_taken")
        with nc.Block() as block:
            @block.sync
            def _(sp):
                sp.dma_start(lora[0:64, :], a["w_lora_w"][0]).then_inc(lora_in, 16)
                sp.dma_start(lora[64:128, :], a["w_lora_a"][0]).then_inc(lora_in, 16)

            @block.tensor
            def _(pe):
                pe.wait_ge(lora_in, 32)
                for g in range(16):
                    t, e = g // 2, g % 2
                    if g == 0:
                        pe.wait_ge(tanhed, 1)
                    if g >= 4:
                        pe.wait_ge(taken, g - 3)
                    rhs = th[0:64, :] if e == 0 else z[64:128, 24, :]
                    nc.tensor.matmul(bank[g % 4][:, 0:NT], lora[64 * e:64 * e + 64, t * P:(t + 1) * P], rhs, start=True, stop=True).then_inc(made, 1)

            @block.scalar
            def _(act):
                nc.scalar.activation(th[0:64, :], z[0:64, 24, :], ACT.Tanh).then_inc(tanhed, 1)
                for g in range(16):
                    t, e = g // 2, g % 2
                    act.wait_ge(made, g + 1)
                    nc.scalar.activation((rate if e else decay_in)[:, t, :], bank[g % 4][:, 0:NT], ACT.Sigmoid,
                                         bias=vec("a0" if e else "w0", t)).then_inc(taken, 1)

    low_rank()

    def recurrence():
        PAD = 3 * P
        v = Carve(ringflat)
        lw, lg, kk0, kk, k2, bb, bon, tmp = (v(NT) for _ in range(8))
        before, to_end = v(NT), v(NT)
        dec, inv, rk = v(NT), v(NT), v(NT)
        AR = v(2, PAD)
        bT, kT, bE, kE, vP = (v(PAD) for _ in range(5))
        tm = v(4, 3, P)
        GM = v(3, 4, P)
        Np, NTp = v(2, 3, P), v(2, 3, P)
        N0 = v(3, P)
        Z = v(3, P)
        Bm, Vm, Wm = v(2, 512), v(2, 512), v(2, 512)
        v2 = Carve(work, rwkv_work)
        PTc = v2(24, HD)
        Qc = v2(24, HD)
        S = v2(17, HD)
        S0 = v2(DB, HD)
        S1 = v2(DB, HD)
        v3 = v
        Rh = v3(PAD)
        y = v3(NT)
        srows = v2(DB, P)
        orows = GM.rearrange("p a b c -> p (a b c)")[:, 0:(1 + DB) * P].rearrange("p (a b) -> p a b", b=P)
        yc, yq = lw, lg
        state_in, state_out = sem("rw_state_in"), sem("rw_state_out")
        LV = range(4)
        PE = Steps(sem("rw_pe"), ["norms", "bonus", "states", "rows"] + [
            f"{n}{e}" for e in (0, 1) for n in ["gram", "ngram", "mv"] + [x for l in LV for x in (
                [f"apply{l}_"] + [f"sqT{l}_"] * (l < 3) + [f"sq{l}_"] * (l < 2))]
            + ["rhat", "p0_", "q0_", "p1_", "q1_", "p2_", "q2_", "y"]] + [f"scan{c}" for c in range(CH)]
            + ["sample", "read", "turned", "mean", "var"])
        DV = Steps(sem("rw_dve"), ["logs", "kk0sq", "rkprod", "clamped", "ready"] + [
            f"{n}{e}" for e in (0, 1) for n in ["gram", "ngram", "mv", "z0_", "z1_", "z2_", "z3_", "rhat",
                                                "wm0_", "wm1_", "q0_", "wm2_", "q1_", "q2_"]]
            + [f"state{c}" for c in range(CH)] + ["state_s", "y", "centred", "squared", "out"])
        AC = Steps(sem("rw_act"), ["dec", "inv", "before", "to_end", "root", "bonus", "states", "tm0", "tm1", "tm2", "tm3"] + [
            f"{n}{e}" for e in (0, 1) for n in ["alpha", "sqT0_", "sq0_", "sqT1_", "sq1_", "sqT2_", "p0_", "p1_", "p2_"]]
            + ["y", "out_p", "out_s0", "out_s1", "lnroot"])
        PL = Steps(sem("rw_pool"), ["v"] + [f"{n}{e}" for e in (0, 1) for n in ["m0_", "m1_", "m2_"]])
        zeroed = sem("rw_zeroed")
        NPAIR = NH // 2
        gram = const("gram", 2, 4, P)
        nmask = const("nmask", 2, P)
        chunk = const("chunk", 2, 8)
        halves = const("halves")

        def ends(x):
            return x[:, 0:T].rearrange("p (c t) -> p c t", t=CH)[:, :, CH - 1:CH], x[:, T:NT].rearrange("p (c t) -> p c t", t=TS)[:, :, TS - 1:TS]

        with nc.Block() as block:
            @block.sync
            def _(sp):
                sp.sem_inc(state_out, 1)
                with sp.Fori(0, NPAIR) as p:
                    sp.wait_ge(PE.sem, PE.before(p))
                    for e in range(2):
                        src = a["state_wkv"][0, :, ds(p * 2 + e, 1), :, :].rearrange("b h v k -> v (b h) k")
                        sp.dma_start(srows[0:64, :, e * HD:(e + 1) * HD], src).then_inc(state_in, 16)
                    sp.wait_ge(AC.sem, AC.at("out_s1", p))
                    for e in range(2):
                        dst = o["wkv_prompt"][0, 0, ds(p * 2 + e, 1), :, :].rearrange("h v k -> v h k")
                        sp.dma_start(dst, orows[0:64, 0:1, e * HD:(e + 1) * HD]).then_inc(state_out, 16)
                        dst = o["wkv_sample"][0, :, ds(p * 2 + e, 1), :, :].rearrange("b h v k -> v (b h) k")
                        sp.dma_start(dst, orows[0:64, 1:1 + DB, e * HD:(e + 1) * HD]).then_inc(state_out, 16)
                sp.wait_ge(state_out, 64 * NPAIR + 1)

            @block.tensor
            def _(pe):
                PE.start(pe)
                mm = nc.tensor.matmul
                with pe.Fori(0, NPAIR) as p:
                    pe.wait_ge(DV.sem, DV.at("kk0sq", p))
                    PE.done("norms", mm(bank[0][:, 0:NT], halves, tmp, start=True, stop=True))
                    pe.wait_ge(DV.sem, DV.at("rkprod", p))
                    PE.done("bonus", mm(bank[1][:, 0:NT], halves, rk, start=True, stop=True))
                    pe.wait_ge(state_in, p * 32 + 32)
                    settled(pe)
                    for b in range(DB):
                        last = nc.tensor.transpose(bank[2][:, b * HD:(b + 1) * HD], srows[0:64, b, :], ident[0:64, 0:64])
                    PE.done("states", last)
                    pe.wait_ge(DV.sem, DV.at("ready", p))
                    pe.wait_ge(PL.sem, PL.at("v", p))
                    for q, src in enumerate((AR[:, 0, :], bE, kE, vP)):
                        for j in range(3):
                            last = nc.tensor.transpose(bank[3 + q][:, j * P:(j + 1) * P], src[:, j * P:(j + 1) * P], ident)
                    PE.done("rows", last)
                    for e in range(2):
                        h = slice(64 * e, 64 * e + 64)
                        if e == 0:
                            pe.wait_ge(AC.sem, AC.at("states", p))
                        else:
                            pe.wait_ge(AC.sem, AC.at("p2_0", p))
                            pe.wait_ge(DV.sem, DV.at("q2_0", p))
                        for j in range(3):
                            js = slice(j * P, (j + 1) * P)
                            mm(bank[j][:, 0:256].rearrange("p (a b) -> p a b", b=P), bT[h, js], AR[h, :, js], start=True, stop=True)
                            last = mm(bank[j][:, 256:512].rearrange("p (a b) -> p a b", b=P), kT[h, js], AR[h, :, js], start=True, stop=True)
                        PE.done(f"gram{e}", last)
                        for j in range(3):
                            js = slice(j * P, (j + 1) * P)
                            last = mm(bank[7][:, js], AR[h, 0, js], bT[h, js], start=True, stop=True)
                        PE.done(f"ngram{e}", last)
                        if e == 0:
                            pe.wait_ge(AC.sem, AC.at("tm3", p))
                        pe.wait_ge(DV.sem, DV.at(f"gram{e}", p))
                        for j in range(3):
                            last = mm(bank[3][:, j * HD:(j + 1) * HD], GM[:, j, 2, :], tm[:, 3, j, h], start=True, stop=True)
                        PE.done(f"mv{e}", last)
                        for l in LV:
                            nt = GM[:, :, 0, :] if l == 0 else NTp[:, l % 2]
                            n = N0 if l == 0 else Np[:, l % 2]
                            if l == 0:
                                pe.wait_ge(DV.sem, DV.at(f"mv{e}", p))
                                pe.wait_ge(AC.sem, AC.at(f"alpha{e}", p))
                            else:
                                pe.wait_ge(DV.sem, DV.at(f"z{l - 1}_{e}", p))
                                pe.wait_ge(AC.sem, AC.at(f"sqT{l - 1}_{e}", p))
                            for j in range(3):
                                last = mm(bank[4][:, j * P:(j + 1) * P], nt[:, j], Z[:, j], start=True, stop=True)
                            PE.done(f"apply{l}_{e}", last)
                            if l == 0:
                                pe.wait_ge(DV.sem, DV.at(f"ngram{e}", p))
                                if e == 1:
                                    pe.wait_ge(AC.sem, AC.at("p2_0", p))
                            elif l < 3:
                                if l < 3:
                                    pe.wait_ge(AC.sem, AC.at(f"sq{l - 1}_{e}", p))
                            if l < 3:
                                for j in range(3):
                                    last = mm(bank[5][:, j * P:(j + 1) * P], n[:, j], nt[:, j], start=True, stop=True)
                                PE.done(f"sqT{l}_{e}", last)
                            if l < 2:
                                for j in range(3):
                                    last = mm(bank[6][:, j * P:(j + 1) * P], nt[:, j], n[:, j], start=True, stop=True)
                                PE.done(f"sq{l}_{e}", last)
                        pe.wait_ge(DV.sem, DV.at(f"z3_{e}", p))
                        for j in range(3):
                            js = slice(j * P, (j + 1) * P)
                            last = mm(bank[7][h, js], Z[:, j, 0:HD], GM[:, j, 1, :], start=True, stop=True)
                        PE.done(f"rhat{e}", last)
                        for j in range(3):
                            bp, bq = bank[2 * (j % 2)], bank[1 + 2 * (j % 2)]
                            pe.wait_ge(PL.sem, PL.at(f"m{j}_{e}", p))
                            if j == 2:
                                pe.wait_ge(AC.sem, AC.at(f"p0_{e}", p))
                            PE.done(f"p{j}_{e}", mm(bp[h, :], Z[:, j, 0:HD], Bm[:, j % 2, :], start=True, stop=True))
                            pe.wait_ge(DV.sem, DV.at(f"wm{j}_{e}", p))
                            if j == 2:
                                pe.wait_ge(DV.sem, DV.at(f"q0_{e}", p))
                            mm(bq[h, :], tm[:, 2, j, h], Vm[:, j % 2, :], start=True, stop=False)
                            PE.done(f"q{j}_{e}", mm(bq[h, :], tm[:, 1, j, h], Wm[:, j % 2, :], start=False, stop=True))
                        pe.wait_ge(AC.sem, AC.at(f"sqT2_{e}", p))
                        ybank = bank[5] if e == 0 else bank[6]
                        for j in range(3):
                            js = slice(j * P, (j + 1) * P)
                            mm(ybank[h, js], tm[:, 3, j, h], GM[:, j, 3, :], start=True, stop=False)
                            last = mm(ybank[h, js], Z[:, j, HD:P], GM[:, j, 1, :], start=False, stop=True)
                        PE.done(f"y{e}", last)
                        if e == 0:
                            pe.wait_ge(AC.sem, AC.at("p2_0", p))
                    pe.wait_ge(AC.sem, AC.at("p2_1", p))
                    pe.wait_ge(DV.sem, DV.at("q2_1", p))
                    pe.wait_ge(DV.sem, DV.at("rhat1", p))
                    for c in range(CH):
                        if c:
                            pe.wait_ge(DV.sem, DV.at(f"state{c - 1}", p))
                        settled(pe)
                        sp_ = bank[3] if c % 2 else bank[7]
                        for e in range(2):
                            h = slice(64 * e, 64 * e + 64)
                            last = mm(sp_[h, 0:HD], PTc[h, c, :], S[h, c, :], start=True, stop=True)
                        PE.done(f"scan{c}", last)
                        for e in range(2):
                            h = slice(64 * e, 64 * e + 64)
                            mm(bank[4][h, c * CH:(c + 1) * CH], S[h, c, :], Rh[h, c * CH:(c + 1) * CH], start=True, stop=True)
                    for b in range(DB):
                        for e in range(2):
                            h = slice(64 * e, 64 * e + 64)
                            last = mm(bank[0][h, b * HD:(b + 1) * HD], PTc[h, 16 + b, :], S0[h, b, :], start=True, stop=True)
                    PE.done("sample", last)
                    for b in range(DB):
                        for e in range(2):
                            h = slice(64 * e, 64 * e + 64)
                            cs = slice(T + b * TS, T + (b + 1) * TS)
                            last = mm(bank[4][h, cs], S0[h, b, :], Rh[h, cs], start=True, stop=True)
                    PE.done("read", last)
                    pe.wait_ge(DV.sem, DV.at("state_s", p))
                    settled(pe)
                    nc.tensor.transpose(bank[1][0:64, 0:P], S[:, CH, :], ident)
                    for b in range(DB):
                        last = nc.tensor.transpose(bank[2 + b // 4][0:64, (b % 4) * P:(b % 4 + 1) * P], S1[:, b, :], ident)
                    PE.done("turned", last)
                    pe.wait_ge(DV.sem, DV.at("y", p))
                    PE.done("mean", mm(bank[5][:, 0:NT], halves, y, start=True, stop=True))
                    pe.wait_ge(DV.sem, DV.at("squared", p))
                    PE.done("var", mm(bank[6][:, 0:NT], halves, yq, start=True, stop=True))
                    PE.turn()

            @block.scalar
            def _(act):
                AC.start(act)
                own = Chain(act, sem("rw_act_own"))
                with act.Fori(0, NPAIR) as p:
                    own.body(p, 1)
                    act.wait_ge(DV.sem, DV.at("logs", p))
                    act.wait_ge(PE.sem, PE.before(p))
                    AC.done("dec", nc.scalar.activation(dec, lg, ACT.Exp))
                    AC.done("inv", nc.scalar.activation(inv, lg, ACT.Exp, scale=-1.0))
                    AC.done("before", nc.scalar.activation(before, before, ACT.Exp))
                    AC.done("to_end", nc.scalar.activation(to_end, to_end, ACT.Exp))
                    act.wait_ge(DV.sem, DV.at("clamped", p))
                    AC.done("root", nc.scalar.activation(bb, bb, ACT.Sqrt))
                    act.wait_ge(PE.sem, PE.at("bonus", p))
                    AC.done("bonus", nc.scalar.copy(bon, bank[1][:, 0:NT]))
                    act.wait_ge(PE.sem, PE.at("states", p))
                    AC.done("states", nc.scalar.copy(S0, bank[2][:, :].rearrange("p (b v) -> p b v", v=HD)))
                    act.wait_ge(PE.sem, PE.at("rows", p))
                    for q in range(4):
                        src = bank[3 + q][:, 0:3 * P].rearrange("p (a b) -> p a b", b=P)
                        AC.done(f"tm{q}", nc.scalar.mul(tm[:, q], src, -1.0 if q == 1 else 1.0))
                    for e in range(2):
                        h = slice(64 * e, 64 * e + 64)
                        if e == 0:
                            act.wait_ge(AC.sem, AC.at("tm3", p))
                        else:
                            act.wait_ge(PE.sem, PE.at("y0", p))
                        AC.done(f"alpha{e}", nc.scalar.copy(Z[:, :, 0:HD], tm[:, 0, :, h]))
                        for l in range(3):
                            act.wait_ge(PE.sem, PE.at(f"sqT{l}_{e}", p))
                            AC.done(f"sqT{l}_{e}", nc.scalar.copy(NTp[:, (l + 1) % 2], bank[5][:, 0:3 * P].rearrange("p (a b) -> p a b", b=P)))
                            if l < 2:
                                act.wait_ge(PE.sem, PE.at(f"sq{l}_{e}", p))
                                AC.done(f"sq{l}_{e}", nc.scalar.copy(Np[:, (l + 1) % 2], bank[6][:, 0:3 * P].rearrange("p (a b) -> p a b", b=P)))
                        for j in range(3):
                            act.wait_ge(PE.sem, PE.at(f"p{j}_{e}", p))
                            if j == 2 and e == 0:
                                act.wait_ge(PE.sem, PE.at("y0", p))
                                own(nc.scalar.copy(y[0:64, :], bank[5][0:64, 0:NT]))
                            AC.done(f"p{j}_{e}", nc.scalar.copy(PTc[h, 8 * j:8 * j + 8, :], bank[2 * (j % 2)][h, :].rearrange("p (c k) -> p c k", k=HD)))
                    act.wait_ge(PE.sem, PE.at("y1", p))
                    AC.done("y", nc.scalar.copy(y[64:128, :], bank[6][64:128, 0:NT]))
                    act.wait_ge(PE.sem, PE.at("turned", p))
                    act.wait_ge(state_out, p * 64 + 1)
                    AC.done("out_p", nc.scalar.copy(orows[0:64, 0, :], bank[1][0:64, 0:P]))
                    for s in range(2):
                        AC.done(f"out_s{s}", nc.scalar.copy(orows[0:64, 1 + 4 * s:5 + 4 * s, :], bank[2 + s][0:64, :].rearrange("p (b k) -> p b k", k=P)))
                    act.wait_ge(PE.sem, PE.at("var", p))
                    AC.done("lnroot", nc.scalar.activation(yq, bank[6][:, 0:NT], ACT.Sqrt, bias=const("eps")[:, 1:2], scale=1.0 / HD))
                    AC.turn()
                    own.end(NPAIR)

            @block.gpsimd
            def _(pool):
                PL.start(pool)
                for t in (AR[:, :, NT:PAD], bT[:, NT:PAD], kT[:, NT:PAD], bE[:, NT:PAD], kE[:, NT:PAD], vP[:, NT:PAD]):
                    nc.gpsimd.memset(t, 0.0).then_inc(zeroed, 1)
                nc.gpsimd.memset(S[:, 0, :], 0.0).then_inc(zeroed, 1)
                with pool.Fori(0, NPAIR) as p:
                    pool.wait_ge(PE.sem, PE.before(p))
                    PL.done("v", nc.gpsimd.tensor_copy(vP[:, 0:NT], z[:, ds(p + 16, 1), :].rearrange("p a t -> p (a t)")))
                    pool.wait_ge(AC.sem, AC.at("tm3", p))
                    for e in range(2):
                        h = slice(64 * e, 64 * e + 64)
                        for j in range(3):
                            if j == 2:
                                pool.wait_ge(PE.sem, PE.at(f"q0_{e}", p))
                            elif e == 1:
                                pool.wait_ge(PE.sem, PE.at("q2_0", p))
                            m = chunk[:, j // 2, :].unsqueeze(2).to_broadcast([P, 8, HD])
                            for dst, q in ((Bm, 1), (Vm, 3)):
                                src = tm[:, q, j, h].unsqueeze(1).to_broadcast([P, 8, HD])
                                last = nc.gpsimd.tensor_tensor(dst[:, j % 2, :].rearrange("p (c k) -> p c k", k=HD), src, m, ALU.mult)
                            PL.done(f"m{j}_{e}", last)
                    PL.turn()

            @block.vector
            def _(dve):
                DV.start(dve)
                own = Chain(dve, sem("rw_dve_own"))
                tt = nc.vector.tensor_tensor
                dve.wait_ge(zeroed, 7)
                with dve.Fori(0, NPAIR) as p:
                    own.body(p, 43)

                    def zt(base):
                        return z[:, ds(p + base, 1), :].rearrange("p a t -> p (a t)")

                    def pv(name):
                        return vecs[:, ds(p + VEC[name][0], 1)]

                    dve.wait_ge(PE.sem, PE.before(p))
                    dve.wait_ge(AC.sem, AC.before(p))
                    dve.wait_ge(PL.sem, PL.before(p))
                    dve.wait_ge(DV.sem, DV.before(p))
                    own(nc.vector.tensor_scalar(lw, decay_in[:, ds(p, 1), :].rearrange("p a t -> p (a t)"), -float(np.exp(-0.5)), None, ALU.mult))
                    own(nc.vector.tensor_tensor_scan(lg, const("reset"), lw, 0.0, ALU.mult, ALU.add))
                    own(tt(before, lg, lw, ALU.subtract))
                    ep, es = ends(lg)
                    own(tt(to_end[:, 0:T].rearrange("p (c t) -> p c t", t=CH), ep.to_broadcast([P, 16, CH]), lg[:, 0:T].rearrange("p (c t) -> p c t", t=CH), ALU.subtract))
                    DV.done("logs", tt(to_end[:, T:NT].rearrange("p (c t) -> p c t", t=TS), es.to_broadcast([P, 8, TS]), lg[:, T:NT].rearrange("p (c t) -> p c t", t=TS), ALU.subtract))
                    own(nc.vector.tensor_scalar(kk0, zt(8), pv("k_k"), None, ALU.mult))
                    DV.done("kk0sq", tt(tmp, kk0, kk0, ALU.mult))
                    own(nc.vector.tensor_scalar(kk, rate[:, ds(p, 1), :].rearrange("p a t -> p (a t)"), -1.0, pv("k_a"), ALU.add, ALU.mult))
                    own(nc.vector.scalar_tensor_tensor(out=k2, in0=kk, scalar=1.0, in1=zt(8), op0=ALU.add, op1=ALU.mult))
                    DV.done("rkprod", nc.vector.scalar_tensor_tensor(out=rk, in0=zt(0), scalar=pv("r_k"), in1=k2, op0=ALU.mult, op1=ALU.mult))
                    dve.wait_ge(PE.sem, PE.at("norms", p))
                    DV.done("clamped", nc.vector.tensor_scalar(bb, bank[0][:, 0:NT], 1e-24, None, ALU.max))
                    dve.wait_ge(AC.sem, AC.at("root", p))
                    own(nc.vector.reciprocal(kk, bb))
                    own(tt(kk, kk, kk0, ALU.mult))
                    own(tt(bb, kk, rate[:, ds(p, 1), :].rearrange("p a t -> p (a t)"), ALU.mult))
                    own(tt(AR[:, 0, 0:NT], before, kk, ALU.mult))
                    own(tt(AR[:, 1, 0:NT], dec, zt(0), ALU.mult))
                    own(tt(bT[:, 0:NT], bb, inv, ALU.mult))
                    own(tt(kT[:, 0:NT], k2, inv, ALU.mult))
                    own(tt(bE[:, 0:NT], bb, to_end, ALU.mult))
                    DV.done("ready", tt(kE[:, 0:NT], k2, to_end, ALU.mult))
                    for e in range(2):
                        h = slice(64 * e, 64 * e + 64)
                        dve.wait_ge(PE.sem, PE.at(f"gram{e}", p))
                        if e == 0:
                            dve.wait_ge(state_out, p * 64 + 1)
                        for j in range(3):
                            ins = tt(GM[:, j], bank[j][:, :].rearrange("p (a b) -> p a b", b=P), gram[:, j // 2], ALU.mult)
                            if j < 2:
                                own(ins)
                            else:
                                DV.done(f"gram{e}", ins)
                        dve.wait_ge(PE.sem, PE.at(f"ngram{e}", p))
                        own(tt(N0[:, 0:2], bank[7][:, 0:2 * P].rearrange("p (a b) -> p a b", b=P), nmask[:, 0:1, :].to_broadcast([P, 2, P]), ALU.mult))
                        DV.done(f"ngram{e}", tt(N0[:, 2], bank[7][:, 2 * P:3 * P], nmask[:, 1], ALU.mult))
                        dve.wait_ge(PE.sem, PE.at(f"mv{e}", p))
                        if e == 1:
                            dve.wait_ge(PE.sem, PE.at("y0", p))
                        DV.done(f"mv{e}", nc.vector.tensor_copy(Z[:, :, HD:P], bank[3][:, 0:3 * HD].rearrange("p (a b) -> p a b", b=HD)))
                        for l in LV:
                            dve.wait_ge(PE.sem, PE.at(f"apply{l}_{e}", p))
                            if l == 0:
                                dve.wait_ge(DV.sem, DV.at(f"mv{e}", p))
                                dve.wait_ge(AC.sem, AC.at(f"alpha{e}", p))
                            else:
                                dve.wait_ge(DV.sem, DV.at(f"z{l - 1}_{e}", p))
                            DV.done(f"z{l}_{e}", tt(Z, Z, bank[4][:, 0:3 * P].rearrange("p (a b) -> p a b", b=P), ALU.add))
                        dve.wait_ge(PE.sem, PE.at(f"rhat{e}", p))
                        DV.done(f"rhat{e}", tt(Rh[h, :], AR[h, 1, :], bank[7][h, 0:PAD], ALU.add))
                        dve.wait_ge(DV.sem, DV.at(f"z3_{e}", p))

                        def wm(j):
                            m = chunk[:, j // 2, :].unsqueeze(2).to_broadcast([P, 8, HD])
                            src = Z[:, j, HD:P].unsqueeze(1).to_broadcast([P, 8, HD])
                            DV.done(f"wm{j}_{e}", tt(Wm[:, j % 2, :].rearrange("p (c k) -> p c k", k=HD), src, m, ALU.mult))

                        def qc(j):
                            dve.wait_ge(PE.sem, PE.at(f"q{j}_{e}", p))
                            DV.done(f"q{j}_{e}", nc.vector.tensor_copy(Qc[h, 8 * j:8 * j + 8, :], bank[1 + 2 * (j % 2)][h, :].rearrange("p (c k) -> p c k", k=HD)))

                        wm(0)
                        wm(1)
                        qc(0)
                        wm(2)
                        qc(1)
                        qc(2)
                    dve.wait_ge(DV.sem, DV.at("q2_1", p))
                    for c in range(CH):
                        if c:
                            dve.wait_ge(DV.sem, DV.at(f"state{c - 1}", p))
                        end = c * CH + CH - 1
                        own(nc.vector.scalar_tensor_tensor(out=S[:, c + 1, :], in0=S[:, c, :], scalar=dec[:, end:end + 1], in1=Qc[:, c, :], op0=ALU.mult, op1=ALU.add))
                        dve.wait_ge(PE.sem, PE.at(f"scan{c}", p))
                        DV.done(f"state{c}", tt(S[:, c + 1, :], S[:, c + 1, :], (bank[3] if c % 2 else bank[7])[:, 0:HD], ALU.add))
                    _, es = ends(dec)
                    own(tt(S1, S0, es.to_broadcast([P, DB, HD]), ALU.mult))
                    own(tt(S1, S1, Qc[:, 16:24, :], ALU.add))
                    dve.wait_ge(PE.sem, PE.at("sample", p))
                    DV.done("state_s", tt(S1, S1, bank[0][:, :].rearrange("p (b v) -> p b v", v=HD), ALU.add))
                    dve.wait_ge(PE.sem, PE.at("read", p))
                    dve.wait_ge(AC.sem, AC.at("y", p))
                    DV.done("y", tt(y, y, bank[4][:, 0:NT], ALU.add))
                    dve.wait_ge(PE.sem, PE.at("mean", p))
                    DV.done("centred", nc.vector.scalar_tensor_tensor(out=yc, in0=bank[5][:, 0:NT], scalar=-1.0 / HD, in1=y, op0=ALU.mult, op1=ALU.add))
                    dve.wait_ge(DV.sem, DV.at("centred", p))
                    DV.done("squared", tt(yq, yc, yc, ALU.mult))
                    dve.wait_ge(AC.sem, AC.at("lnroot", p))
                    own(nc.vector.reciprocal(yq, yq))
                    own(tt(yc, yc, yq, ALU.mult))
                    own(nc.vector.tensor_scalar(yc, yc, pv("ln_x_w"), pv("ln_x_b"), ALU.mult, ALU.add))
                    own(tt(bon, bon, zt(16), ALU.mult))
                    DV.done("out", tt(yT[:, ds(p, 1), :].rearrange("p a t -> p (a t)"), yc, bon, ALU.add))
                    DV.turn()
                own.end(NPAIR)

    recurrence()
    w = Carve(work, 8 * NT)
    mT = w(KD, NT)

    def merge():
        sg = w(4, NT)
        pr = w(4, NT)
        landed = [sem(f"mg_landed{i}") for i in range(4)]
        used, made, gated, merged = sem("mg_used"), sem("mg_made"), sem("mg_gated"), sem("mg_merged")
        half = DM // 2
        wi = a["w_in"].rearrange("l (k p) c -> p (l k) c", p=P)[:, :, C_MERGE:]
        wa = a["w_branch_a"].rearrange("l (k p) c -> p (l k) c", p=P)
        wb = a["w_branch_b"].rearrange("l (k p) c -> p (l k) c", p=P)
        big = [ring[:, i, :].rearrange("p (k n) -> p k n", n=256) for i in range(2)]
        small = [ring[:, i, 0:2048].rearrange("p (k n) -> p k n", n=256) for i in (2, 3)]
        with nc.Block() as block:
            @block.sync
            def _(sp):
                with sp.Fori(0, 8) as i:
                    for s, (dst, src) in enumerate(((big[0], wi[:, :, ds(i * 256, 256)]), (big[1], wi[:, :, ds(i * 256 + DM, 256)]),
                                                    (small[0], wa[:, :, ds(i * 256, 256)]), (small[1], wb[:, :, ds(i * 256, 256)]))):
                        sp.wait_ge(used, i * 4 + (s + 1))
                        settled(sp)
                        sp.dma_start(dst, src).then_inc(landed[s], 16)

            @block.tensor
            def _(pe):
                pe.sem_inc(used, 4)
                with pe.Fori(0, 8) as i:
                    for s, (src, wt, nk) in enumerate(((nT, big[0], KD), (nT, big[1], KD), (oT, small[0], 8), (yT, small[1], 8))):
                        pe.wait_ge(landed[s], i * 16 + 16)
                        for h in range(2):
                            if s < 2:
                                pe.wait_ge(gated, i * 4 + (2 * s + h + 1))
                            else:
                                pe.wait_ge(merged, i * 2 + (h + 1))
                            for k in range(nk):
                                last = nc.tensor.matmul(bank[2 * s + h][:, 0:NT], wt[:, k, h * P:(h + 1) * P], src[:, k, :], start=k == 0, stop=k == nk - 1)
                            last.then_inc(made, 1)
                        pe.wait_ge(made, i * 8 + 2 * s + 2)
                        pe.sem_inc(used, 1)

            @block.scalar
            def _(act):
                act.sem_inc(gated, 4)
                with act.Fori(0, 8) as i:
                    act.wait_ge(merged, i * 2 + 2)
                    for s in range(4):
                        act.wait_ge(made, i * 8 + (s + 1))
                        nc.scalar.activation(sg[:, s, :], bank[s][:, 0:NT], ACT.Sigmoid).then_inc(gated, 1)

            @block.vector
            def _(dve):
                dve.sem_inc(merged, 2)
                own = Chain(dve, sem("mg_dve"))
                with dve.Fori(0, 8) as i:
                    own.body(i, 4)
                    for h in range(2):
                        for s in range(2):
                            dve.wait_ge(gated, i * 4 + (2 * s + h + 1 + 4))
                            dve.wait_ge(made, i * 8 + (4 + 2 * s + h + 1))
                            own(nc.vector.tensor_tensor(pr[:, 2 * s + h, :], sg[:, 2 * s + h, :], bank[4 + 2 * s + h][:, 0:NT], ALU.mult))
                        nc.vector.tensor_tensor(mT[:, ds(i * 2 + h, 1), :].rearrange("p a t -> p (a t)"), pr[:, h, :], pr[:, 2 + h, :], ALU.add).then_inc(merged, 1)
                    dve.wait_ge(merged, i * 2 + 4)
                own.end(8)

    merge()

    def project_out():
        landed = [sem(f"wo_landed{i}") for i in range(4)]
        used, made, added = sem("wo_used"), sem("wo_made"), sem("wo_added")
        squared, summed, rooted, inverted = sem("wo_squared"), sem("wo_summed"), sem("wo_rooted"), sem("wo_inverted")
        v = Carve(work, 0)
        sq, rms, rstd = v(2, NT), v(NT), v(NT)
        wv = a["w_out"].rearrange("l (k p) c -> p (l k) c", p=P)
        slot = [ring[:, i, :].rearrange("p (k n) -> p k n", n=256) for i in range(4)]
        with nc.Block() as block:
            @block.sync
            def _(sp):
                with sp.Fori(0, 2) as i:
                    for c in range(4):
                        sp.wait_ge(used, i * 4 + (c + 1))
                        sp.dma_start(slot[c], wv[:, :, ds(i * 1024 + c * 256, 256)]).then_inc(landed[c], 16)

            @block.tensor
            def _(pe):
                pe.sem_inc(used, 4)
                with pe.Fori(0, 2) as i:
                    for c in range(4):
                        pe.wait_ge(landed[c], i * 16 + 16)
                        for h in range(2):
                            g = 2 * c + h
                            pe.wait_ge(added, i * 8 + (g + 1))
                            for k in range(KD):
                                last = nc.tensor.matmul(bank[g][:, 0:NT], slot[c][:, k, h * P:(h + 1) * P], mT[:, k, :], start=k == 0, stop=k == KD - 1)
                            last.then_inc(made, 1)
                        pe.wait_ge(made, i * 8 + 2 * c + 2)
                        pe.sem_inc(used, 1)
                pe.wait_ge(added, KD + 8)
                for k in range(KD):
                    pe.wait_ge(squared, k + 1)
                    nc.tensor.matmul(bank[0][:, 0:NT], const("ones"), sq[:, k % 2, :], start=k == 0, stop=k == KD - 1).then_inc(summed, 1)

            @block.vector
            def _(dve):
                dve.sem_inc(added, 8)
                with dve.Fori(0, 2) as i:
                    for g in range(8):
                        dve.wait_ge(made, i * 8 + (g + 1))
                        x = xT[:, ds(i * 8 + g, 1), :].rearrange("p a t -> p (a t)")
                        nc.vector.tensor_tensor(x, x, bank[g][:, 0:NT], ALU.add).then_inc(added, 1)
                dve.wait_ge(added, KD + 8)
                for k in range(KD):
                    if k >= 2:
                        dve.wait_ge(summed, k - 1)
                    nc.vector.tensor_tensor(sq[:, k % 2, :], xT[:, k, :], xT[:, k, :], ALU.mult).then_inc(squared, 1)
                dve.wait_ge(rooted, 1)
                nc.vector.reciprocal(rstd, rms).then_inc(inverted, 1)
                dve.wait_ge(inverted, 1)
                for k in range(KD):
                    nc.vector.scalar_tensor_tensor(out=nT[:, k, :], in0=xT[:, k, :], scalar=vec("norm2_g", k), in1=rstd, op0=ALU.mult, op1=ALU.mult)

            @block.scalar
            def _(act):
                act.wait_ge(summed, KD)
                nc.scalar.activation(rms, bank[0][:, 0:NT], ACT.Sqrt, bias=const("eps")[:, 0:1], scale=1.0 / DM).then_inc(rooted, 1)

    project_out()

    w = Carve(work)
    NF = DFF // P
    gT = w(NF, NT)

    def up_and_conv():
        rows = work[0:2 * DB, 0:2 * DFF]
        prev = w(2 * NF, 2 * DB)
        UB = 2 + T + DB * (TS + 2)
        ub = w(4, UB)
        cb = w(4, NT)
        ov = Carve(oT[:, :, :].rearrange("p a b -> p (a b)"))
        tails = ov(8, 2 + 2 * DB)
        trow = ov(2, 512)
        landed = [sem(f"up_landed{i}") for i in range(4)]
        used, made = sem("up_used"), sem("up_made")
        rows_in, rows_t, rows_got, zeroed = sem("up_rows_in"), sem("up_rows_t"), sem("up_rows_got"), sem("up_zeroed")
        taken, tapped, mixed, active, done = sem("up_taken"), sem("up_tapped"), sem("up_mixed"), sem("up_active"), sem("up_done")
        kept, turned, copied, stored = sem("up_kept"), sem("up_turned"), sem("up_copied"), sem("up_stored")
        wv = a["w_up"].rearrange("l (k p) c -> p (l k) c", p=P)
        slot = [ring[:, i, :].rearrange("p (k n) -> p k n", n=256) for i in range(4)]
        NTURN = NF // 4

        def seg(x, lo, n, width):
            base = 2 if width > TS else 0
            s = x[:, base + T:].rearrange("p (b t) -> p b t", t=width)
            return x[:, lo:lo + T], s[:, :, lo:lo + TS]

        with nc.Block() as block:
            @block.sync
            def _(sp):
                sp.dma_start(rows, a["state_conv"].rearrange("l b w c -> (l b w) c")).then_inc(rows_in, 16)

                with sp.Fori(0, NTURN) as i:
                    for c in range(4):
                        sp.wait_ge(used, i * 4 + (2 * (c // 2) + 2))
                        sp.dma_start(slot[c], wv[:, :, ds(i * 512 + ((c // 2) * 256 + (c % 2) * DFF), 256)]).then_inc(landed[c], 16)

            @block.tensor
            def _(pe):
                pe.sem_inc(used, 4)
                pe.sem_inc(turned, 1)
                pe.wait_ge(rows_in, 16)
                for g in range(3):
                    for t in range(32 * g, min(32 * g + 32, 2 * NF)):
                        last = nc.tensor.transpose(bank[g][:, 16 * (t - 32 * g):16 * (t - 32 * g) + 16], rows[:, t * P:(t + 1) * P], ident[0:2 * DB, 0:2 * DB])
                last.then_inc(rows_t, 1)
                pe.wait_ge(rows_got, 3)

                def tails_to_rows(i):
                    pe.wait_ge(kept, i * 8 + (8 + 4))
                    pe.wait_ge(copied, i * 2 + 1)
                    for s in range(2):
                        for q in range(4):
                            last = nc.tensor.transpose(bank[6 + s][0:2 + 2 * DB, q * P:(q + 1) * P], tails[:, 4 * s + q, :], ident)
                    last.then_inc(turned, 1)

                def turn(i, first):
                    for c in range(0, 4, 2):
                        for h in range(2):
                            for v in range(2):
                                g = 2 * c + 2 * h + v
                                if h == 0:
                                    pe.wait_ge(landed[c + v], i * 16 + 16)
                                pe.wait_ge(taken, i * 8 + (g + 3 if g >= 6 else g + 7 if g < 2 else g + 1))
                                for k in range(KD):
                                    last = nc.tensor.matmul(bank[g % 6][:, 0:NT], slot[c + v][:, k, h * P:(h + 1) * P], nT[:, k, :], start=k == 0, stop=k == KD - 1)
                                last.then_inc(made, 1)
                                if g == 2 and not first:
                                    tails_to_rows(i - 1)
                        pe.wait_ge(made, i * 8 + (2 * c + 4))
                        pe.sem_inc(used, 2)

                turn(0, True)
                with pe.Fori(1, NTURN) as i:
                    turn(i, False)
                tails_to_rows(NTURN - 1)

            @block.scalar
            def _(act):
                act.sem_inc(stored, 1)
                act.sem_inc(taken, 8)
                act.sem_inc(copied, 1)
                own = Chain(act, sem("up_act_own"))
                act.wait_ge(rows_t, 1)
                for g in range(3):
                    n = min(32, 2 * NF - 32 * g)
                    nc.scalar.copy(prev[:, 32 * g:32 * g + n, :], bank[g][:, 0:16 * n].rearrange("p (a b) -> p a b", b=16)).then_inc(rows_got, 1)
                act.wait_ge(rows_got, 3)
                act.wait_ge(zeroed, 1)

                def rows_out(i):
                    act.wait_ge(turned, i + 2)
                    act.wait_ge(stored, i * 64 + 1)
                    for s in range(2):
                        nc.scalar.copy(trow[0:2 + 2 * DB, s, :], bank[6 + s][0:2 + 2 * DB, :]).then_inc(copied, 1)
                    act.wait_ge(copied, i * 2 + (2 + 1))
                    for s in range(2):
                        cols = ds(i * 512 + s * DFF, 512)
                        act.dma_start(o["conv_prompt"][0, 0, :, cols], trow[0:2, s, :]).then_inc(stored, 16)
                        act.dma_start(o["conv_sample"].rearrange("l b w c -> (l b w) c")[:, cols], trow[2:2 + 2 * DB, s, :]).then_inc(stored, 16)

                def turn(i, first):
                    for g in range(8):
                        if g == 4 and not first:
                            rows_out(i - 1)
                        f, v = g // 2, g % 2
                        u = g % 4
                        act.wait_ge(made, i * 8 + (g + 1))
                        act.wait_ge(mixed, i * 8 + (g + 1))
                        act.wait_ge(kept, i * 8 + (g + 1))
                        s = ub[:, u, 2 + T:].rearrange("p (b t) -> p b t", t=TS + 2)
                        pr = prev[:, ds(i * 4 + (f + v * NF), 1), :].rearrange("p a (b j) -> p (a b) j", j=2)
                        nc.scalar.copy(s[:, :, 0:2], pr)
                        nc.scalar.copy(s[:, :, 2:], bank[g % 6][:, T:NT].rearrange("p (b t) -> p b t", t=TS))
                        nc.scalar.copy(ub[:, u, 2:2 + T], bank[g % 6][:, 0:T]).then_inc(taken, 1)
                        if v == 1:
                            act.wait_ge(mixed, i * 8 + (g + 1 + 4))
                            nc.scalar.activation(cb[:, u - 1, :], cb[:, u - 1, :], ACT.Silu).then_inc(active, 1)

                turn(0, True)
                with act.Fori(1, NTURN) as i:
                    turn(i, False)
                rows_out(NTURN - 1)
                act.wait_ge(stored, 64 * NTURN + 1)

            @block.gpsimd
            def _(pool):
                pool.sem_inc(kept, 4)
                nc.gpsimd.memset(ub[:, :, 0:2], 0.0).then_inc(zeroed, 1)
                with pool.Fori(0, NTURN) as i:
                    for g in range(8):
                        f, v = g // 2, g % 2
                        pool.wait_ge(taken, i * 8 + (g + 1 + 8))
                        pool.wait_ge(turned, i + 1)
                        settled(pool)
                        u = g % 4
                        s = ub[:, u, 2 + T:].rearrange("p (b t) -> p b t", t=TS + 2)
                        dst = tails[:, 4 * v + f, :]
                        nc.gpsimd.tensor_copy(dst[:, 0:2], ub[:, u, T:T + 2])
                        nc.gpsimd.tensor_copy(dst[:, 2:].rearrange("p (b j) -> p b j", j=2), s[:, :, TS:TS + 2]).then_inc(kept, 1)

            @block.vector
            def _(dve):
                dve.sem_inc(mixed, 4)
                dve.sem_inc(done, 2)
                own = Chain(dve, sem("up_dve_own"))
                stt = nc.vector.scalar_tensor_tensor
                dve.wait_ge(zeroed, 1)
                with dve.Fori(0, NTURN) as i:
                    own.body(i, 16)
                    for g in range(8):
                        f, v = g // 2, g % 2
                        u = g % 4
                        dve.wait_ge(taken, i * 8 + (g + 1 + 8))

                        def tap(j):
                            return conv[:, j, ds(i * 4 + (f + v * NF), 1)]

                        dve.wait_ge(done, i * 4 + (f + 1))
                        cp, cs = cb[:, u, 0:T], cb[:, u, T:NT].rearrange("p (b t) -> p b t", t=TS)
                        (p0, s0), (p1, s1), (p2, s2) = (seg(ub[:, u], j, T, TS + 2) for j in range(3))
                        nc.vector.tensor_scalar(cs, s0, tap(0), tap(3), ALU.mult, ALU.add)
                        own(nc.vector.tensor_scalar(cp, p0, tap(0), tap(3), ALU.mult, ALU.add))
                        stt(out=cs, in0=s1, scalar=tap(1), in1=cs, op0=ALU.mult, op1=ALU.add)
                        own(stt(out=cp, in0=p1, scalar=tap(1), in1=cp, op0=ALU.mult, op1=ALU.add))
                        stt(out=cs, in0=s2, scalar=tap(2), in1=cs, op0=ALU.mult, op1=ALU.add)
                        stt(out=cp, in0=p2, scalar=tap(2), in1=cp, op0=ALU.mult, op1=ALU.add).then_inc(mixed, 1)
                        if v == 1:
                            dve.wait_ge(mixed, i * 8 + (g + 1 + 4))
                            dve.wait_ge(active, i * 4 + (f + 1))
                            nc.vector.tensor_tensor(gT[:, ds(i * 4 + f, 1), :].rearrange("p a t -> p (a t)"), cb[:, u - 1, :], cb[:, u, :], ALU.mult).then_inc(done, 1)
                own.end(NTURN)

    up_and_conv()

    def down():
        landed = [sem(f"dn_landed{i}") for i in range(4)]
        used, made, added, turned, copied, stored = (sem(f"dn_{n}") for n in ("used", "made", "added", "turned", "copied", "stored"))
        v = Carve(nT[:, :, :].rearrange("p a b -> p (a b)"))
        yrow = v(2, 3, 256)
        wv = a["w_down"].rearrange("l (k p) c -> p (l k) c", p=P)
        KQ = NF // 4
        slot = [ring[:, i, 0:KQ * 256].rearrange("p (k n) -> p k n", n=256) for i in range(4)]
        with nc.Block() as block:
            @block.sync
            def _(sp):
                with sp.Fori(0, 4) as i:
                    for u in range(2):
                        for c in range(4):
                            sp.wait_ge(used, i * 8 + (4 * u + c + 1))
                            sp.dma_start(slot[c], wv[:, KQ * c:KQ * (c + 1), ds(i * 512 + u * 256, 256)]).then_inc(landed[c], 16)

            @block.scalar
            def _(act):
                act.sem_inc(copied, 8)
                act.sem_inc(stored, 48)
                with act.Fori(0, 4) as i:
                    for u in range(2):
                        act.wait_ge(stored, i * 96 + (48 if u else 48))
                        for h in range(2):
                            act.wait_ge(turned, i * 4 + (2 * u + h + 1 + 4))
                            b = bank[4 + 2 * u + h]
                            nc.scalar.copy(yrow[:, u, 0:2, h * P:(h + 1) * P], b[:, 0:256].rearrange("p (a b) -> p a b", b=P)).then_inc(copied, 1)
                            nc.scalar.copy(yrow[0:64, u, 2, h * P:(h + 1) * P], b[0:64, 256:384]).then_inc(copied, 1)
                        act.wait_ge(copied, i * 8 + (4 * u + 4 + 8))
                        cols = ds(i * 512 + u * 256, 256)
                        for t, (t0, n) in enumerate(TOK):
                            dst = o["y_prompt"][0, t0:t0 + n, cols] if t < 2 else o["y_sample"].rearrange("b t d -> (b t) d")[:, cols]
                            act.dma_start(dst, yrow[0:n, u, t, :]).then_inc(stored, 16)
                act.wait_ge(stored, 96 * 4 + 48)

            @block.tensor
            def _(pe):
                pe.sem_inc(used, 4)
                pe.sem_inc(turned, 4)

                def to_rows(i, u):
                    for h in range(2):
                        pe.wait_ge(added, i * 4 + (2 * u + h + 1 + 4))
                        pe.wait_ge(copied, i * 8 + (4 * u + 2 * h + 2))
                        for t, (t0, n) in enumerate(TOK):
                            last = nc.tensor.transpose(bank[4 + 2 * u + h][0:n, t * P:(t + 1) * P], yo[:, 2 * u + h, t0:t0 + n], ident)
                        last.then_inc(turned, 1)

                def turn(i, first):
                    for u in range(2):
                        pe.wait_ge(added, i * 4 + (2 * u + 2))
                        for c in range(4):
                            if c == 1:
                                if u == 1:
                                    to_rows(i, 0)
                                elif not first:
                                    to_rows(i - 1, 1)
                            pe.wait_ge(landed[c], i * 32 + 16 * (u + 1))
                            for h in range(2):
                                for k in range(KQ):
                                    last = nc.tensor.matmul(bank[2 * u + h][:, 0:NT], slot[c][:, k, h * P:(h + 1) * P], gT[:, KQ * c + k, :],
                                                            start=c == 0 and k == 0, stop=c == 3 and k == KQ - 1)
                                last.then_inc(made, 1)
                            pe.wait_ge(made, i * 16 + (8 * u + 2 * c + 2))
                            pe.sem_inc(used, 1)

                turn(0, True)
                with pe.Fori(1, 4) as i:
                    turn(i, False)
                to_rows(3, 1)

            @block.vector
            def _(dve):
                dve.sem_inc(added, 4)
                with dve.Fori(0, 4) as i:
                    for u in range(2):
                        for h in range(2):
                            dve.wait_ge(made, i * 16 + (8 * u + 7 + h))
                            x = xT[:, ds(i * 4 + 2 * u + h, 1), :].rearrange("p a t -> p (a t)")
                            dve.wait_ge(turned, i * 4 + (2 * u + h + 1))
                            nc.vector.tensor_tensor(yo[:, 2 * u + h, :], x, bank[2 * u + h][:, 0:NT], ALU.add).then_inc(added, 1)

    yo = oT[:, 0:4, :]
    down()


INPUTS = ["x_prompt", "x_sample", "cache_kv_cmp", "cache_kv_sel", "page_table", "cache_kv_win", "state_wkv",
          "state_shift", "state_conv", "norm1_g", "w_in", "q_gain", "k_gains", "w_cmp", "mu_shift", "w0", "w_lora_w",
          "a0", "w_lora_a", "k_k", "k_a", "r_k", "ln_x_w", "ln_x_b", "w_branch_a", "w_branch_b", "w_out", "norm2_g",
          "w_up", "conv_w", "conv_b", "w_down"]
OUTPUTS = [("y_prompt", (1, T, DM)), ("y_sample", (DB, TS, DM)),
           ("kv_cmp_prompt", (1, 1, T, 2, NKV, HD)), ("kv_cmp_sample", (1, DB, TS, 2, NKV, HD)),
           ("kv_sel_prompt", (1, 1, T, 2, NKV, HD)), ("kv_sel_sample", (1, DB, TS, 2, NKV, HD)),
           ("kv_win_prompt", (1, 1, T, 2, NKV, HD)), ("kv_win_sample", (1, DB, WIN, 2, NKV, HD)),
           ("wkv_prompt", (1, 1, NH, HD, HD)), ("wkv_sample", (1, DB, NH, HD, HD)),
           ("shift_prompt", (1, 1, SHIFT)), ("shift_sample", (1, DB, SHIFT)),
           ("conv_prompt", (1, 1, 2, 2 * DFF)), ("conv_sample", (1, DB, 2, 2 * DFF))]


def kernel(**inputs):
    import concourse.bacc as bacc
    from concourse.bass_utils import run_bass_kernel_spmd

    nc = bacc.Bacc("TRN2", target_bir_lowering=False, num_devices=1)
    arrays = {name: np.ascontiguousarray(inputs[name]) for name in INPUTS}
    arrays["shape_constants"] = shape_constants()
    a = {n: nc.dram_tensor(n, v.shape, mybir.dt.from_np(v.dtype), kind="ExternalInput").ap() for n, v in arrays.items()}
    o = {n: nc.dram_tensor("out_" + n, shape, F32, kind="ExternalOutput").ap() for n, shape in OUTPUTS}
    build_layer(nc, a, o)
    got = run_bass_kernel_spmd(nc, [arrays], core_ids=[0]).results[0]
    return tuple(got["out_" + n] for n, _ in OUTPUTS)
```

```python
from contextlib import ExitStack

import numpy as np

import concourse.bass as bass
from concourse import mybir

F32 = mybir.dt.float32
F32R = mybir.dt.float32r
I32 = mybir.dt.int32
ALU = mybir.AluOpType
ACT = mybir.ActivationFunctionType
AX = mybir.AxisListType
ds = bass.ds

DM = 2048
T = 256
DB = 8
TS = 8
PAST = 2048
PAGE = 128
NH = 16
NKV = 4
HPG = NH // NKV
HD = 64
ROPE = HD // 4
THETA = 500000.0
BLOCK = 64
NSEL = 16
WIN = 512
RW = 1024
LORA = 64
LNX_EPS = 64e-5
DFF = 5632
EPS = 1e-6
NEG = -1e30

P = 128
NS = DB * TS
NT = T + NS
ATT = NH * HD
KVC = 2 * NKV * HD
SHIFT = 3 * RW + 2 * LORA
C_GATE = ATT + 3 * KVC
C_SHIFT = C_GATE + 3 * NH
C_MERGE = C_SHIFT + SHIFT
KD = DM // P
NPG = PAST // PAGE
NBLK = PAST // BLOCK
TOK = [(0, 128), (128, 128), (256, 64)]
NP_BLK = T // BLOCK
CH = 16
WORK = 18680
RING = KD * NT + 3 * 4096

CONST = {}


def _const_layout():
    at = 0
    for name, n in (("ident", 128), ("halves", 128), ("group", 128), ("blocksum", 62), ("rope", 48),
                    ("causal", 256), ("newmask", 8), ("winmask", 8), ("earlier", 1024), ("vis", 16),
                    ("gram", 1024), ("nmask", 256), ("chunk", 16), ("reset", 320), ("eps", 4), ("ones", 128)):
        CONST[name] = (at, n)
        at += n
    return at


NCONST = _const_layout()


def shape_constants():
    c = np.zeros((P, NCONST), np.float32)

    def put(name, v):
        a, n = CONST[name]
        v = np.asarray(v, np.float32)
        c[:, a:a + n] = v.reshape(v.shape[0], n)

    p = np.arange(P)
    put("ident", np.eye(P))
    put("halves", (p[:, None] // 64 == p[None, :] // 64))
    g, q = p // 32, p % 8
    put("group", (g[:, None] == g[None, :]) & (q[:, None] == q[None, :]))
    put("blocksum", np.arange(62)[None, :] == 30 + p[:, None] // BLOCK)
    inv = np.float32(THETA) ** (-np.arange(ROPE // 2, dtype=np.float32) * np.float32(2.0) / np.float32(ROPE))
    pos = np.zeros((P, 3), np.float32)
    pos[:, 0], pos[:, 1] = p, 128 + p
    pos[:, 2] = PAST + p % TS
    ang = (pos[:, :, None] * inv.astype(np.float32)).astype(np.float32)
    put("rope", np.stack([np.cos(ang.astype(np.float64)), np.sin(ang.astype(np.float64))], 2))
    m = np.zeros((P, 256))
    m[:, 128:] = np.where(p[None, :] <= p[:, None], 0, NEG)
    put("causal", m)
    put("newmask", np.where(np.arange(8)[None, :] <= q[:, None], 0, NEG))
    put("winmask", np.where(np.arange(8)[None, :] >= q[:, None], 0, NEG))
    i = np.arange(NBLK)
    put("earlier", np.broadcast_to(i[None, :] < i[:, None], (P, NBLK, NBLK)))
    b4 = np.arange(NP_BLK)
    vis = np.stack([((b4[None, :] + 1) * BLOCK - 1 <= p[:, None] + 128 * t) for t in range(2)], 1)
    put("vis", np.stack([vis, np.where(vis, 0, NEG)], 2))
    s, t = p[:, None], p[None, :]
    sets, nm = [], []
    for size, top in ((CH, 128), (TS, 64)):
        same = (s // size == t // size) & (s < top) & (t < top)
        strict, incl = same & (s < t), same & (s <= t)
        sets.append(np.stack([-1.0 * strict, -1.0 * incl, strict, incl], 1))
        nm.append(-1.0 * (same & (t < s)))
    put("gram", np.stack(sets, 1))
    put("nmask", np.stack(nm, 1))
    put("chunk", np.stack([p[:, None] // CH == np.arange(8)[None], p[:, None] // TS == np.arange(8)[None]], 1))
    r = np.ones(320)
    r[0:256:CH] = 0
    r[256::TS] = 0
    put("reset", np.broadcast_to(r, (P, 320)))
    put("eps", np.broadcast_to([EPS, LNX_EPS, 0, 0], (P, 4)))
    put("ones", np.ones((P, 128)))
    return c


VEC = {}
_at = 0
for _n, _r in (("norm1_g", 16), ("norm2_g", 16), ("mu_shift", 25), ("w0", 8), ("a0", 8), ("k_k", 8), ("k_a", 8),
               ("r_k", 8), ("ln_x_w", 8), ("ln_x_b", 8)):
    VEC[_n] = (_at, _r)
    _at += _r
NVEC = _at


class Steps:

    def __init__(self, sem, names):
        self.sem, self.names, self.cursor = sem, list(names), 0

    def done(self, name, ins):
        assert self.names[self.cursor] == name, (self.names[self.cursor], name)
        self.cursor += 1
        ins.then_inc(self.sem, 1)

    def turn(self):
        assert self.cursor == len(self.names), self.names[self.cursor:]
        self.cursor = 0

    def start(self, eng):
        eng.sem_inc(self.sem, 1)

    def at(self, name, turn=0):
        return turn * len(self.names) + (self.names.index(name) + 2)

    def before(self, turn):
        return turn * len(self.names) + 1


class Chain:

    def __init__(self, eng, sem):
        self.eng, self.sem, self.n, self.base, self.before = eng, sem, 0, 0, None

    def __call__(self, ins):
        self.n += 1
        ins.then_inc(self.sem, 1)
        self.eng.wait_ge(self.sem, self.base + self.n)

    def body(self, turn, per_turn):
        if self.before is None:
            self.before = self.n
        self.base, self.n, self.per = turn * per_turn, self.before, per_turn

    def end(self, turns):
        assert self.n - self.before == self.per, (self.n - self.before, self.per)
        self.base, self.n, self.before = 0, self.before + self.per * turns, None


class Parts:
    SLOTS, KG, COLS = 4, 4, 256

    def __init__(self, nc, scope, sems, name, granules):
        def sb(part, dt):
            return scope.enter_context(nc.sbuf_tensor(f"{name}_{part}", [P, self.SLOTS, self.KG, self.COLS], dt))

        self.nc = nc
        self.raw, self.hi, self.lo = sb("raw", F32), sb("hi", F32R), sb("lo", F32R)
        self.landed, self.rounded, self.split, self.used = sems["landed"], sems["rounded"], sems["split"], sems["used"]
        self.first = sems["count"]
        sems["count"] += granules

    def start_split(self, dve):
        if self.first == 0:
            dve.sem_inc(self.split, self.SLOTS)

    def start_use(self, pe):
        if self.first == 0:
            pe.sem_inc(self.used, self.SLOTS)

    def load(self, sp, at, j, src, n=256, before_dma=None):
        sp.wait_ge(self.split, at + (self.first + j + 1))
        if before_dma is not None:
            before_dma(sp)
        sp.dma_start(self.raw[:, j % 4, :, 0:n], src).then_inc(self.landed[j % 4], 16)

    def round(self, act, at, j, n=256):
        act.wait_ge(self.landed[j % 4], at * 4 + 16 * ((self.first + j) // 4 + 1))
        act.wait_ge(self.used, at + (self.first + j + 1))
        self.nc.scalar.copy(self.hi[:, j % 4, :, 0:n], self.raw[:, j % 4, :, 0:n]).then_inc(self.rounded, 1)

    def cut(self, dve, at, j, n=256):
        dve.wait_ge(self.rounded, at + (self.first + j + 1))
        self.nc.vector.tensor_tensor(self.lo[:, j % 4, :, 0:n], self.raw[:, j % 4, :, 0:n],
                                     self.hi[:, j % 4, :, 0:n].bitcast(F32), ALU.subtract).then_inc(self.split, 1)

    def ready(self, pe, at, j):
        pe.wait_ge(self.split, at + (self.first + j + 1 + self.SLOTS))

    def done(self, eng, at, j):
        eng.wait_ge(self.used, at + (self.first + j + 1 + self.SLOTS))


def build_layer(nc, a, o):
    top = ExitStack()
    with top:
        _layer(nc, a, o, top)


def _layer(nc, a, o, top):
    def sb(name, shape, dt=F32):
        return top.enter_context(nc.sbuf_tensor(name, shape, dt))

    def sem(name):
        return top.enter_context(nc.semaphore(name))

    def settled(eng):
        eng.sem_inc(passed, 1)

    const_in = sem("const_in")
    passed = sem("passed")

    cst = sb("cst", [P, NCONST])
    vecs = sb("vecs", [P, NVEC])
    conv = sb("conv", [P, 4, 88])
    gains = sb("gains", [P, 4, HD])
    xT = sb("xT", [P, KD, NT])
    oT = sb("oT", [P, 8, NT])
    nH = sb("n_hi", [P, KD, NT], F32R)
    mixer = ExitStack()
    work = mixer.enter_context(nc.sbuf_tensor("work", [P, WORK], F32))
    low_dram = nc.dram_tensor("n_lo_kept", (P, KD, NT), F32R, kind="Internal").ap()

    def low_part(scope, name):
        return scope.enter_context(nc.sbuf_tensor(name, [P, KD, NT], F32R))

    def ring_of(scope, name):
        return scope.enter_context(nc.sbuf_tensor(name, [P, RING], F32))[:, :]

    bank = [top.enter_context(nc.psum_tensor(f"bank{i}", [P, 512], F32)) for i in range(8)]

    def const(name, *shape):
        at, n = CONST[name]
        v = cst[:, at:at + n]
        if len(shape) == 2:
            v = v.rearrange("p (a b) -> p a b", b=shape[1])
        if len(shape) == 3:
            v = v.rearrange("p (a b c) -> p a b c", b=shape[1], c=shape[2])
        return v

    def vec(name, t):
        return vecs[:, VEC[name][0] + t:VEC[name][0] + t + 1]

    class Carve:
        def __init__(self, region, at=0):
            self.region, self.at = region, at

        def __call__(self, *shape, dt=F32):
            n = int(np.prod(shape))
            v = self.region[:, self.at:self.at + n]
            self.at += n
            assert self.at <= self.region.shape[1], (self.at, self.region.shape)
            if len(shape) == 2:
                v = v.rearrange("p (a b) -> p a b", b=shape[1])
            if len(shape) == 3:
                v = v.rearrange("p (a b c) -> p a b c", b=shape[1], c=shape[2])
            if len(shape) == 4:
                v = v.rearrange("p (a b c d) -> p a b c d", b=shape[1], c=shape[2], d=shape[3])
            return v

    ident = const("ident")
    win_stores = sem("win_stores")

    def three_passes(out, wh, wl, xh, xl, weights_first, first, last):
        for n, (wp, xp) in enumerate(((wh, xh), (wh, xl), (wl, xh)) if weights_first else ((wh, xh), (wl, xh), (wh, xl))):
            lhs, rhs = (wp, xp) if weights_first else (xp, wp)
            ins = nc.tensor.matmul(out, lhs, rhs, start=first and n == 0, stop=last and n == 2)
        return ins

    def tile_pair(pe, parts, at, j, banks, nL, cols=(0, 1)):
        parts.ready(pe, at, j)
        for h in cols:
            for kk in range(4):
                k = j % 4 * 4 + kk
                last = three_passes(banks[h][:, 0:NT], parts.hi[:, j % 4, kk, h * P:(h + 1) * P], parts.lo[:, j % 4, kk, h * P:(h + 1) * P],
                                    nH[:, k, :], nL[:, k, :], True, k == 0, k == KD - 1)
        last.then_inc(parts.used, 1)

    def norm_full(dve, k, full, gain, rstd, normed, lowered):
        if k >= 2:
            dve.wait_ge(lowered, k - 1)
        nc.vector.scalar_tensor_tensor(out=full[:, k % 2, :], in0=xT[:, k, :], scalar=vec(gain, k), in1=rstd,
                                       op0=ALU.mult, op1=ALU.mult).then_inc(normed, 1)

    def norm_low(dve, k, full, nL, halved, lowered):
        dve.wait_ge(halved, k + 1)
        nc.vector.tensor_tensor(nL[:, k, :], full[:, k % 2, :], nH[:, k, :].bitcast(F32), ALU.subtract).then_inc(lowered, 1)

    def norm_parts(dve, parts, full, nL, gain, rstd, normed, halved, lowered):
        for k in range(KD + 1):
            if k < KD:
                norm_full(dve, k, full, gain, rstd, normed, lowered)
            if k:
                norm_low(dve, k - 1, full, nL, halved, lowered)
            if k and k % 4 == 0:
                parts.cut(dve, 0, k // 4 - 1)

    def norm_high(act, parts, full, normed, halved):
        for k in range(KD):
            act.wait_ge(normed, k + 1)
            nc.scalar.copy(nH[:, k, :], full[:, k % 2, :]).then_inc(halved, 1)
            if k % 4 == 3:
                parts.round(act, 0, k // 4)

    parts_sems = dict(landed=[sem(f"parts_landed{s}") for s in range(Parts.SLOTS)], rounded=sem("parts_rounded"),
                      split=sem("parts_split"), used=sem("parts_used"), count=0)
    low_landed = [sem(f"low_landed{q}") for q in range(4)]

    def load_low(eng, nL):
        for q in range(4):
            eng.dma_start(nL[:, 4 * q:4 * q + 4, :], low_dram[:, 4 * q:4 * q + 4, :]).then_inc(low_landed[q], 16)

    products = ExitStack()
    nL = low_part(products, "n_lo_qkv")

    oflat = oT[:, :, :].rearrange("p a b -> p (a b)")
    full1 = oflat[:, 0:2 * NT].rearrange("p (a b) -> p a b", b=NT)
    rstd1 = oflat[:, 2 * NT:3 * NT]
    parts = Parts(nc, products, parts_sems, "qkv", 44)

    def load_and_norm():
        w = Carve(work)
        xin = w(3, DM)
        vrow = w(P)
        crow = w(4, P)
        sq = w(2, NT)
        rms = w(NT)
        grow = w(4 * HD)
        vec_in, x_in = sem("vec_in"), sem("x_in")
        vec_t, vec_got, x_t, x_got = sem("vec_t"), sem("vec_got"), sem("x_t"), sem("x_got")
        squared, summed, rooted, inverted = (sem(f"n1_{n}") for n in ("squared", "summed", "rooted", "inverted"))
        with nc.Block() as block:
            @block.sync
            def _(sp):
                sp.dma_start(cst[:, :], a["shape_constants"]).then_inc(const_in, 16)
                for t, (t0, n) in enumerate(TOK):
                    src = a["x_prompt"][0, t0:t0 + n, :] if t < 2 else a["x_sample"].rearrange("b t d -> (b t) d")
                    sp.dma_start(xin[0:n, t, :], src).then_inc(x_in, 16)
                sp.wait_ge(x_in, 48)
                for g in range(4):
                    parts.load(sp, 0, g, a["w_in"].rearrange("l (k p) c -> p (l k) c", p=P)[:, 4 * g:4 * g + 4, 0:256])

            @block.scalar
            def _(act):
                for name, (r0, n) in VEC.items():
                    act.dma_start(vrow[r0:r0 + n, :], a[name].rearrange("l (t p) -> (l t) p", p=P)).then_inc(vec_in, 16)
                cw = a["conv_w"].rearrange("l w (t p) -> (l w) t p", p=P)
                for j in range(3):
                    act.dma_start(crow[0:88, j, :], cw[j]).then_inc(vec_in, 16)
                act.dma_start(crow[0:88, 3, :], a["conv_b"].rearrange("l (t p) -> (l t) p", p=P)).then_inc(vec_in, 16)
                act.dma_start(grow[0:1, 0:HD], a["q_gain"]).then_inc(vec_in, 16)
                act.dma_start(grow[0:1, HD:4 * HD], a["k_gains"].rearrange("l a d -> l (a d)")).then_inc(vec_in, 16)
                act.wait_ge(vec_t, 1)
                nc.scalar.copy(vecs[:, :], bank[7][:, 0:NVEC]).then_inc(vec_got, 1)
                nc.scalar.copy(conv[:, :, :], bank[6][:, 0:352].rearrange("p (a b) -> p a b", b=88)).then_inc(vec_got, 1)
                nc.scalar.copy(gains[:, :, :], bank[5][:, 0:256].rearrange("p (a b) -> p a b", b=HD)).then_inc(vec_got, 1)
                for k in range(KD):
                    act.wait_ge(x_t, k + 1)
                    nc.scalar.copy(xT[:, k, :], bank[k % 4][:, 0:NT]).then_inc(x_got, 1)
                act.wait_ge(summed, 1)
                nc.scalar.activation(rms, bank[4][:, 0:NT], ACT.Sqrt, bias=const("eps")[:, 0:1], scale=1.0 / DM).then_inc(rooted, 1)

            @block.tensor
            def _(pe):
                pe.wait_ge(const_in, 16)
                pe.wait_ge(vec_in, 16 * (len(VEC) + 6))
                nc.tensor.transpose(bank[7][:, 0:NVEC], vrow[0:NVEC, :], ident[0:NVEC, 0:NVEC])
                for j in range(4):
                    nc.tensor.transpose(bank[6][:, 88 * j:88 * j + 88], crow[0:88, j, :], ident[0:88, 0:88])
                nc.tensor.matmul(bank[5][:, 0:256], const("ones")[0:1, :], grow[0:1, :], start=True, stop=True).then_inc(vec_t, 1)
                pe.wait_ge(x_in, 48)
                for k in range(KD):
                    if k >= 4:
                        pe.wait_ge(x_got, k - 3)
                    for t, (t0, n) in enumerate(TOK):
                        last = nc.tensor.transpose(bank[k % 4][:, t0:t0 + n], xin[0:n, t, k * P:(k + 1) * P], ident[0:n, 0:n])
                    last.then_inc(x_t, 1)
                for k in range(KD):
                    pe.wait_ge(squared, k + 1)
                    last = nc.tensor.matmul(bank[4][:, 0:NT], const("ones"), sq[:, k % 2, :], start=k == 0, stop=k == KD - 1)
                    last.then_inc(summed_each, 1)
                pe.wait_ge(summed_each, KD)
                pe.sem_inc(summed, 1)

            @block.vector
            def _(dve):
                parts.start_split(dve)
                for k in range(KD):
                    dve.wait_ge(x_got, k + 1)
                    if k >= 2:
                        dve.wait_ge(summed_each, k - 1)
                    nc.vector.tensor_tensor(sq[:, k % 2, :], xT[:, k, :], xT[:, k, :], ALU.mult).then_inc(squared, 1)
                dve.wait_ge(rooted, 1)
                nc.vector.reciprocal(rstd1, rms).then_inc(inverted, 1)

    summed_each = sem("summed_each")
    load_and_norm()

    w = Carve(work)
    pkv = w(3, ATT + 3 * KVC)
    gates = w(3, 48)

    def project_qkv():
        v = Carve(work, w.at)
        sqr = v(3, 4, HD)
        ss, rt, rs = v(3, 4), v(3, 4), v(3, 4)
        rope = v(4, 3, 4, 8)
        normed, halved, lowered = sem("n1_normed"), sem("n1_halved"), sem("n1_lowered")
        taken, cleared, low_out = sem("qkv_taken"), sem("qkv_cleared"), sem("qkv_low_out")
        norm_sq, rooted, ready, stored = sem("qkv_sq"), sem("qkv_root"), sem("qkv_ready"), sem("qkv_stored")
        wv = a["w_in"].rearrange("l (k p) c -> p (l k) c", p=P)
        NCH = 11
        NORMED = (0, 1, 2, 3, 4, 6, 8)

        def width(c):
            return 256 if c < 10 else 48

        with nc.Block() as block:
            @block.sync
            def _(sp):
                def store_rows(j):
                    name = ("cmp", "sel", "win")[j]
                    sp.wait_ge(ready, 5 + j)
                    sp.wait_ge(taken, 3 * (6 + 2 * j))
                    for t, (t0, n) in enumerate(TOK):
                        src = pkv[0:n, t, ATT + j * KVC:ATT + (j + 1) * KVC]
                        if t < 2:
                            dst = o["kv_%s_prompt" % name][0, 0, t0:t0 + n].rearrange("t c g d -> t (c g d)")
                            sp.dma_start(dst, src).then_inc(stored, 16)
                        elif name != "win":
                            dst = o["kv_%s_sample" % name].rearrange("l b t c g d -> (l b t) (c g d)")
                            sp.dma_start(dst, src).then_inc(stored, 16)
                        else:
                            for b in range(DB):
                                dst = o["kv_win_sample"][0, b, WIN - TS:WIN].rearrange("t c g d -> t (c g d)")
                                sp.dma_start(dst, src[b * TS:(b + 1) * TS, :]).then_inc(stored, 16)

                for g in range(4, 4 * NCH):
                    c, n = g // 4, width(g // 4)
                    parts.load(sp, 0, g, wv[:, g % 4 * 4:g % 4 * 4 + 4, c * 256:c * 256 + n], n)
                    if g == 12:
                        for b in range(DB):
                            sp.dma_start(o["kv_win_sample"][0, b, 0:WIN - TS].rearrange("t c g d -> t (c g d)"),
                                         a["cache_kv_win"][0, b, TS:WIN].rearrange("t c g d -> t (c g d)")).then_inc(win_stores, 16)
                for j in range(3):
                    store_rows(j)
                sp.wait_ge(stored, 16 * (3 * 2 + 2 + DB))
                sp.wait_ge(win_stores, 16 * DB)

            @block.tensor
            def _(pe):
                parts.start_use(pe)
                for g in range(4 * NCH):
                    c, n = g // 4, width(g // 4)
                    parts.ready(pe, 0, g)
                    if g < 4:
                        pe.wait_ge(lowered, 4 * g + 4)
                    if g % 4 == 0 and c >= 2:
                        pe.wait_ge(taken, 3 * (c - 1))
                    for t, (t0, m) in enumerate(TOK):
                        for kk in range(4):
                            k = g % 4 * 4 + kk
                            last = three_passes(bank[3 * (c % 2) + t][0:m, 0:n], parts.hi[:, g % 4, kk, 0:n], parts.lo[:, g % 4, kk, 0:n],
                                                nH[:, k, t0:t0 + m], nL[:, k, t0:t0 + m], False, k == 0, k == KD - 1)
                    last.then_inc(parts.used, 1)

            @block.scalar
            def _(act):
                def take(c):
                    parts.done(act, 0, 4 * c + 3)
                    for t, (t0, m) in enumerate(TOK):
                        src = bank[3 * (c % 2) + t][0:m, 0:width(c)]
                        if c < 10:
                            nc.scalar.copy(pkv[0:m, t, c * 256:(c + 1) * 256], src).then_inc(taken, 1)
                        else:
                            nc.scalar.activation(gates[0:m, t, :], src, ACT.Sigmoid).then_inc(taken, 1)

                def root(c):
                    act.wait_ge(norm_sq, NORMED.index(c) + 1)
                    nc.scalar.activation(rt, ss, ACT.Sqrt, bias=const("eps")[:, 0:1], scale=1.0 / HD).then_inc(rooted, 1)

                norm_high(act, parts, full1, normed, halved)
                act.wait_ge(cleared, 1)
                for c in range(NCH):
                    for g in range(4 * c, 4 * c + 4) if c else ():
                        parts.round(act, 0, g, width(c))
                    if c >= 1:
                        take(c - 1)
                        if c - 1 in NORMED:
                            root(c - 1)
                take(NCH - 1)

            @block.gpsimd
            def _(pool):
                nc.gpsimd.memset(pkv[64:P, 2, :], 0.0).then_inc(cleared, 1)
                pool.wait_ge(lowered, KD)
                pool.dma_start(low_dram, nL[:, :, :]).then_inc(low_out, 16)
                pool.wait_ge(low_out, 16)

            @block.vector
            def _(dve):
                own = Chain(dve, sem("qkv_dve"))
                tt = nc.vector.tensor_tensor
                norm_parts(dve, parts, full1, nL, "norm1_g", rstd1, normed, halved, lowered)

                def norm_and_rotate(c):
                    n = NORMED.index(c)
                    dve.wait_ge(taken, 3 * c + 3)
                    x = pkv[:, :, c * 256:(c + 1) * 256].rearrange("p t (h d) -> p t h d", d=HD)
                    own(tt(sqr, x, x, ALU.mult))
                    nc.vector.tensor_reduce(ss, sqr, AX.X, ALU.add).then_inc(norm_sq, 1)
                    dve.wait_ge(rooted, n + 1)
                    own(nc.vector.reciprocal(rs, rt))
                    own(tt(x, x, rs.unsqueeze(3).to_broadcast([P, 3, 4, HD]), ALU.mult))
                    gain = gains[:, max(n - 3, 0):max(n - 3, 0) + 1, :].unsqueeze(2).to_broadcast([P, 3, 4, HD])
                    own(tt(x, x, gain, ALU.mult))
                    cos, sin = (const("rope", 3, 2, 8)[:, :, j:j + 1, :].to_broadcast([P, 3, 4, 8]) for j in range(2))
                    x1, x2 = x[:, :, :, 0:8], x[:, :, :, 8:16]
                    own(tt(rope[:, 0], x1, cos, ALU.mult))
                    own(tt(rope[:, 1], x2, sin, ALU.mult))
                    own(tt(rope[:, 2], x2, cos, ALU.mult))
                    own(tt(rope[:, 3], x1, sin, ALU.mult))
                    own(tt(x1, rope[:, 0], rope[:, 1], ALU.subtract))
                    tt(x2, rope[:, 2], rope[:, 3], ALU.add).then_inc(ready, 1)
                    dve.wait_ge(ready, n + 1)

                for c in range(NCH):
                    for g in range(4 * c, 4 * c + 4) if c else ():
                        parts.cut(dve, 0, g, width(c))
                    if c - 1 in NORMED:
                        norm_and_rotate(c - 1)

    project_qkv()
    products.close()
    attention = ExitStack()
    ringflat = ring_of(attention, "ring_attention")

    pages = [ringflat[:, 2048 * i:2048 * (i + 1)].rearrange("p (j c) -> p j c", c=KVC) for i in range(6)]
    wcmp = w(2, HD)
    qrows = w(DB, 2, P)
    kT = w(2, 2, NT)
    qT = w(2, HPG, T)
    table = w(NPG * DB)
    gcol = w(DB, 3)
    gates_dram = nc.dram_tensor("gates_rows", (NS, 48), F32, kind="Internal").ap()
    att_w = w.at
    SCALE = HD ** -0.5

    def prompt_setup():
        v = Carve(ringflat)
        prod = v(2, KVC)
        qp = v(3, ATT)
        permuted = sem("ps_permuted")
        summ = vsum
        kc_in, table_in, gd_out, gd_in = sem("ps_wcmp"), sem("ps_table"), sem("ps_gd_out"), sem("ps_gd_in")
        zeroed, q_t, q_got, multiplied, sum_made, sum_got, kct, kcgot = (
            sem(f"ps_{n}") for n in ("zeroed", "q_t", "q_got", "mult", "sum_made", "sum_got", "kct", "kcgot"))
        with nc.Block() as block:
            @block.sync
            def _(sp):
                for half in range(2):
                    sp.dma_start(wcmp[64 * half:64 * half + 64], a["w_cmp"][0].rearrange("c l d -> l c d")).then_inc(kc_in, 16)
                sp.dma_start(table[0:1, :].bitcast(I32), a["page_table"].rearrange("b n -> (b n)").unsqueeze(0)).then_inc(table_in, 16)
                sp.wait_ge(table_in, 16)
                sp.dma_start(gates_dram, gates[0:NS, 2, :]).then_inc(gd_out, 16)
                sp.wait_ge(gd_out, 16)
                for h in range(NH):
                    sp.dma_start(gcol[8 * h:8 * h + 8], gates_dram[:, 3 * h:3 * h + 3].rearrange("(b q) c -> q b c", q=TS)).then_inc(gd_in, 16)
                sp.wait_ge(gd_in, 16 * NH)

            @block.tensor
            def _(pe):
                for u in range(8):
                    gp, h = u // 4, u % 4
                    if u >= 6:
                        pe.wait_ge(q_got, 3 * (u - 5))
                    for t, (t0, n) in enumerate(TOK):
                        if u == 0:
                            pe.wait_ge(permuted, 2 * t + 2)
                        src = qp[0:n, t, u * P:(u + 1) * P]
                        last = nc.tensor.transpose(bank[u % 6][:, t0:t0 + n], src, ident[0:n, 0:n])
                    last.then_inc(q_t, 1)
                for u in range(4):
                    kind, gp = u // 2, u % 2
                    pe.wait_ge(q_got, 3 * (u + 3) if u + 3 <= 8 else 24 + (u + 3 - 8))
                    for t, (t0, n) in enumerate(TOK):
                        c0 = ATT + (1 + kind) * KVC + gp * P
                        last = nc.tensor.transpose(bank[(8 + u) % 6][:, t0:t0 + n], pkv[0:n, t, c0:c0 + P], ident[0:n, 0:n])
                    last.then_inc(q_t, 1)
                pe.wait_ge(multiplied, 2)
                for t in range(2):
                    last = nc.tensor.matmul(bank[6][0:NP_BLK, :], const("blocksum")[:, 30 - 2 * t:34 - 2 * t], prod[:, t, :], start=t == 0, stop=t == 1)
                last.then_inc(sum_made, 1)
                pe.wait_ge(sum_got, 1)
                for gp in range(2):
                    last = nc.tensor.transpose(bank[7][:, 4 * gp:4 * gp + 4], summ[0:NP_BLK, gp * P:(gp + 1) * P], ident[0:NP_BLK, 0:NP_BLK])
                last.then_inc(kct, 1)

            @block.scalar
            def _(act):
                act.wait_ge(zeroed, 1)
                for u in range(8):
                    gp, h = u // 4, u % 4
                    act.wait_ge(q_t, u + 1)
                    nc.scalar.mul(qT[:, gp, h, :], bank[u % 6][:, 0:T], SCALE).then_inc(q_got, 1)
                    for e in range(2):
                        row = 32 * (2 * gp + e) + 8 * h
                        nc.scalar.mul(qrows[64 * e:64 * e + 64, :, gp, row:row + 8],
                                      bank[u % 6][64 * e:64 * e + 64, T:NT].rearrange("p (b q) -> p b q", q=TS), SCALE).then_inc(q_got, 1)
                for u in range(4):
                    act.wait_ge(q_t, 9 + u)
                    nc.scalar.copy(kT[:, u // 2, u % 2, :], bank[(8 + u) % 6][:, 0:NT]).then_inc(q_got, 1)
                act.wait_ge(sum_made, 1)
                nc.scalar.copy(summ[0:NP_BLK, :], bank[6][0:NP_BLK, :]).then_inc(sum_got, 1)
                act.wait_ge(kct, 1)
                nc.scalar.copy(kcT[:, :, 0:NP_BLK], bank[7][:, 0:8].rearrange("p (a b) -> p a b", b=4)).then_inc(kcgot, 1)

            @block.gpsimd
            def _(pool):
                for t, (t0, n) in enumerate(TOK):
                    for gp in range(2):
                        src = pkv[0:n, t, gp * 512:gp * 512 + 512].rearrange("p (e h d) -> p h e d", e=2, d=HD)
                        dst = qp[0:n, t, gp * 512:gp * 512 + 512].rearrange("p (h e d) -> p h e d", e=2, d=HD)
                        nc.gpsimd.tensor_copy(dst, src).then_inc(permuted, 1)
                nc.gpsimd.memset(qrows[:, :, :, :], 0.0).then_inc(zeroed, 1)

            @block.vector
            def _(dve):
                dve.wait_ge(kc_in, 32)
                for t in range(2):
                    shape = [P, 2, NKV, HD]
                    nc.vector.tensor_tensor(prod[:, t, :].rearrange("p (c g d) -> p c g d", c=2, d=HD),
                                            pkv[:, t, ATT:ATT + KVC].rearrange("p (c g d) -> p c g d", c=2, d=HD),
                                            wcmp.unsqueeze(2).to_broadcast(shape), ALU.mult).then_inc(multiplied, 1)

    vsum = w(KVC)
    kcT = w(2, NBLK)
    att_w = w.at
    prompt_setup()

    def prompt_attention():
        v = Carve(ringflat)
        orow = v(2, ATT)
        qs = v(2, T)
        gs = v(2, 4, 3)
        sc, ec = v(8, NP_BLK), v(8, NP_BLK)
        mc, lc, rc = v(8), v(8), v(8)
        pcT = v(8, P)
        S = v(2, 2, T)
        PT = v(2, 512)
        nm, sm, rc2, cf = v(2, 2), v(2, 2), v(2, 2), v(2, 2)
        ob = v(2, 2, HD)
        U = range(8)
        PE = Steps(sem("pa_pe"), ["cmp", "s0", "s1", "ctrans"] + [x for u in U for x in [f"t{u}"] + [f"s{u + 2}"] * (u < 6) + [f"o{u - 1}"] * (u > 0)] + ["o7"])
        DV = Steps(sem("pa_dve"), ["gates", "csub", "cp", "soft0", "soft1"] + [x for u in U for x in [f"soft{u + 2}"] * (u < 6) + [f"o{u - 1}"] * (u > 0)] + ["o7"])
        AC = Steps(sem("pa_act"), ["q0", "q1", "cexp", "cpT", "exp0_0", "exp1_0"] + [x for u in U for x in [f"exp0_{u + 1}", f"exp1_{u + 1}"] * (u < 7) + [f"pt{u}"]])
        turned, copied = sem("pa_turned"), sem("pa_copied")

        def unit(u):
            gp, e, qi = u // 4, u // 2 % 2, u % 2
            return gp, e, qi, slice(64 * e, 64 * e + 64), P * (qi + 1)

        with nc.Block() as block:
            @block.tensor
            def _(pe):
                PE.start(pe)
                mm = nc.tensor.matmul

                def scores(u, h):
                    gp, e, qi, hs, nk = unit(u)
                    if u >= 2:
                        pe.wait_ge(DV.sem, DV.at(f"soft{u - 2}", h))
                    for kind in range(2):
                        last = mm(bank[u % 2][:, kind * nk:(kind + 1) * nk], qs[hs, gp, qi * P:(qi + 1) * P], kT[hs, kind, gp, 0:nk], start=True, stop=True)
                    PE.done(f"s{u}", last)

                with pe.Fori(0, HPG) as h:
                    pe.wait_ge(AC.sem, AC.at("q1", h))
                    pe.wait_ge(DV.sem, DV.before(h))
                    settled(pe)
                    for u in U:
                        gp, e, qi, hs, nk = unit(u)
                        last = mm(bank[2 + e][:, u * 4:u * 4 + 4], qs[hs, gp, qi * P:(qi + 1) * P], kcT[hs, gp, 0:NP_BLK], start=True, stop=True)
                    PE.done("cmp", last)
                    scores(0, h)
                    scores(1, h)
                    pe.wait_ge(DV.sem, DV.at("cp", h))
                    for u in U:
                        last = nc.tensor.transpose(bank[4 + u // 4][0:NP_BLK, (u % 4) * P:(u % 4 + 1) * P], ec[:, u, :], ident)
                    PE.done("ctrans", last)

                    def product(u):
                        gp, e, qi, hs, nk = unit(u)
                        pe.wait_ge(AC.sem, AC.at(f"pt{u}", h))
                        if u >= 2:
                            pe.wait_ge(DV.sem, DV.at(f"o{u - 2}", h))
                        ps = bank[6 + u % 2]
                        c0 = HD * (2 * gp + e)
                        mm(ps[:, 128:192], pcT[0:NP_BLK, u, :], vsum[0:NP_BLK, 256 + c0:256 + c0 + HD], start=True, stop=True)
                        n = 0
                        for kind in range(2):
                            for j in range(qi + 1):
                                vv = pkv[:, j, ATT + (1 + kind) * KVC + 256 + c0:ATT + (1 + kind) * KVC + 256 + c0 + HD]
                                last = mm(ps[:, kind * HD:(kind + 1) * HD], PT[:, u % 2, n * P:(n + 1) * P], vv, start=j == 0, stop=j == qi)
                                n += 1
                        PE.done(f"o{u}", last)

                    for u in U:
                        gp, e, qi, hs, nk = unit(u)
                        pe.wait_ge(AC.sem, AC.at(f"exp1_{u}", h))
                        n = 0
                        for kind in range(2):
                            for j in range(qi + 1):
                                last = nc.tensor.transpose(bank[4 + u % 2][:, n * P:(n + 1) * P], S[:, u % 2, kind, j * P:(j + 1) * P], ident)
                                n += 1
                        PE.done(f"t{u}", last)
                        if u + 2 < 8:
                            scores(u + 2, h)
                        if u:
                            product(u - 1)
                    product(7)
                    PE.turn()
                pe.wait_ge(DV.sem, DV.before(HPG))
                for j in range(8):
                    if j >= 4:
                        pe.wait_ge(copied, j - 3)
                    for qi in range(2):
                        last = nc.tensor.transpose(bank[j % 4][:, qi * P:(qi + 1) * P], orow[:, qi, j * P:(j + 1) * P], ident)
                    last.then_inc(turned, 1)

            @block.scalar
            def _(act):
                AC.start(act)
                with act.Fori(0, HPG) as h:
                    act.wait_ge(PE.sem, PE.before(h))
                    for gp in range(2):
                        AC.done(f"q{gp}", nc.scalar.copy(qs[:, gp:gp + 1, :], qT[:, gp, ds(h, 1), :]))
                    act.wait_ge(DV.sem, DV.at("csub", h))
                    AC.done("cexp", nc.scalar.activation(ec, sc, ACT.Exp))

                    def exps(u):
                        gp, e, qi, hs, nk = unit(u)
                        act.wait_ge(DV.sem, DV.at(f"soft{u}", h))
                        for kind in range(2):
                            x = S[:, u % 2, kind, 0:nk]
                            AC.done(f"exp{kind}_{u}", nc.scalar.activation(x, x, ACT.Exp, bias=nm[:, u % 2, kind:kind + 1], accum_out=sm[:, u % 2, kind:kind + 1]))

                    act.wait_ge(PE.sem, PE.at("ctrans", h))
                    for s in range(2):
                        ins = nc.scalar.copy(pcT[0:NP_BLK, 4 * s:4 * s + 4, :], bank[4 + s][0:NP_BLK, :].rearrange("p (a b) -> p a b", b=P))
                        if s:
                            AC.done("cpT", ins)
                    exps(0)
                    for u in U:
                        gp, e, qi, hs, nk = unit(u)
                        if u + 1 < 8:
                            exps(u + 1)
                        act.wait_ge(PE.sem, PE.at(f"t{u}", h))
                        AC.done(f"pt{u}", nc.scalar.copy(PT[:, u % 2, 0:2 * nk], bank[4 + u % 2][:, 0:2 * nk]))
                    AC.turn()
                for j in range(8):
                    act.wait_ge(turned, j + 1)
                    nc.scalar.copy(oT[:, j, 0:T], bank[j % 4][:, 0:T]).then_inc(copied, 1)

            @block.vector
            def _(dve):
                DV.start(dve)
                own = Chain(dve, sem("pa_own"))
                tt = nc.vector.tensor_tensor
                vis = const("vis", 2, 2, 4)
                with dve.Fori(0, HPG) as h:
                    own.body(h, OWN)
                    dve.wait_ge(PE.sem, PE.before(h))
                    dve.wait_ge(AC.sem, AC.before(h))
                    dve.wait_ge(DV.sem, DV.before(h))
                    gv = gates[:, 0:2, :].rearrange("p t (g h c) -> p t g h c", h=HPG, c=3)[:, :, :, ds(h, 1), :].rearrange("p t g a c -> p t g (a c)")
                    DV.done("gates", nc.vector.tensor_copy(gs, gv))
                    dve.wait_ge(PE.sem, PE.at("cmp", h))
                    e4 = ec.rearrange("p (a b) c -> p a b c", b=2)
                    for e in range(2):
                        ps = bank[2 + e][:, 0:32].rearrange("p (a e b c) -> p a e b c", a=2, e=2, b=2)[:, :, e]
                        dst = sc.rearrange("p (a e b) c -> p a e b c", e=2, b=2)[:, :, e]
                        own(tt(dst, ps, vis[:, :, 1, :].unsqueeze(1).to_broadcast([P, 2, 2, 4]), ALU.add))
                    own(nc.vector.tensor_reduce(mc, sc, AX.X, ALU.max))
                    DV.done("csub", tt(sc, sc, mc.unsqueeze(2).to_broadcast([P, 8, 4]), ALU.subtract))
                    dve.wait_ge(AC.sem, AC.at("cexp", h))
                    own(tt(e4, e4, vis[:, :, 0, :].unsqueeze(1).to_broadcast([P, 4, 2, 4]), ALU.mult))
                    own(nc.vector.tensor_reduce(lc, ec, AX.X, ALU.add))
                    own(nc.vector.tensor_scalar(lc, lc, 1e-30, None, ALU.max))
                    own(nc.vector.reciprocal(rc, lc))
                    DV.done("cp", tt(ec, ec, rc.unsqueeze(2).to_broadcast([P, 8, 4]), ALU.mult))

                    def soft(u):
                        gp, e, qi, hs, nk = unit(u)
                        dve.wait_ge(PE.sem, PE.at(f"s{u}", h))
                        if u >= 2:
                            dve.wait_ge(PE.sem, PE.at(f"t{u - 2}", h))
                        m = const("causal")[:, 0:T] if qi else const("causal")[:, P:T]
                        own(tt(S[:, u % 2, :, 0:nk], bank[u % 2][:, 0:2 * nk].rearrange("p (a b) -> p a b", b=nk), m.unsqueeze(1).to_broadcast([P, 2, nk]), ALU.add))
                        DV.done(f"soft{u}", nc.vector.tensor_reduce(nm[:, u % 2, :], S[:, u % 2, :, 0:nk], AX.X, ALU.max, negate=True))

                    def factors(u):
                        gp, e, qi, hs, nk = unit(u)
                        b = u % 2
                        dve.wait_ge(AC.sem, AC.at(f"exp1_{u}", h))
                        own(nc.vector.reciprocal(rc2[:, b, :], sm[:, b, :]))
                        own(tt(cf[:, b, :], rc2[:, b, :], gs[:, qi, 2 * gp + e, 1:3], ALU.mult))

                    def out(u):
                        gp, e, qi, hs, nk = unit(u)
                        b = u % 2
                        dve.wait_ge(PE.sem, PE.at(f"o{u}", h))
                        ps = bank[6 + u % 2]
                        own(nc.vector.tensor_scalar(ob[:, b, 0, :], ps[:, 128:192], gs[:, qi, 2 * gp + e, 0:1], None, ALU.mult))
                        own(nc.vector.scalar_tensor_tensor(out=ob[:, b, 1, :], in0=ps[:, 0:HD], scalar=cf[:, b, 0:1], in1=ob[:, b, 0, :], op0=ALU.mult, op1=ALU.add))
                        dst = orow[:, qi, :].rearrange("p (g h d) -> p g h d", h=HPG, d=HD)[:, 2 * gp + e, ds(h, 1), :].rearrange("p a d -> p (a d)")
                        DV.done(f"o{u}", nc.vector.scalar_tensor_tensor(out=dst, in0=ps[:, HD:2 * HD], scalar=cf[:, b, 1:2], in1=ob[:, b, 1, :], op0=ALU.mult, op1=ALU.add))

                    soft(0)
                    soft(1)
                    for u in U:
                        factors(u)
                        if u + 2 < 8:
                            soft(u + 2)
                        if u:
                            out(u - 1)
                    out(7)
                    DV.turn()
                own.end(HPG)

    OWN = 47
    prompt_attention()

    def sample_attention():
        v = Carve(ringflat, 6 * 2048)
        Kq = v(2, 2, 512)
        Sw = v(WIN + TS)
        PTn = v(2, P)
        imp, rank, bias, sc, pc = v(NBLK), v(NBLK), v(NBLK), v(NBLK), v(NBLK)
        pcT = v(P)
        vnew = v(2, 256)
        small = v(16)
        v2 = Carve(work, att_w)
        S = v2(PAST + TS)
        PT = v2(3, 512)
        gt = v2(NBLK, NBLK)
        eq = v(NBLK, NBLK)
        v3 = Carve(work, 0)
        ob = v3(3, HD)
        qb = v3(2, P)
        more = [v3(4, KVC) for _ in range(3)]
        slot = dict(s0=pages[0], s1=pages[1], s2=pages[2], s3=pages[3], w=pages[4], c0=pages[5], c1=more[0], c2=more[1], c3=more[2])
        landed = {n: sem(f"sa_landed_{n}") for n in slot}
        summed, sums_got = sem("sa_summed"), sem("sa_sums_got")
        v_in = sem("sa_v_in")
        Q = range(4)
        PE = Steps(sem("sa_pe"), ["k0", "kc", "sc", "k1", "s0", "imp", "k2", "s1", "ocmp", "k3", "s2", "kw", "s3", "snew", "sw", "swnew",
                                  "tp0", "tp1", "pv0", "tp2", "pv1", "tp3", "pv2", "tpn", "pv3", "tpw", "tpwn", "pvn", "pvw", "fin"])
        AC = Steps(sem("sa_act"), ["q", "k0", "kc", "cexp", "k1", "pct", "k2", "k3", "kw", "exps", "expw", "pt0", "pt1", "pt2", "pt3", "ptn", "ptw", "ptwn", "out0", "out1"])
        DV = Steps(sem("sa_dve"), ["cmax", "pc", "bias", "s0", "s1", "s2", "s3", "snew", "smax", "wmax", "o"])
        PL = Steps(sem("sa_pool"), ["m0", "m1", "m2", "m3"])

        def arrived(eng, name, b):
            eng.wait_ge(landed[name], b * 64 + 64)

        LAST = DB - 1

        with nc.Block() as block:
            @block.sync
            def _(sp):
                cmp_, sel_ = (a[n][0].rearrange("n t c g d -> n t (c g d)") for n in ("cache_kv_cmp", "cache_kv_sel"))

                def load(name, cache, b):
                    for j in range(4):
                        page = sp.value_load(table[0:1, ds(b * NPG + (4 * int(name[1]) + j), 1)].bitcast(I32), min_val=0, max_val=cache.shape[0] - 1)
                        sp.dma_start(slot[name][:, j:j + 1, :], cache[ds(page, 1), :, :].rearrange("n t c -> t n c")).then_inc(landed[name], 16)

                def load_rest(b):
                    for j in range(4):
                        sp.dma_start(slot["w"][:, j:j + 1, :], a["cache_kv_win"][0, ds(b, 1), j * P:(j + 1) * P].rearrange("b t c g d -> t b (c g d)")).then_inc(landed["w"], 16)
                    sp.dma_start(vnew[0:TS, 0:1, :], o["kv_sel_sample"][0, ds(b, 1), :, 1].rearrange("b t g d -> t b (g d)")).then_inc(v_in, 16)
                    sp.dma_start(vnew[0:TS, 1:2, :], o["kv_win_sample"][0, ds(b, 1), WIN - TS:WIN, 1].rearrange("b t g d -> t b (g d)")).then_inc(v_in, 16)

                for q in Q:
                    load(f"c{q}", cmp_, 0)
                for q in Q:
                    load(f"s{q}", sel_, 0)
                load_rest(0)
                with sp.Fori(0, LAST) as b:
                    sp.wait_ge(summed, b * 1 + 1)
                    settled(sp)
                    for q in Q:
                        load(f"c{q}", cmp_, b + 1)
                    for q in Q:
                        sp.wait_ge(PE.sem, PE.at(f"pv{q}", b))
                        settled(sp)
                        load(f"s{q}", sel_, b + 1)
                    sp.wait_ge(PE.sem, PE.at("pvw", b))
                    settled(sp)
                    load_rest(b + 1)

            @block.gpsimd
            def _(pool):
                PL.start(pool)
                with pool.Fori(0, DB) as b:
                    for n in Q:
                        arrived(pool, f"c{n}", b)
                        pg = slot[f"c{n}"]
                        for j in range(4):
                            x = pg[:, j, :].rearrange("p (c g d) -> p c g d", c=2, d=HD)
                            last = nc.gpsimd.tensor_tensor(x, x, wcmp.unsqueeze(2).to_broadcast([P, 2, NKV, HD]), ALU.mult)
                        PL.done(f"m{n}", last)
                    PL.turn()

            @block.tensor
            def _(pe):
                PE.start(pe)
                mm, tr = nc.tensor.matmul, nc.tensor.transpose

                def block_sums(b):
                    for n in Q:
                        pe.wait_ge(PL.sem, PL.at(f"m{n}", b))
                        for j in range(4):
                            pg = 4 * n + j
                            last = mm(bank[0][0:NBLK, :], const("blocksum")[:, 30 - 2 * pg:62 - 2 * pg], slot[f"c{n}"][:, j, :], start=pg == 0, stop=pg == NPG - 1)
                    last.then_inc(summed, 1)

                def turn(b, last_one):
                    def ktrans(name, src):
                        arrived(pe, src, b)
                        for gp in range(2):
                            for j in range(4):
                                last = tr(bank[1 + gp][:, j * P:(j + 1) * P], slot[src][:, j, gp * P:(gp + 1) * P], ident)
                        PE.done(name, last)

                    def score(name, bk, src, n):
                        for gp in range(2):
                            last = mm(bank[bk][:, 0:n] if not isinstance(bk, tuple) else bank[bk[0]][:, bk[1]:bk[1] + n], qb[:, gp, :], src(gp), start=gp == 0, stop=gp == 1)
                        PE.done(name, last)

                    ktrans("k0", "s0")
                    pe.wait_ge(sums_got, b * 1 + 1)
                    settled(pe)
                    for gp in range(2):
                        last = tr(bank[7][:, 32 * gp:32 * gp + 32], vsum[0:NBLK, gp * P:(gp + 1) * P], ident[0:NBLK, 0:NBLK])
                    PE.done("kc", last)
                    pe.wait_ge(AC.sem, AC.at("kc", b))
                    score("sc", (7, 64), lambda gp: kcT[:, gp, :], NBLK)
                    ktrans("k1", "s1")
                    score("s0", 3, lambda gp: Kq[:, 0, gp, :], 512)
                    pe.wait_ge(DV.sem, DV.at("pc", b))
                    mm(bank[7][:, 96:128], const("group"), pc, start=True, stop=True)
                    last = tr(bank[6][0:NBLK, 0:P], pc, ident)
                    PE.done("imp", last)
                    pe.wait_ge(AC.sem, AC.at("k1", b))
                    ktrans("k2", "s2")
                    score("s1", 4, lambda gp: Kq[:, 1, gp, :], 512)
                    pe.wait_ge(AC.sem, AC.at("pct", b))
                    PE.done("ocmp", mm(bank[6][:, 256:512], pcT[0:NBLK, :], vsum[0:NBLK, 256:512], start=True, stop=True))
                    pe.wait_ge(AC.sem, AC.at("k2", b))
                    ktrans("k3", "s3")
                    pe.wait_ge(DV.sem, DV.at("s0", b))
                    score("s2", 3, lambda gp: Kq[:, 0, gp, :], 512)
                    pe.wait_ge(AC.sem, AC.at("k3", b))
                    ktrans("kw", "w")
                    pe.wait_ge(DV.sem, DV.at("s1", b))
                    score("s3", 4, lambda gp: Kq[:, 1, gp, :], 512)
                    new = ds(b * TS + T, TS)
                    score("snew", (0, 0), lambda gp: kT[:, 0, gp, new], TS)
                    pe.wait_ge(AC.sem, AC.at("kw", b))
                    score("sw", 5, lambda gp: Kq[:, 0, gp, :], 512)
                    score("swnew", (7, 128), lambda gp: kT[:, 1, gp, new], TS)
                    if not last_one:
                        pe.wait_ge(DV.sem, DV.at("snew", b))
                        block_sums(b + 1)

                    def tp(q, bk):
                        for j in range(4):
                            last = tr(bank[bk][:, j * P:(j + 1) * P], S[:, (4 * q + j) * P:(4 * q + j + 1) * P], ident)
                        PE.done(f"tp{q}", last)

                    def pv(q):
                        pe.wait_ge(AC.sem, AC.at(f"pt{q}", b))
                        for j in range(4):
                            last = mm(bank[6][:, 0:256], PT[:, q % 3, j * P:(j + 1) * P], slot[f"s{q}"][:, j, 256:512], start=q == 0 and j == 0, stop=False)
                        PE.done(f"pv{q}", last)

                    pe.wait_ge(AC.sem, AC.at("exps", b))
                    tp(0, 1)
                    tp(1, 2)
                    pv(0)
                    tp(2, 3)
                    pv(1)
                    pe.wait_ge(AC.sem, AC.at("pt0", b))
                    tp(3, 1)
                    pv(2)
                    pe.wait_ge(AC.sem, AC.at("pt1", b))
                    PE.done("tpn", tr(bank[2][0:TS, 0:P], S[:, PAST:PAST + TS], ident))
                    pv(3)
                    pe.wait_ge(AC.sem, AC.at("expw", b))
                    for j in range(4):
                        last = tr(bank[3][:, j * P:(j + 1) * P], Sw[:, j * P:(j + 1) * P], ident)
                    PE.done("tpw", last)
                    PE.done("tpwn", tr(bank[4][0:TS, 0:P], Sw[:, WIN:WIN + TS], ident))
                    pe.wait_ge(v_in, b * 32 + 32)
                    pe.wait_ge(AC.sem, AC.at("ptn", b))
                    settled(pe)
                    PE.done("pvn", mm(bank[6][:, 0:256], PTn[0:TS, 0, :], vnew[0:TS, 0, :], start=False, stop=True))
                    pe.wait_ge(AC.sem, AC.at("ptwn", b))
                    for j in range(4):
                        mm(bank[7][:, 256:512], PT[:, 1, j * P:(j + 1) * P], slot["w"][:, j, 256:512], start=j == 0, stop=False)
                    PE.done("pvw", mm(bank[7][:, 256:512], PTn[0:TS, 1, :], vnew[0:TS, 1, :], start=False, stop=True))
                    pe.wait_ge(DV.sem, DV.at("o", b))
                    if not last_one:
                        pe.wait_ge(sums_got, b * 1 + 2)
                    settled(pe)
                    PE.done("fin", tr(bank[0][0:HD, 128:256], ob[:, 0, :], ident))
                    PE.turn()

                block_sums(0)
                with pe.Fori(0, LAST) as b:
                    turn(b, False)
                turn(LAST, True)

            @block.scalar
            def _(act):
                AC.start(act)

                def take_sums(b):
                    act.wait_ge(summed, b * 1 + 1)
                    nc.scalar.copy(vsum[0:NBLK, :], bank[0][0:NBLK, :]).then_inc(sums_got, 1)

                def turn(b, last_one):
                    act.wait_ge(PE.sem, PE.before(b))
                    AC.done("q", nc.scalar.copy(qb.unsqueeze(1), qrows[:, ds(b, 1), :, :]))

                    def keys(n):
                        act.wait_ge(PE.sem, PE.at(n, b))
                        u = 1 if n in ("k1", "k3") else 0
                        nc.scalar.copy(Kq[:, u, 0, :], bank[1][:, :])
                        AC.done(n, nc.scalar.copy(Kq[:, u, 1, :], bank[2][:, :]))

                    keys("k0")
                    act.wait_ge(PE.sem, PE.at("kc", b))
                    AC.done("kc", nc.scalar.copy(kcT, bank[7][:, 0:64].rearrange("p (a b) -> p a b", b=NBLK)))
                    act.wait_ge(DV.sem, DV.at("cmax", b))
                    AC.done("cexp", nc.scalar.activation(sc, sc, ACT.Exp, bias=small[:, 0:1], accum_out=small[:, 1:2]))
                    keys("k1")
                    act.wait_ge(PE.sem, PE.at("imp", b))
                    AC.done("pct", nc.scalar.copy(pcT[0:NBLK, :], bank[6][0:NBLK, 0:P]))
                    keys("k2")
                    keys("k3")
                    keys("kw")
                    act.wait_ge(DV.sem, DV.at("smax", b))
                    AC.done("exps", nc.scalar.activation(S, S, ACT.Exp, bias=small[:, 2:3], accum_out=small[:, 3:4]))
                    act.wait_ge(DV.sem, DV.at("wmax", b))
                    AC.done("expw", nc.scalar.activation(Sw, Sw, ACT.Exp, bias=small[:, 4:5], accum_out=small[:, 5:6]))
                    if not last_one:
                        take_sums(b + 1)
                    for q, bk in ((0, 1), (1, 2), (2, 3)):
                        act.wait_ge(PE.sem, PE.at(f"tp{q}", b))
                        AC.done(f"pt{q}", nc.scalar.copy(PT[:, q, :], bank[bk][:, :]))
                    act.wait_ge(PE.sem, PE.at("tp3", b))
                    AC.done("pt3", nc.scalar.copy(PT[:, 0, :], bank[1][:, :]))
                    act.wait_ge(PE.sem, PE.at("tpn", b))
                    AC.done("ptn", nc.scalar.copy(PTn[0:TS, 0, :], bank[2][0:TS, 0:P]))
                    act.wait_ge(PE.sem, PE.at("tpw", b))
                    AC.done("ptw", nc.scalar.copy(PT[:, 1, :], bank[3][:, :]))
                    act.wait_ge(PE.sem, PE.at("tpwn", b))
                    AC.done("ptwn", nc.scalar.copy(PTn[0:TS, 1, :], bank[4][0:TS, 0:P]))
                    act.wait_ge(PE.sem, PE.at("fin", b))
                    for e in range(2):
                        src = bank[0][0:HD, 128:256].rearrange("p (j e q) -> p j e q", e=2, q=TS)[:, :, e, :]
                        AC.done(f"out{e}", nc.scalar.copy(oT[64 * e:64 * e + 64, :, ds(b * TS + T, TS)], src))
                    AC.turn()

                take_sums(0)
                with act.Fori(0, LAST) as b:
                    turn(b, False)
                turn(LAST, True)

            @block.vector
            def _(dve):
                DV.start(dve)
                own = Chain(dve, sem("sa_own"))
                tt = nc.vector.tensor_tensor

                def turn(b):
                    dve.wait_ge(PE.sem, PE.at("sc", b))
                    dve.wait_ge(AC.sem, AC.before(b))
                    dve.wait_ge(DV.sem, DV.before(b))
                    own(nc.vector.tensor_copy(sc, bank[7][:, 64:96]))
                    DV.done("cmax", nc.vector.tensor_reduce(small[:, 0:1], sc, AX.X, ALU.max, negate=True))
                    dve.wait_ge(AC.sem, AC.at("cexp", b))
                    own(nc.vector.reciprocal(small[:, 6:7], small[:, 1:2]))
                    DV.done("pc", nc.vector.tensor_scalar(pc, sc, small[:, 6:7], None, ALU.mult))
                    dve.wait_ge(PE.sem, PE.at("imp", b))
                    own(nc.vector.tensor_copy(imp, bank[7][:, 96:128]))
                    each, other = imp.unsqueeze(2).to_broadcast([P, NBLK, NBLK]), imp.unsqueeze(1).to_broadcast([P, NBLK, NBLK])
                    own(tt(gt, other, each, ALU.is_gt))
                    own(tt(eq, other, each, ALU.is_equal))
                    own(tt(eq, eq, const("earlier", NBLK, NBLK), ALU.mult))
                    own(tt(gt, gt, eq, ALU.add))
                    own(nc.vector.tensor_reduce(rank, gt, AX.X, ALU.add))
                    DV.done("bias", nc.vector.tensor_scalar(bias, rank, NSEL - 1.5, NEG, ALU.is_gt, ALU.mult))
                    dve.wait_ge(DV.sem, DV.at("bias", b))
                    for q in Q:
                        dve.wait_ge(PE.sem, PE.at(f"s{q}", b))
                        dst = S[:, q * 512:(q + 1) * 512].rearrange("p (n l) -> p n l", l=BLOCK)
                        src = bank[3 + q % 2][:, :].rearrange("p (n l) -> p n l", l=BLOCK)
                        DV.done(f"s{q}", tt(dst, src, bias[:, 8 * q:8 * q + 8].unsqueeze(2).to_broadcast([P, 8, BLOCK]), ALU.add))
                    dve.wait_ge(PE.sem, PE.at("snew", b))
                    DV.done("snew", tt(S[:, PAST:], bank[0][:, 0:TS], const("newmask"), ALU.add))
                    dve.wait_ge(DV.sem, DV.at("snew", b))
                    DV.done("smax", nc.vector.tensor_reduce(small[:, 2:3], S, AX.X, ALU.max, negate=True))
                    dve.wait_ge(PE.sem, PE.at("swnew", b))
                    own(nc.vector.tensor_copy(Sw[:, TS:WIN], bank[5][:, TS:WIN]))
                    own(tt(Sw[:, 0:TS], bank[5][:, 0:TS], const("winmask"), ALU.add))
                    own(tt(Sw[:, WIN:], bank[7][:, 128:136], const("newmask"), ALU.add))
                    DV.done("wmax", nc.vector.tensor_reduce(small[:, 4:5], Sw, AX.X, ALU.max, negate=True))
                    dve.wait_ge(AC.sem, AC.at("expw", b))
                    own(nc.vector.reciprocal(small[:, 7:8], small[:, 3:4]))
                    own(nc.vector.reciprocal(small[:, 8:9], small[:, 5:6]))
                    gb = gcol[:, ds(b, 1), :].rearrange("p a c -> p (a c)")
                    own(nc.vector.tensor_copy(small[:, 12:15], gb))
                    own(tt(small[:, 9:11], small[:, 7:9], small[:, 13:15], ALU.mult))
                    dve.wait_ge(PE.sem, PE.at("pvw", b))
                    for g in range(NKV):
                        r, c = slice(32 * g, 32 * g + 32), slice(HD * g, HD * g + HD)
                        own(nc.vector.tensor_scalar(ob[r, 2, :], bank[6][r, 256 + HD * g:256 + HD * g + HD], small[r, 12:13], None, ALU.mult))
                    for g in range(NKV):
                        r, c = slice(32 * g, 32 * g + 32), slice(HD * g, HD * g + HD)
                        own(nc.vector.scalar_tensor_tensor(out=ob[r, 1, :], in0=bank[6][r, c], scalar=small[r, 9:10], in1=ob[r, 2, :], op0=ALU.mult, op1=ALU.add))
                    for g in range(NKV):
                        r, c = slice(32 * g, 32 * g + 32), slice(256 + HD * g, 256 + HD * g + HD)
                        ins = nc.vector.scalar_tensor_tensor(out=ob[r, 0, :], in0=bank[7][r, c], scalar=small[r, 10:11], in1=ob[r, 1, :], op0=ALU.mult, op1=ALU.add)
                        if g < NKV - 1:
                            own(ins)
                        else:
                            DV.done("o", ins)
                    DV.turn()

                with dve.Fori(0, LAST) as b:
                    own.body(b, OWN2)
                    turn(b)
                own.end(LAST)
                turn(LAST)

    OWN2 = 26
    sample_attention()

    attention.close()
    products = ExitStack()
    nL = low_part(products, "n_lo_shift")

    w = Carve(work)
    z = w(25, NT)
    yT = z[:, 0:8, :]
    decay_in = w(8, NT)
    rate = w(8, NT)
    rwkv_work = w.at

    def project_shift():
        v = Carve(work, 8000)
        srow = v(SHIFT)
        v.at = rwkv_work
        prevT = v(25, DB)
        lastT = v(25, 1 + DB)
        ub = v(4, 1 + T + DB * (TS + 1))
        parts = Parts(nc, products, parts_sems, "shift", 52)
        taken = sem("sh_taken")
        prev_in, prev_t, prev_got = sem("sh_prev_in"), sem("sh_prev_t"), sem("sh_prev_got")
        mixed, kept, zeroed = sem("sh_mixed"), sem("sh_kept"), sem("sh_zeroed")
        last_t, last_got, last_out = sem("sh_last_t"), sem("sh_last_got"), sem("sh_last_out")
        wv = a["w_in"].rearrange("l (k p) c -> p (l k) c", p=P)[:, :, C_SHIFT:C_MERGE]
        with nc.Block() as block:
            @block.sync
            def _(sp):
                sp.dma_start(srow[0:DB, :], a["state_shift"][0]).then_inc(prev_in, 16)
                with sp.Fori(0, 3) as i:
                    for g in range(16):
                        k = g % 4 * 4
                        parts.load(sp, i * 16, g, wv[:, k:k + 4, ds(i * 1024 + g // 4 * 256, 256)])
                for g in range(4):
                    parts.load(sp, 48, g, wv[:, g * 4:g * 4 + 4, 3072:3200], P)
                sp.wait_ge(last_got, 7)
                sp.dma_start(o["shift_prompt"][0], srow[0:1, :]).then_inc(last_out, 16)
                sp.dma_start(o["shift_sample"][0], srow[1:1 + DB, :]).then_inc(last_out, 16)
                sp.wait_ge(last_out, 32)

            @block.tensor
            def _(pe):
                parts.start_use(pe)
                pe.wait_ge(prev_in, 16)
                for t in range(25):
                    last = nc.tensor.transpose(bank[7][:, 8 * t:8 * t + 8], srow[0:DB, t * P:(t + 1) * P], ident[0:DB, 0:DB])
                last.then_inc(prev_t, 1)


                def turn(i, first):
                    for c in range(4):
                        pe.wait_ge(taken, i * 8 + (2 * c + 2))
                        for g in range(4 * c, 4 * c + 4):
                            if first and c == 0:
                                pe.wait_ge(low_landed[g], 16)
                            tile_pair(pe, parts, i * 16, g, bank[2 * (c % 2):2 * (c % 2) + 2], nL)

                turn(0, True)
                with pe.Fori(1, 3) as i:
                    turn(i, False)
                pe.wait_ge(taken, 24 + 1)
                for g in range(4):
                    tile_pair(pe, parts, 48, g, bank[0:1], nL, (0,))
                pe.wait_ge(kept, 25 + 4)
                for q in range(7):
                    n = 4 if q < 6 else 1
                    if q >= 2:
                        pe.wait_ge(last_got, q - 1)
                    for j in range(n):
                        last = nc.tensor.transpose(bank[5 + q % 2][0:9, j * P:(j + 1) * P], lastT[:, 4 * q + j, :], ident)
                    last.then_inc(last_t, 1)

            @block.scalar
            def _(act):
                act.sem_inc(taken, 4)
                act.wait_ge(prev_t, 1)
                nc.scalar.copy(prevT, bank[7][:, 0:200].rearrange("p (a b) -> p a b", b=DB)).then_inc(prev_got, 1)
                act.wait_ge(prev_got, 1)
                act.wait_ge(zeroed, 1)

                def take(b, u, prev):
                    s = ub[:, u, 1 + T:].rearrange("p (b t) -> p b t", t=TS + 1)
                    nc.scalar.copy(s[:, :, 0:1], prev)
                    nc.scalar.copy(s[:, :, 1:], bank[b][:, T:NT].rearrange("p (b t) -> p b t", t=TS))
                    nc.scalar.copy(ub[:, u, 1:1 + T], bank[b][:, 0:T]).then_inc(taken, 1)

                def take_chunk(i, c):
                    parts.done(act, i * 16, 4 * c + 3)
                    for g in (2 * c, 2 * c + 1):
                        act.wait_ge(mixed, i * 8 + (g + 1))
                        act.wait_ge(kept, i * 8 + (g + 1))
                        take(g % 4, g % 4, prevT[:, ds(i * 8 + g, 1), :].rearrange("p a b -> p b a"))

                def turn(i, first):
                    for c in range(4):
                        for g in range(4 * c, 4 * c + 4):
                            parts.round(act, i * 16, g)
                        if c:
                            take_chunk(i, c - 1)
                        elif not first:
                            take_chunk(i - 1, 3)

                turn(0, True)
                with act.Fori(1, 3) as i:
                    turn(i, False)
                for g in range(4):
                    parts.round(act, 48, g, P)
                take_chunk(2, 3)
                parts.done(act, 48, 3)
                act.wait_ge(mixed, 24 + 1)
                act.wait_ge(kept, 24 + 1)
                take(0, 0, prevT[:, 24:25, :].rearrange("p a b -> p b a"))
                for q in range(7):
                    n = 4 if q < 6 else 1
                    act.wait_ge(last_t, q + 1)
                    nc.scalar.copy(srow[0:9, 4 * q * P:(4 * q + n) * P], bank[5 + q % 2][0:9, 0:n * P]).then_inc(last_got, 1)

            @block.gpsimd
            def _(pool):
                load_low(pool, nL)
                pool.sem_inc(kept, 4)
                nc.gpsimd.memset(ub[:, :, 0:1], 0.0).then_inc(zeroed, 1)

                def keep(n, u, dst):
                    pool.wait_ge(taken, n + (1 + 4))
                    s = ub[:, u, 1 + T:].rearrange("p (b t) -> p b t", t=TS + 1)
                    nc.gpsimd.tensor_copy(dst[:, :, 0:1], ub[:, u:u + 1, T:T + 1])
                    nc.gpsimd.tensor_copy(dst[:, :, 1:].rearrange("p a b -> p b a"), s[:, :, TS:TS + 1]).then_inc(kept, 1)

                with pool.Fori(0, 3) as i:
                    for g in range(8):
                        keep(i * 8 + g, g % 4, lastT[:, ds(i * 8 + g, 1), :])
                keep(24, 0, lastT[:, 24:25, :])

            @block.vector
            def _(dve):
                dve.sem_inc(mixed, 4)
                parts.start_split(dve)
                own = Chain(dve, sem("sh_dve"))
                dve.wait_ge(zeroed, 1)

                def mix(n, u, zt, mu):
                    dve.wait_ge(taken, n + (1 + 4))
                    s = ub[:, u, 1 + T:].rearrange("p (b t) -> p b t", t=TS + 1)
                    zp = zt[:, :, 0:T].rearrange("p a t -> p (a t)")
                    zs = zt[:, :, T:NT].rearrange("p a (b t) -> p (a b) t", t=TS)
                    nc.vector.tensor_tensor(zp, ub[:, u, 0:T], ub[:, u, 1:1 + T], ALU.subtract)
                    own(nc.vector.tensor_tensor(zs, s[:, :, 0:TS], s[:, :, 1:], ALU.subtract))
                    nc.vector.scalar_tensor_tensor(out=zs, in0=zs, scalar=mu, in1=s[:, :, 1:], op0=ALU.mult, op1=ALU.add)
                    nc.vector.scalar_tensor_tensor(out=zp, in0=zp, scalar=mu, in1=ub[:, u, 1:1 + T], op0=ALU.mult, op1=ALU.add).then_inc(mixed, 1)

                at = VEC["mu_shift"][0]

                def mix_chunk(i, c):
                    for g in (2 * c, 2 * c + 1):
                        own.body(i * 8 + g, 1)
                        mix(i * 8 + g, g % 4, z[:, ds(i * 8 + g, 1), :], vecs[:, ds(i * 8 + (g + at), 1)])

                def turn(i, first):
                    for c in range(4):
                        for g in range(4 * c, 4 * c + 4):
                            parts.cut(dve, i * 16, g)
                        if c:
                            mix_chunk(i, c - 1)
                        elif not first:
                            mix_chunk(i - 1, 3)

                turn(0, True)
                with dve.Fori(1, 3) as i:
                    turn(i, False)
                for g in range(4):
                    parts.cut(dve, 48, g, P)
                mix_chunk(2, 3)
                own.body(24, 1)
                mix(24, 0, z[:, 24:25, :], vec("mu_shift", 24))

    project_shift()
    products.close()
    recurrent = ExitStack()
    ringflat = ring_of(recurrent, "ring_recurrence")

    def low_rank():
        v = Carve(ringflat)
        lora = v(RW)
        th = v(NT)
        lora_in, tanhed, made, taken = sem("lr_in"), sem("lr_tanh"), sem("lr_made"), sem("lr_taken")
        with nc.Block() as block:
            @block.sync
            def _(sp):
                sp.dma_start(lora[0:64, :], a["w_lora_w"][0]).then_inc(lora_in, 16)
                sp.dma_start(lora[64:128, :], a["w_lora_a"][0]).then_inc(lora_in, 16)

            @block.tensor
            def _(pe):
                pe.wait_ge(lora_in, 32)
                for g in range(16):
                    t, e = g // 2, g % 2
                    if g == 0:
                        pe.wait_ge(tanhed, 1)
                    if g >= 4:
                        pe.wait_ge(taken, g - 3)
                    rhs = th[0:64, :] if e == 0 else z[64:128, 24, :]
                    nc.tensor.matmul(bank[g % 4][:, 0:NT], lora[64 * e:64 * e + 64, t * P:(t + 1) * P], rhs, start=True, stop=True).then_inc(made, 1)

            @block.scalar
            def _(act):
                nc.scalar.activation(th[0:64, :], z[0:64, 24, :], ACT.Tanh).then_inc(tanhed, 1)
                for g in range(16):
                    t, e = g // 2, g % 2
                    act.wait_ge(made, g + 1)
                    nc.scalar.activation((rate if e else decay_in)[:, t, :], bank[g % 4][:, 0:NT], ACT.Sigmoid,
                                         bias=vec("a0" if e else "w0", t)).then_inc(taken, 1)

    low_rank()

    def recurrence():
        PAD = 3 * P
        v = Carve(ringflat)
        lw, lg, kk0, kk, k2, bb, bon, tmp = (v(NT) for _ in range(8))
        before, to_end = v(NT), v(NT)
        dec, inv, rk = v(NT), v(NT), v(NT)
        AR = v(2, PAD)
        bT, kT, bE, kE, vP = (v(PAD) for _ in range(5))
        tm = v(4, 3, P)
        GM = v(3, 4, P)
        Np, NTp = v(2, 3, P), v(2, 3, P)
        N0 = v(3, P)
        Z = v(3, P)
        Bm, Vm, Wm = v(2, 512), v(2, 512), v(2, 512)
        v2 = Carve(work, rwkv_work)
        PTc = v2(24, HD)
        Qc = v2(24, HD)
        S = v2(17, HD)
        S0 = v2(DB, HD)
        S1 = v2(DB, HD)
        v3 = v
        Rh = v3(PAD)
        y = v3(NT)
        srows = v3(DB, P)
        bonv = v3(NT)
        dend = v3(24)
        orows = ringflat[:, 2 * NT:2 * NT + (1 + DB) * P].rearrange("p (a b) -> p a b", b=P)
        yc, yq = lw, lg
        state_in, state_out = sem("rw_state_in"), sem("rw_state_out")
        LV = range(4)
        PE = Steps(sem("rw_pe"), [
            f"{n}{e}" for e in (0, 1) for n in ["gram0_", "gram1_", "gram2_", "ngram", "mv"] + [x for l in LV for x in (
                [f"apply{l}_"] + [f"sqT{l}_"] * (l < 3) + [f"sq{l}_"] * (l < 2))]
            + ["rhat", "p0_", "q0_", "p1_", "q1_", "p2_", "q2_", "y"]] + [
            x for c in range(CH) for x in [f"scan{c}"] + {7: ["sample"], 13: ["turned_s"], 15: ["read"]}.get(c, [])] + ["turned_p"])
        PE2 = Steps(sem("rw_pe_next"), ["norms", "bonus", "rows0", "rows1", "rows2", "rows3", "states"])
        DV2 = Steps(sem("rw_dve_next"), ["logs", "kk0sq", "rkprod", "clamped", "ready"])
        AC2 = Steps(sem("rw_act_next"), ["dec", "inv", "before", "to_end", "root", "bonus", "tm0", "tm1", "tm2", "tm3", "states"])
        PL2 = Steps(sem("rw_pool_next"), ["v"])
        PE3 = Steps(sem("rw_pe_norm"), ["mean", "var"])
        DV3 = Steps(sem("rw_dve_norm"), ["y", "centred", "squared", "out"])
        AC3 = Steps(sem("rw_act_norm"), ["lnroot"])
        DV = Steps(sem("rw_dve"), [
            f"{n}{e}" for e in (0, 1) for n in ["gram", "ngram", "mv"] + ["saved"] * (e == 0) + ["z0_", "z1_", "z2_", "z3_", "rhat",
                                                "wm0_", "wm1_", "q0_", "wm2_", "q1_", "q2_"]]
            + [x for c in range(CH) for x in ["state_s"] * (c == 11) + [f"state{c}"]])
        AC = Steps(sem("rw_act"), [
            f"{n}{e}" for e in (0, 1) for n in ["alpha", "sqT0_", "sq0_", "sqT1_", "sq1_", "sqT2_", "p0_", "p1_", "p2_"] + ["y"] * (e == 0)]
            + ["y1", "out_s0", "out_s1", "out_p"])
        PL = Steps(sem("rw_pool"), [f"{n}{e}" for e in (0, 1) for n in ["m0_", "m1_", "m2_"]])
        zeroed = sem("rw_zeroed")
        NPAIR = NH // 2
        gram = const("gram", 2, 4, P)
        nmask = const("nmask", 2, P)
        chunk = const("chunk", 2, 8)
        halves = const("halves")

        def ends(x):
            return x[:, 0:T].rearrange("p (c t) -> p c t", t=CH)[:, :, CH - 1:CH], x[:, T:NT].rearrange("p (c t) -> p c t", t=TS)[:, :, TS - 1:TS]

        with nc.Block() as block:
            @block.sync
            def _(sp):
                sp.sem_inc(state_out, 1)

                def load(p):
                    sp.wait_ge(PE2.sem, PE2.before(p))
                    for e in range(2):
                        src = a["state_wkv"][0, :, ds(p * 2 + e, 1), :, :].rearrange("b h v k -> v (b h) k")
                        sp.dma_start(srows[0:64, :, e * HD:(e + 1) * HD], src).then_inc(state_in, 16)

                def store(p):
                    sp.wait_ge(AC.sem, AC.at("out_p", p))
                    for e in range(2):
                        dst = o["wkv_prompt"][0, 0, ds(p * 2 + e, 1), :, :].rearrange("h v k -> v h k")
                        sp.dma_start(dst, orows[0:64, 0:1, e * HD:(e + 1) * HD]).then_inc(state_out, 16)
                        dst = o["wkv_sample"][0, :, ds(p * 2 + e, 1), :, :].rearrange("b h v k -> v (b h) k")
                        sp.dma_start(dst, orows[0:64, 1:1 + DB, e * HD:(e + 1) * HD]).then_inc(state_out, 16)

                load(0)
                with sp.Fori(0, NPAIR - 1) as p:
                    load(p + 1)
                    store(p)
                store(NPAIR - 1)
                sp.wait_ge(state_out, 64 * NPAIR + 1)

            @block.tensor
            def _(pe):
                PE.start(pe)
                PE2.start(pe)
                PE3.start(pe)
                mm = nc.tensor.matmul

                def norms(p):
                    pe.wait_ge(DV2.sem, DV2.at("kk0sq", p))
                    PE2.done("norms", mm(bank[6][:, 0:NT], halves, tmp, start=True, stop=True))

                def bonus(p):
                    pe.wait_ge(DV2.sem, DV2.at("rkprod", p))
                    PE2.done("bonus", mm(bank[4][:, 0:NT], halves, rk, start=True, stop=True))

                def rows(p, n):
                    q, j = n // 3, n % 3
                    if n == 0:
                        pe.wait_ge(DV2.sem, DV2.at("ready", p))
                        pe.wait_ge(PL2.sem, PL2.at("v", p))
                    src = (AR[:, 0, :], bE, kE, vP)[q]
                    last = nc.tensor.transpose(bank[(1, 2, 5, 6)[q]][:, j * P:(j + 1) * P], src[:, j * P:(j + 1) * P], ident)
                    if j == 2:
                        PE2.done(f"rows{q}", last)

                def states(p):
                    pe.wait_ge(state_in, p * 32 + 32)
                    settled(pe)
                    for b in range(DB):
                        last = nc.tensor.transpose(bank[0][:, b * HD:(b + 1) * HD], srows[0:64, b, :], ident[0:64, 0:64])
                    PE2.done("states", last)
                    PE2.turn()

                def spread(p):
                    pe.wait_ge(DV3.sem, DV3.at("squared", p))
                    PE3.done("var", mm(bank[6][:, 0:NT], halves, yq, start=True, stop=True))
                    PE3.turn()

                def turn(p, first, final):
                    for e in range(2):
                        h = slice(64 * e, 64 * e + 64)
                        if e == 0:
                            pe.wait_ge(AC2.sem, AC2.at("states", p))
                            pe.wait_ge(AC.sem, AC.before(p))
                            settled(pe)
                        else:
                            pe.wait_ge(AC.sem, AC.at("p2_0", p))
                            pe.wait_ge(DV.sem, DV.at("q2_0", p))
                        for j in range(3):
                            js = slice(j * P, (j + 1) * P)
                            mm(bank[j][:, 0:256].rearrange("p (a b) -> p a b", b=P), bT[h, js], AR[h, :, js], start=True, stop=True)
                            PE.done(f"gram{j}_{e}", mm(bank[j][:, 256:512].rearrange("p (a b) -> p a b", b=P), kT[h, js], AR[h, :, js], start=True, stop=True))
                        if e == 0 and not first:
                            spread(p - 1)
                        for j in range(3):
                            js = slice(j * P, (j + 1) * P)
                            last = mm(bank[7][:, js], AR[h, 0, js], bT[h, js], start=True, stop=True)
                        PE.done(f"ngram{e}", last)
                        if e == 0:
                            pe.wait_ge(AC2.sem, AC2.at("tm3", p))
                        pe.wait_ge(DV.sem, DV.at(f"gram{e}", p))
                        for j in range(3):
                            last = mm(bank[3][:, j * HD:(j + 1) * HD], GM[:, j, 2, :], tm[:, 3, j, h], start=True, stop=True)
                        PE.done(f"mv{e}", last)
                        for l in LV:
                            nt = GM[:, :, 0, :] if l == 0 else NTp[:, l % 2]
                            n = N0 if l == 0 else Np[:, l % 2]
                            if l == 0:
                                pe.wait_ge(DV.sem, DV.at(f"mv{e}", p))
                                pe.wait_ge(AC.sem, AC.at(f"alpha{e}", p))
                            else:
                                pe.wait_ge(DV.sem, DV.at(f"z{l - 1}_{e}", p))
                                pe.wait_ge(AC.sem, AC.at(f"sqT{l - 1}_{e}", p))
                            for j in range(3):
                                last = mm(bank[4][:, j * P:(j + 1) * P], nt[:, j], Z[:, j], start=True, stop=True)
                            PE.done(f"apply{l}_{e}", last)
                            if l == 0:
                                pe.wait_ge(DV.sem, DV.at(f"ngram{e}", p))
                                if e == 0 and not first:
                                    pe.wait_ge(AC3.sem, AC3.at("lnroot", p - 1))
                                if e == 1:
                                    pe.wait_ge(AC.sem, AC.at("y0", p))
                                    if not final:
                                        pe.wait_ge(DV2.sem, DV2.at("clamped", p + 1))
                            elif l < 3:
                                pe.wait_ge(AC.sem, AC.at(f"sq{l - 1}_{e}", p))
                            if l < 3:
                                for j in range(3):
                                    last = mm(bank[5][:, j * P:(j + 1) * P], n[:, j], nt[:, j], start=True, stop=True)
                                PE.done(f"sqT{l}_{e}", last)
                            if l < 2:
                                for j in range(3):
                                    last = mm(bank[6][:, j * P:(j + 1) * P], nt[:, j], n[:, j], start=True, stop=True)
                                PE.done(f"sq{l}_{e}", last)
                        pe.wait_ge(DV.sem, DV.at(f"z3_{e}", p))
                        for j in range(3):
                            js = slice(j * P, (j + 1) * P)
                            last = mm(bank[7][h, js], Z[:, j, 0:HD], GM[:, j, 1, :], start=True, stop=True)
                        PE.done(f"rhat{e}", last)
                        if e == 1 and not final:
                            bonus(p + 1)
                        for j in range(3):
                            bp, bq = bank[2 * (j % 2)], bank[1 + 2 * (j % 2)]
                            pe.wait_ge(PL.sem, PL.at(f"m{j}_{e}", p))
                            if j == 2:
                                pe.wait_ge(AC.sem, AC.at(f"p0_{e}", p))
                            PE.done(f"p{j}_{e}", mm(bp[h, :], Z[:, j, 0:HD], Bm[:, j % 2, :], start=True, stop=True))
                            pe.wait_ge(DV.sem, DV.at(f"wm{j}_{e}", p))
                            if j == 2:
                                pe.wait_ge(DV.sem, DV.at(f"q0_{e}", p))
                            mm(bq[h, :], tm[:, 2, j, h], Vm[:, j % 2, :], start=True, stop=False)
                            PE.done(f"q{j}_{e}", mm(bq[h, :], tm[:, 1, j, h], Wm[:, j % 2, :], start=False, stop=True))
                        pe.wait_ge(AC.sem, AC.at(f"sqT2_{e}", p))
                        ybank = bank[5] if e == 0 else bank[6]
                        for j in range(3):
                            js = slice(j * P, (j + 1) * P)
                            mm(ybank[h, js], tm[:, 3, j, h], GM[:, j, 3, :], start=True, stop=False)
                            last = mm(ybank[h, js], Z[:, j, HD:P], GM[:, j, 1, :], start=False, stop=True)
                        PE.done(f"y{e}", last)
                        if e == 0 and not final:
                            norms(p + 1)
                    pe.wait_ge(AC.sem, AC.at("p2_1", p))
                    pe.wait_ge(DV.sem, DV.at("q2_1", p))
                    pe.wait_ge(DV.sem, DV.at("rhat1", p))
                    for c in range(CH):
                        if c:
                            pe.wait_ge(DV.sem, DV.at(f"state{c - 1}", p))
                        settled(pe)
                        sp_ = bank[3] if c % 2 else bank[7]
                        for e in range(2):
                            h = slice(64 * e, 64 * e + 64)
                            last = mm(sp_[h, 0:HD], PTc[h, c, :], S[h, c, :], start=True, stop=True)
                        PE.done(f"scan{c}", last)
                        if c == 0 and not final:
                            pe.wait_ge(AC2.sem, AC2.at("bonus", p + 1))
                            settled(pe)
                        for e in range(2):
                            h = slice(64 * e, 64 * e + 64)
                            last = mm(bank[4][h, c * CH:(c + 1) * CH], S[h, c, :], Rh[h, c * CH:(c + 1) * CH], start=True, stop=True)
                        if c == CH - 1:
                            PE.done("read", last)
                        if c < DB:
                            for e in range(2):
                                h = slice(64 * e, 64 * e + 64)
                                last = mm(bank[0][h, c * HD:(c + 1) * HD], PTc[h, 16 + c, :], S0[h, c, :], start=True, stop=True)
                            if c == DB - 1:
                                PE.done("sample", last)
                            for e in range(2):
                                h = slice(64 * e, 64 * e + 64)
                                cs = slice(T + c * TS, T + (c + 1) * TS)
                                mm(bank[4][h, cs], S0[h, c, :], Rh[h, cs], start=True, stop=True)
                        if 6 <= c < 12 and not final:
                            if c == 10:
                                pe.wait_ge(AC.sem, AC.at("y1", p))
                            for n in (2 * c - 12, 2 * c - 11):
                                rows(p + 1, n)
                        if c == 12:
                            pe.wait_ge(DV.sem, DV.at("state_s", p))
                            if not final:
                                pe.wait_ge(AC2.sem, AC2.at("tm1", p + 1))
                            settled(pe)
                        if c in (12, 13):
                            for b in range(4 * (c - 12), 4 * (c - 12) + 4):
                                last = nc.tensor.transpose(bank[14 - c][0:64, (b % 4) * P:(b % 4 + 1) * P], S1[:, b, :], ident)
                            if c == 13:
                                PE.done("turned_s", last)
                        if c == 14 and not final:
                            states(p + 1)
                    pe.wait_ge(DV.sem, DV.at(f"state{CH - 1}", p))
                    if not final:
                        pe.wait_ge(AC2.sem, AC2.at("tm3", p + 1))
                    settled(pe)
                    PE.done("turned_p", nc.tensor.transpose(bank[5][0:64, 0:P], S[:, CH, :], ident))
                    pe.wait_ge(DV3.sem, DV3.at("y", p))
                    PE3.done("mean", mm(bank[6][:, 0:NT], halves, y, start=True, stop=True))
                    PE.turn()

                norms(0)
                bonus(0)
                for n in range(12):
                    rows(0, n)
                states(0)
                turn(0, True, False)
                with pe.Fori(1, NPAIR - 1) as p:
                    turn(p, False, False)
                turn(NPAIR - 1, False, True)
                spread(NPAIR - 1)

            @block.scalar
            def _(act):
                AC.start(act)
                AC2.start(act)

                def decays(p):
                    act.wait_ge(DV2.sem, DV2.at("logs", p))
                    AC2.done("dec", nc.scalar.activation(dec, lg, ACT.Exp))
                    AC2.done("inv", nc.scalar.activation(inv, lg, ACT.Exp, scale=-1.0))
                    AC2.done("before", nc.scalar.activation(before, before, ACT.Exp))
                    AC2.done("to_end", nc.scalar.activation(to_end, to_end, ACT.Exp))

                def root(p):
                    act.wait_ge(DV2.sem, DV2.at("clamped", p))
                    AC2.done("root", nc.scalar.activation(bb, bb, ACT.Sqrt))

                def bonus(p):
                    act.wait_ge(PE2.sem, PE2.at("bonus", p))
                    AC2.done("bonus", nc.scalar.copy(bon, bank[4][:, 0:NT]))

                def rows(p):
                    for q in range(4):
                        act.wait_ge(PE2.sem, PE2.at(f"rows{q}", p))
                        src = bank[(1, 2, 5, 6)[q]][:, 0:3 * P].rearrange("p (a b) -> p a b", b=P)
                        AC2.done(f"tm{q}", nc.scalar.mul(tm[:, q], src, -1.0 if q == 1 else 1.0))

                def states(p):
                    act.wait_ge(PE2.sem, PE2.at("states", p))
                    AC2.done("states", nc.scalar.copy(S0, bank[0][:, :].rearrange("p (b v) -> p b v", v=HD)))
                    AC2.turn()

                def norm_root(p):
                    act.wait_ge(PE3.sem, PE3.at("var", p))
                    AC3.done("lnroot", nc.scalar.activation(yq, bank[6][:, 0:NT], ACT.Sqrt, bias=const("eps")[:, 1:2], scale=1.0 / HD))
                    AC3.turn()

                def turn(p, first, final):
                    for e in range(2):
                        h = slice(64 * e, 64 * e + 64)
                        if e == 0:
                            act.wait_ge(AC2.sem, AC2.at("tm3", p))
                        else:
                            act.wait_ge(PE.sem, PE.at("y0", p))
                        AC.done(f"alpha{e}", nc.scalar.copy(Z[:, :, 0:HD], tm[:, 0, :, h]))
                        if e == 0 and not first:
                            norm_root(p - 1)
                        if e == 1 and not final:
                            root(p + 1)
                        for l in range(3):
                            act.wait_ge(PE.sem, PE.at(f"sqT{l}_{e}", p))
                            AC.done(f"sqT{l}_{e}", nc.scalar.copy(NTp[:, (l + 1) % 2], bank[5][:, 0:3 * P].rearrange("p (a b) -> p a b", b=P)))
                            if l < 2:
                                act.wait_ge(PE.sem, PE.at(f"sq{l}_{e}", p))
                                AC.done(f"sq{l}_{e}", nc.scalar.copy(Np[:, (l + 1) % 2], bank[6][:, 0:3 * P].rearrange("p (a b) -> p a b", b=P)))
                        for j in range(3):
                            if e == 0 and j == 1 and not final:
                                act.wait_ge(DV.sem, DV.at("saved0", p))
                                decays(p + 1)
                            if e == 1 and j == 1 and not final:
                                bonus(p + 1)
                            act.wait_ge(PE.sem, PE.at(f"p{j}_{e}", p))
                            AC.done(f"p{j}_{e}", nc.scalar.copy(PTc[h, 8 * j:8 * j + 8, :], bank[2 * (j % 2)][h, :].rearrange("p (c k) -> p c k", k=HD)))
                        if e == 0:
                            act.wait_ge(PE.sem, PE.at("y0", p))
                            AC.done("y0", nc.scalar.copy(y[0:64, :], bank[5][0:64, 0:NT]))
                    act.wait_ge(PE.sem, PE.at("y1", p))
                    AC.done("y1", nc.scalar.copy(y[64:128, :], bank[6][64:128, 0:NT]))
                    if not final:
                        rows(p + 1)
                    act.wait_ge(PE.sem, PE.at("turned_s", p))
                    act.wait_ge(state_out, p * 64 + 1)
                    for s in range(2):
                        AC.done(f"out_s{s}", nc.scalar.copy(orows[0:64, 1 + 4 * s:5 + 4 * s, :], bank[2 - s][0:64, :].rearrange("p (b k) -> p b k", k=P)))
                    if not final:
                        states(p + 1)
                    act.wait_ge(PE.sem, PE.at("turned_p", p))
                    AC.done("out_p", nc.scalar.copy(orows[0:64, 0, :], bank[5][0:64, 0:P]))
                    AC.turn()

                decays(0)
                root(0)
                bonus(0)
                rows(0)
                states(0)
                AC3.start(act)
                turn(0, True, False)
                with act.Fori(1, NPAIR - 1) as p:
                    turn(p, False, False)
                turn(NPAIR - 1, False, True)
                norm_root(NPAIR - 1)

            @block.gpsimd
            def _(pool):
                PL.start(pool)
                for t in (AR[:, :, NT:PAD], bT[:, NT:PAD], kT[:, NT:PAD], bE[:, NT:PAD], kE[:, NT:PAD], vP[:, NT:PAD]):
                    nc.gpsimd.memset(t, 0.0).then_inc(zeroed, 1)
                nc.gpsimd.memset(S[:, 0, :], 0.0).then_inc(zeroed, 1)
                PL2.start(pool)

                def values(p):
                    pool.wait_ge(PE2.sem, PE2.before(p))
                    settled(pool)
                    PL2.done("v", nc.gpsimd.tensor_copy(vP[:, 0:NT], z[:, ds(p + 16, 1), :].rearrange("p a t -> p (a t)")))
                    PL2.turn()

                def turn(p, final):
                    if not final:
                        values(p + 1)
                    pool.wait_ge(AC2.sem, AC2.at("tm3", p))
                    for e in range(2):
                        h = slice(64 * e, 64 * e + 64)
                        for j in range(3):
                            if j == 2:
                                pool.wait_ge(PE.sem, PE.at(f"q0_{e}", p))
                            elif e == 1:
                                pool.wait_ge(PE.sem, PE.at("q2_0", p))
                            m = chunk[:, j // 2, :].unsqueeze(2).to_broadcast([P, 8, HD])
                            for dst, q in ((Bm, 1), (Vm, 3)):
                                src = tm[:, q, j, h].unsqueeze(1).to_broadcast([P, 8, HD])
                                last = nc.gpsimd.tensor_tensor(dst[:, j % 2, :].rearrange("p (c k) -> p c k", k=HD), src, m, ALU.mult)
                            PL.done(f"m{j}_{e}", last)
                    PL.turn()

                values(0)
                with pool.Fori(0, NPAIR - 1) as p:
                    turn(p, False)
                turn(NPAIR - 1, True)

            @block.vector
            def _(dve):
                DV.start(dve)
                own = Chain(dve, sem("rw_dve_own"))
                tt = nc.vector.tensor_tensor
                dve.wait_ge(zeroed, 7)
                DV2.start(dve)

                def at_pair(x, p):
                    return x[:, ds(p, 1), :].rearrange("p a t -> p (a t)")

                def zt(p, base):
                    return at_pair(z, p + base)

                def pv(name, p):
                    return vecs[:, ds(p + VEC[name][0], 1)]

                def logs(p):
                    own(nc.vector.tensor_scalar(lw, at_pair(decay_in, p), -float(np.exp(-0.5)), None, ALU.mult))
                    own(nc.vector.tensor_tensor_scan(lg, const("reset"), lw, 0.0, ALU.mult, ALU.add))

                def logs_apart(p):
                    own(tt(before, lg, lw, ALU.subtract))
                    ep, es = ends(lg)
                    own(tt(to_end[:, 0:T].rearrange("p (c t) -> p c t", t=CH), ep.to_broadcast([P, 16, CH]), lg[:, 0:T].rearrange("p (c t) -> p c t", t=CH), ALU.subtract))
                    DV2.done("logs", tt(to_end[:, T:NT].rearrange("p (c t) -> p c t", t=TS), es.to_broadcast([P, 8, TS]), lg[:, T:NT].rearrange("p (c t) -> p c t", t=TS), ALU.subtract))

                def key(p):
                    own(nc.vector.tensor_scalar(kk0, zt(p, 8), pv("k_k", p), None, ALU.mult))
                    DV2.done("kk0sq", tt(tmp, kk0, kk0, ALU.mult))

                def key_rate(p):
                    own(nc.vector.tensor_scalar(kk, at_pair(rate, p), -1.0, pv("k_a", p), ALU.add, ALU.mult))
                    own(nc.vector.scalar_tensor_tensor(out=k2, in0=kk, scalar=1.0, in1=zt(p, 8), op0=ALU.add, op1=ALU.mult))
                    DV2.done("rkprod", nc.vector.scalar_tensor_tensor(out=rk, in0=zt(p, 0), scalar=pv("r_k", p), in1=k2, op0=ALU.mult, op1=ALU.mult))

                def clamp(p):
                    dve.wait_ge(PE2.sem, PE2.at("norms", p))
                    DV2.done("clamped", nc.vector.tensor_scalar(bb, bank[6][:, 0:NT], 1e-24, None, ALU.max))

                def invert(p):
                    dve.wait_ge(AC2.sem, AC2.at("root", p))
                    own(nc.vector.reciprocal(kk, bb))

                EARLY = {"z0_0": [logs], "z1_0": [logs_apart], "z2_0": [key], "wm1_0": [key_rate], "q1_0": [clamp]}
                LATE = (invert,
                        lambda p: own(tt(kk, kk, kk0, ALU.mult)),
                        lambda p: own(tt(bb, kk, at_pair(rate, p), ALU.mult)),
                        lambda p: own(tt(AR[:, 0, 0:NT], before, kk, ALU.mult)),
                        lambda p: own(tt(AR[:, 1, 0:NT], dec, zt(p, 0), ALU.mult)),
                        lambda p: own(tt(bT[:, 0:NT], bb, inv, ALU.mult)),
                        lambda p: own(tt(kT[:, 0:NT], k2, inv, ALU.mult)),
                        lambda p: own(tt(bE[:, 0:NT], bb, to_end, ALU.mult)),
                        lambda p: DV2.done("ready", tt(kE[:, 0:NT], k2, to_end, ALU.mult)))

                NEXT = dict(EARLY, z0_1=LATE[0:1], z1_1=LATE[1:2], z2_1=LATE[2:3], **{f"scan{c}": LATE[3 + c:4 + c] for c in range(6)})

                def prepare(after, p, final):
                    for step in () if final else NEXT.get(after, ()):
                        step(p + 1)

                def save(p):
                    dve.wait_ge(AC2.sem, AC2.at("bonus", p))
                    dve.wait_ge(DV3.sem, DV3.before(p))
                    own(tt(bonv, bon, zt(p, 16), ALU.mult))
                    ep, es = ends(dec)
                    own(nc.vector.tensor_copy(dend[:, 0:16].unsqueeze(2), ep))
                    DV.done("saved0", nc.vector.tensor_copy(dend[:, 16:24].unsqueeze(2), es))

                def norm_out(p):
                    dve.wait_ge(AC3.sem, AC3.at("lnroot", p))
                    own(nc.vector.reciprocal(yq, yq))
                    own(tt(yc, yc, yq, ALU.mult))
                    own(nc.vector.tensor_scalar(yc, yc, pv("ln_x_w", p), pv("ln_x_b", p), ALU.mult, ALU.add))
                    DV3.done("out", tt(at_pair(yT, p), yc, bonv, ALU.add))
                    DV3.turn()

                def turn(p, first, final):
                    for e in range(2):
                        h = slice(64 * e, 64 * e + 64)
                        for j in range(3):
                            dve.wait_ge(PE.sem, PE.at(f"gram{j}_{e}", p))
                            ins = tt(GM[:, j], bank[j][:, :].rearrange("p (a b) -> p a b", b=P), gram[:, j // 2], ALU.mult)
                            if j < 2:
                                own(ins)
                            else:
                                DV.done(f"gram{e}", ins)
                        dve.wait_ge(PE.sem, PE.at(f"ngram{e}", p))
                        own(tt(N0[:, 0:2], bank[7][:, 0:2 * P].rearrange("p (a b) -> p a b", b=P), nmask[:, 0:1, :].to_broadcast([P, 2, P]), ALU.mult))
                        DV.done(f"ngram{e}", tt(N0[:, 2], bank[7][:, 2 * P:3 * P], nmask[:, 1], ALU.mult))
                        dve.wait_ge(PE.sem, PE.at(f"mv{e}", p))
                        if e == 1:
                            dve.wait_ge(PE.sem, PE.at("y0", p))
                        DV.done(f"mv{e}", nc.vector.tensor_copy(Z[:, :, HD:P], bank[3][:, 0:3 * HD].rearrange("p (a b) -> p a b", b=HD)))
                        if e == 0:
                            if not first:
                                norm_out(p - 1)
                            save(p)
                        if e == 0 and not final:
                            dve.wait_ge(DV2.sem, DV2.before(p + 1))
                            dve.wait_ge(state_out, p * 64 + 1)
                        for l in LV:
                            dve.wait_ge(PE.sem, PE.at(f"apply{l}_{e}", p))
                            if l == 0:
                                dve.wait_ge(DV.sem, DV.at(f"mv{e}", p))
                                dve.wait_ge(AC.sem, AC.at(f"alpha{e}", p))
                            else:
                                dve.wait_ge(DV.sem, DV.at(f"z{l - 1}_{e}", p))
                            DV.done(f"z{l}_{e}", tt(Z, Z, bank[4][:, 0:3 * P].rearrange("p (a b) -> p a b", b=P), ALU.add))
                            prepare(f"z{l}_{e}", p, final)
                        dve.wait_ge(PE.sem, PE.at(f"rhat{e}", p))
                        DV.done(f"rhat{e}", tt(Rh[h, :], AR[h, 1, :], bank[7][h, 0:PAD], ALU.add))
                        dve.wait_ge(DV.sem, DV.at(f"z3_{e}", p))

                        def wm(j):
                            m = chunk[:, j // 2, :].unsqueeze(2).to_broadcast([P, 8, HD])
                            src = Z[:, j, HD:P].unsqueeze(1).to_broadcast([P, 8, HD])
                            DV.done(f"wm{j}_{e}", tt(Wm[:, j % 2, :].rearrange("p (c k) -> p c k", k=HD), src, m, ALU.mult))

                        def qc(j):
                            dve.wait_ge(PE.sem, PE.at(f"q{j}_{e}", p))
                            DV.done(f"q{j}_{e}", nc.vector.tensor_copy(Qc[h, 8 * j:8 * j + 8, :], bank[1 + 2 * (j % 2)][h, :].rearrange("p (c k) -> p c k", k=HD)))

                        wm(0)
                        wm(1)
                        prepare(f"wm1_{e}", p, final)
                        qc(0)
                        wm(2)
                        prepare(f"wm2_{e}", p, final)
                        qc(1)
                        prepare(f"q1_{e}", p, final)
                        qc(2)
                    dve.wait_ge(DV.sem, DV.at("q2_1", p))
                    for c in range(CH):
                        if c:
                            dve.wait_ge(DV.sem, DV.at(f"state{c - 1}", p))
                        own(nc.vector.scalar_tensor_tensor(out=S[:, c + 1, :], in0=S[:, c, :], scalar=dend[:, c:c + 1], in1=Qc[:, c, :], op0=ALU.mult, op1=ALU.add))
                        prepare(f"scan{c}", p, final)
                        if c == 9:
                            own(tt(S1, S0, dend[:, 16:24].unsqueeze(2).to_broadcast([P, DB, HD]), ALU.mult))
                        if c == 10:
                            own(tt(S1, S1, Qc[:, 16:24, :], ALU.add))
                        if c == 11:
                            dve.wait_ge(PE.sem, PE.at("sample", p))
                            DV.done("state_s", tt(S1, S1, bank[0][:, :].rearrange("p (b v) -> p b v", v=HD), ALU.add))
                        dve.wait_ge(PE.sem, PE.at(f"scan{c}", p))
                        DV.done(f"state{c}", tt(S[:, c + 1, :], S[:, c + 1, :], (bank[3] if c % 2 else bank[7])[:, 0:HD], ALU.add))
                    if not final:
                        DV2.turn()
                    dve.wait_ge(PE.sem, PE.at("read", p))
                    dve.wait_ge(AC.sem, AC.at("y1", p))
                    DV3.done("y", tt(y, y, bank[4][:, 0:NT], ALU.add))
                    dve.wait_ge(PE3.sem, PE3.at("mean", p))
                    DV3.done("centred", nc.vector.scalar_tensor_tensor(out=yc, in0=bank[6][:, 0:NT], scalar=-1.0 / HD, in1=y, op0=ALU.mult, op1=ALU.add))
                    dve.wait_ge(DV3.sem, DV3.at("centred", p))
                    DV3.done("squared", tt(yq, yc, yc, ALU.mult))
                    DV.turn()

                for steps in NEXT.values():
                    for step in steps:
                        step(0)
                DV2.turn()
                DV3.start(dve)
                turn(0, True, False)
                with dve.Fori(1, NPAIR - 1) as p:
                    own.body(p - 1, 44)
                    turn(p, False, False)
                own.end(NPAIR - 2)
                turn(NPAIR - 1, False, True)
                norm_out(NPAIR - 1)

    recurrence()
    recurrent.close()
    products = ExitStack()
    nL = low_part(products, "n_lo_merge")

    w = Carve(work, 8 * NT)
    mT = w(KD, NT)

    def merge():
        sg = w(4, NT)
        pr = w(4, NT)
        direct = [w(8, 256) for _ in range(2)]
        parts = Parts(nc, products, parts_sems, "merge", 64)
        landed = [sem(f"mg_landed{i}") for i in range(2)]
        multiplied, gated, merged = sem("mg_multiplied"), sem("mg_gated"), sem("mg_merged")
        wi = a["w_in"].rearrange("l (k p) c -> p (l k) c", p=P)[:, :, C_MERGE:]
        branch = [a[n].rearrange("l (k p) c -> p (l k) c", p=P) for n in ("w_branch_a", "w_branch_b")]
        with nc.Block() as block:
            @block.sync
            def _(sp):
                with sp.Fori(0, 8) as i:
                    for s in range(2):
                        for g in range(4 * s, 4 * s + 4):
                            k = g % 4 * 4
                            parts.load(sp, i * 8, g, wi[:, k:k + 4, ds(i * 256 + s * DM, 256)], before_dma=settled)
                        sp.wait_ge(multiplied, i * 4 + (2 * s + 2))
                        settled(sp)
                        sp.dma_start(direct[s], branch[s][:, :, ds(i * 256, 256)]).then_inc(landed[s], 16)

            @block.gpsimd
            def _(pool):
                load_low(pool, nL)

            @block.tensor
            def _(pe):
                parts.start_use(pe)
                pe.sem_inc(multiplied, 4)

                def turn(i, first):
                    for s, src in enumerate((oT, yT)):
                        pe.wait_ge(gated, i * 4 + (2 * s + 2))
                        for g in range(4 * s, 4 * s + 4):
                            if first and s == 0:
                                pe.wait_ge(low_landed[g], 32)
                            tile_pair(pe, parts, i * 8, g, bank[2 * s:2 * s + 2], nL)
                        pe.wait_ge(landed[s], i * 16 + 16)
                        for h in range(2):
                            pe.wait_ge(merged, i * 2 + (h + 1))
                            for k in range(8):
                                last = nc.tensor.matmul(bank[4 + 2 * s + h][:, 0:NT], direct[s][:, k, h * P:(h + 1) * P], src[:, k, :], start=k == 0, stop=k == 7)
                            last.then_inc(multiplied, 1)

                turn(0, True)
                with pe.Fori(1, 8) as i:
                    turn(i, False)

            @block.scalar
            def _(act):
                def gate(i, s):
                    parts.done(act, i * 8, 4 * s + 3)
                    act.wait_ge(merged, i * 2 + 2)
                    for h in range(2):
                        nc.scalar.activation(sg[:, 2 * s + h, :], bank[2 * s + h][:, 0:NT], ACT.Sigmoid).then_inc(gated, 1)

                def turn(i, first):
                    for g in range(4):
                        parts.round(act, i * 8, g)
                    if not first:
                        gate(i - 1, 1)
                    for g in range(4, 8):
                        parts.round(act, i * 8, g)
                    gate(i, 0)

                act.sem_inc(gated, 4)
                turn(0, True)
                with act.Fori(1, 8) as i:
                    turn(i, False)
                gate(7, 1)

            @block.vector
            def _(dve):
                dve.sem_inc(merged, 2)
                parts.start_split(dve)
                own = Chain(dve, sem("mg_dve"))

                def merge_turn(i):
                    own.body(i, 4)
                    for h in range(2):
                        for s in range(2):
                            dve.wait_ge(gated, i * 4 + (2 * s + h + 1 + 4))
                            dve.wait_ge(multiplied, i * 4 + (2 * s + h + 1 + 4))
                            own(nc.vector.tensor_tensor(pr[:, 2 * s + h, :], sg[:, 2 * s + h, :], bank[4 + 2 * s + h][:, 0:NT], ALU.mult))
                        nc.vector.tensor_tensor(mT[:, ds(i * 2 + h, 1), :].rearrange("p a t -> p (a t)"), pr[:, h, :], pr[:, 2 + h, :], ALU.add).then_inc(merged, 1)
                    dve.wait_ge(merged, i * 2 + 4)

                def turn(i, first):
                    for g in range(4):
                        parts.cut(dve, i * 8, g)
                    if not first:
                        merge_turn(i - 1)
                    for g in range(4, 8):
                        parts.cut(dve, i * 8, g)

                turn(0, True)
                with dve.Fori(1, 8) as i:
                    turn(i, False)
                merge_turn(7)

    merge()
    products.close()
    output = ExitStack()
    NF = DFF // P
    prev = oflat[:, 0:2 * NF * 2 * DB].rearrange("p (a b) -> p a b", b=2 * DB)
    rstd2 = oflat[:, 2 * NF * 2 * DB:2 * NF * 2 * DB + NT]

    def project_out():
        landed = [sem(f"wo_landed{i}") for i in range(4)]
        used, added = sem("wo_used"), sem("wo_added")
        squared, summed, rooted, inverted = sem("wo_squared"), sem("wo_summed"), sem("wo_rooted"), sem("wo_inverted")
        rows_in, rows_t, rows_got = sem("up_rows_in"), sem("up_rows_t"), sem("up_rows_got")
        later = output.enter_context(nc.sbuf_tensor("rows_later", [P, 24 * P], F32))
        rows = [work[0:2 * DB, 7680:11776], work[0:2 * DB, 11776:15872], later[0:2 * DB, :]]
        GROUPS = (32, 32, 24)
        v = Carve(work, 0)
        sq, rms = v(2, NT), v(NT)
        wv = a["w_out"].rearrange("l (k p) c -> p (l k) c", p=P)
        slots = output.enter_context(nc.sbuf_tensor("ring_out", [P, 4, 8, 256], F32))
        with nc.Block() as block:
            @block.sync
            def _(sp):
                with sp.Fori(0, 4) as i:
                    for c in range(4):
                        sp.wait_ge(used, i * 4 + (c + 1))
                        k = c % 2 * 8
                        sp.dma_start(slots[:, c], wv[:, k:k + 8, ds(i * 512 + c // 2 * 256, 256)]).then_inc(landed[c], 16)

            @block.tensor
            def _(pe):
                pe.sem_inc(used, 4)
                with pe.Fori(0, 4) as i:
                    for c in range(4):
                        pe.wait_ge(landed[c], i * 16 + 16)
                        for h in range(2):
                            g = c // 2 * 2 + h
                            if c % 2 == 0:
                                pe.wait_ge(added, i * 4 + (g + 1))
                            for k in range(8):
                                last = nc.tensor.matmul(bank[g][:, 0:NT], slots[:, c, k, h * P:(h + 1) * P], mT[:, c % 2 * 8 + k, :],
                                                        start=c % 2 == 0 and k == 0, stop=c % 2 == 1 and k == 7)
                        last.then_inc(used, 1)
                pe.wait_ge(rows_in, 48)
                for g, n in enumerate(GROUPS):
                    for t in range(n):
                        last = nc.tensor.transpose(bank[4 + g][:, 16 * t:16 * t + 16], rows[g][:, t * P:(t + 1) * P], ident[0:2 * DB, 0:2 * DB])
                last.then_inc(rows_t, 1)
                pe.wait_ge(added, KD + 4)
                for k in range(KD):
                    pe.wait_ge(squared, k + 1)
                    nc.tensor.matmul(bank[0][:, 0:NT], const("ones"), sq[:, k % 2, :], start=k == 0, stop=k == KD - 1).then_inc(summed, 1)

            @block.vector
            def _(dve):
                dve.sem_inc(added, 4)
                with dve.Fori(0, 4) as i:
                    for g in range(4):
                        dve.wait_ge(used, i * 4 + (2 * (g // 2) + 2 + 4))
                        x = xT[:, ds(i * 4 + g, 1), :].rearrange("p a t -> p (a t)")
                        nc.vector.tensor_tensor(x, x, bank[g][:, 0:NT], ALU.add).then_inc(added, 1)
                dve.wait_ge(added, KD + 4)
                for k in range(KD):
                    if k >= 2:
                        dve.wait_ge(summed, k - 1)
                    nc.vector.tensor_tensor(sq[:, k % 2, :], xT[:, k, :], xT[:, k, :], ALU.mult).then_inc(squared, 1)
                dve.wait_ge(rooted, 1)
                nc.vector.reciprocal(rstd2, rms).then_inc(inverted, 1)

            @block.scalar
            def _(act):
                for g, n in enumerate(GROUPS):
                    act.dma_start(rows[g], a["state_conv"].rearrange("l b w c -> (l b w) c")[:, 4096 * g:4096 * g + n * P]).then_inc(rows_in, 16)
                act.wait_ge(rows_t, 1)
                for g, n in enumerate(GROUPS):
                    nc.scalar.copy(prev[:, 32 * g:32 * g + n, :], bank[4 + g][:, 0:16 * n].rearrange("p (a b) -> p a b", b=16)).then_inc(rows_got, 1)
                act.wait_ge(summed, KD)
                nc.scalar.activation(rms, bank[0][:, 0:NT], ACT.Sqrt, bias=const("eps")[:, 0:1], scale=1.0 / DM).then_inc(rooted, 1)

    project_out()
    output.close()

    mixer.close()
    nL = sb("n_lo_ffn", [P, KD, NT], F32R)
    parts = Parts(nc, top, parts_sems, "ffn", 0)
    PART = (24, 20)
    gH = sb("g_hi", [P, PART[0], NT], F32R)
    gL = sb("g_lo", [P, PART[0], NT], F32R)
    ffn_work = sb("ffn_work", [P, 2800])
    w = Carve(ffn_work)
    UB = 2 + T + DB * (TS + 2)
    ub = w(4, UB)
    cb = w(4, NT)
    tails = w(8, 2 + 2 * DB)
    trow = oflat[:, 1408:1408 + 1024].rearrange("p (a b) -> p a b", b=512)
    zeroed, normed, halved, lowered = sem("up_zeroed"), sem("n2_normed"), sem("n2_halved"), sem("n2_lowered")
    taken, mixed, active = sem("up_taken"), sem("up_mixed"), sem("up_active")
    multiplied, high, low = sem("up_multiplied"), sem("up_high"), sem("up_low")
    kept, turned, copied, stored = sem("up_kept"), sem("up_turned"), sem("up_copied"), sem("up_stored")
    up_own = sem("up_dve_own")
    w_up, w_down = (a[n].rearrange("l (k p) c -> p (l k) c", p=P) for n in ("w_up", "w_down"))

    def up_and_conv(i0, i1):
        begin = i0 == 0
        wv = w_up
        parts.first = parts_sems["count"] - 16 * i0
        parts_sems["count"] += 16 * (i1 - i0)

        def load(sp, i, g):
            c, k = g // 4, g % 4 * 4
            parts.load(sp, i * 16, g, wv[:, k:k + 4, ds(i * 512 + ((c // 2) * 256 + (c % 2) * DFF), 256)])

        def seg(x, lo, n, width):
            base = 2 if width > TS else 0
            s = x[:, base + T:].rearrange("p (b t) -> p b t", t=width)
            return x[:, lo:lo + T], s[:, :, lo:lo + TS]

        with nc.Block() as block:
            @block.sync
            def _(sp):
                for g in range(0 if begin else 4, 16):
                    load(sp, i0, g)
                with sp.Fori(i0 + 1, i1) as i:
                    for g in range(16):
                        load(sp, i, g)
                k0 = 4 * i0
                for g in range(4):
                    parts.load(sp, i1 * 16, g, w_down[:, k0 + 4 * g:k0 + 4 * g + 4, 0:256])

            @block.tensor
            def _(pe):
                if begin:
                    pe.sem_inc(turned, 1)

                def tails_to_rows(i):
                    pe.wait_ge(kept, i * 8 + (8 + 4))
                    pe.wait_ge(copied, i * 2 + 1)
                    for s in range(2):
                        for q in range(4):
                            last = nc.tensor.transpose(bank[6 + s][0:2 + 2 * DB, q * P:(q + 1) * P], tails[:, 4 * s + q, :], ident)
                    last.then_inc(turned, 1)

                def turn(i, first):
                    for c in range(4):
                        pe.wait_ge(taken, i * 8 + (2 * c + 2))
                        for g in range(4 * c, 4 * c + 4):
                            if begin and first and c == 0:
                                pe.wait_ge(lowered, 4 * g + 4)
                            tile_pair(pe, parts, i * 16, g, bank[2 * (c % 2):2 * (c % 2) + 2], nL)
                        if c == 1 and not first:
                            tails_to_rows(i - 1)

                turn(i0, True)
                with pe.Fori(i0 + 1, i1) as i:
                    turn(i, False)
                tails_to_rows(i1 - 1)

            @block.scalar
            def _(act):
                if begin:
                    act.sem_inc(stored, 1)
                    act.sem_inc(taken, 4)
                    act.sem_inc(copied, 1)
                    norm_high(act, parts, cb, normed, halved)
                    act.wait_ge(zeroed, 1)

                def high_part(i, f):
                    for h in range(2):
                        act.wait_ge(multiplied, i * 4 + (f + h + 1))
                        nc.scalar.copy(gH[:, ds(i * 4 + (f + h - 4 * i0), 1), :], cb[:, h:h + 1, :]).then_inc(high, 1)

                def rows_out(i):
                    act.wait_ge(turned, i + 2)
                    act.wait_ge(stored, i * 64 + 1)
                    for s in range(2):
                        nc.scalar.copy(trow[0:2 + 2 * DB, s, :], bank[6 + s][0:2 + 2 * DB, :]).then_inc(copied, 1)
                    act.wait_ge(copied, i * 2 + (2 + 1))
                    for s in range(2):
                        cols = ds(i * 512 + s * DFF, 512)
                        act.dma_start(o["conv_prompt"][0, 0, :, cols], trow[0:2, s, :]).then_inc(stored, 16)
                        act.dma_start(o["conv_sample"].rearrange("l b w c -> (l b w) c")[:, cols], trow[2:2 + 2 * DB, s, :]).then_inc(stored, 16)

                def turn(i, first):
                    for c in range(4):
                        for g in range(4 * c, 4 * c + 4) if c or not (begin and first) else ():
                            parts.round(act, i * 16, g)
                        if c:
                            take_chunk(i, c - 1, first)
                        elif not first:
                            take_chunk(i - 1, 3, first)
                        if c == 2 and not first:
                            rows_out(i - 1)

                def take_chunk(i, c, first):
                    if c == 2:
                        high_part(i, 0)
                    elif c == 0 and not first:
                        high_part(i - 1, 2)
                    parts.done(act, i * 16, 4 * c + 3)
                    for g in (2 * c, 2 * c + 1):
                        f, v, u = c // 2 * 2 + g % 2, c % 2, g % 4
                        act.wait_ge(mixed, i * 8 + (g + 1))
                        act.wait_ge(kept, i * 8 + (g + 1))
                        s = ub[:, u, 2 + T:].rearrange("p (b t) -> p b t", t=TS + 2)
                        pr = prev[:, ds(i * 4 + (f + v * NF), 1), :].rearrange("p a (b j) -> p (a b) j", j=2)
                        nc.scalar.copy(s[:, :, 0:2], pr)
                        nc.scalar.copy(s[:, :, 2:], bank[u][:, T:NT].rearrange("p (b t) -> p b t", t=TS))
                        nc.scalar.copy(ub[:, u, 2:2 + T], bank[u][:, 0:T]).then_inc(taken, 1)
                    if c % 2 == 1:
                        act.wait_ge(mixed, i * 8 + (2 * c + 4))
                        for h in range(2):
                            nc.scalar.activation(cb[:, h, :], cb[:, h, :], ACT.Silu).then_inc(active, 1)

                turn(i0, True)
                with act.Fori(i0 + 1, i1) as i:
                    turn(i, False)
                take_chunk(i1 - 1, 3, False)
                rows_out(i1 - 1)
                high_part(i1 - 1, 2)
                act.wait_ge(stored, 64 * i1 + 1)

            @block.gpsimd
            def _(pool):
                if begin:
                    pool.sem_inc(kept, 4)
                    nc.gpsimd.memset(ub[:, :, 0:2], 0.0).then_inc(zeroed, 1)
                with pool.Fori(i0, i1) as i:
                    for g in range(8):
                        f, v = g // 4 * 2 + g % 2, g // 2 % 2
                        pool.wait_ge(taken, i * 8 + (g + 1 + 4))
                        pool.wait_ge(turned, i + 1)
                        settled(pool)
                        u = g % 4
                        s = ub[:, u, 2 + T:].rearrange("p (b t) -> p b t", t=TS + 2)
                        dst = tails[:, 4 * v + f, :]
                        nc.gpsimd.tensor_copy(dst[:, 0:2], ub[:, u, T:T + 2])
                        nc.gpsimd.tensor_copy(dst[:, 2:].rearrange("p (b j) -> p b j", j=2), s[:, :, TS:TS + 2]).then_inc(kept, 1)

            @block.vector
            def _(dve):
                own = Chain(dve, up_own)
                stt = nc.vector.scalar_tensor_tensor
                if begin:
                    dve.sem_inc(mixed, 4)
                    dve.sem_inc(low, 2)
                    norm_parts(dve, parts, cb, nL, "norm2_g", rstd2, normed, halved, lowered)
                    dve.wait_ge(lowered, KD)
                    dve.wait_ge(zeroed, 1)

                def low_part_of(i, f):
                    for h in range(2):
                        dve.wait_ge(high, i * 4 + (f + h + 1))
                        t = ds(i * 4 + (f + h - 4 * i0), 1)
                        nc.vector.tensor_tensor(gL[:, t, :], cb[:, h:h + 1, :], gH[:, t, :].bitcast(F32), ALU.subtract).then_inc(low, 1)

                def convolve(i, c, first):
                    if c == 2:
                        low_part_of(i, 0)
                    elif c == 0 and not first:
                        low_part_of(i - 1, 2)
                    own.body(i * 4 + c, 4)
                    for g in (2 * c, 2 * c + 1):
                        f, v, u = c // 2 * 2 + g % 2, c % 2, g % 4
                        dve.wait_ge(taken, i * 8 + (g + 1 + 4))

                        def tap(j):
                            return conv[:, j, ds(i * 4 + (f + v * NF), 1)]

                        dve.wait_ge(low, i * 4 + (c // 2 * 2 + 2))
                        cp, cs = cb[:, u, 0:T], cb[:, u, T:NT].rearrange("p (b t) -> p b t", t=TS)
                        (p0, s0), (p1, s1), (p2, s2) = (seg(ub[:, u], j, T, TS + 2) for j in range(3))
                        nc.vector.tensor_scalar(cs, s0, tap(0), tap(3), ALU.mult, ALU.add)
                        own(nc.vector.tensor_scalar(cp, p0, tap(0), tap(3), ALU.mult, ALU.add))
                        stt(out=cs, in0=s1, scalar=tap(1), in1=cs, op0=ALU.mult, op1=ALU.add)
                        own(stt(out=cp, in0=p1, scalar=tap(1), in1=cp, op0=ALU.mult, op1=ALU.add))
                        stt(out=cs, in0=s2, scalar=tap(2), in1=cs, op0=ALU.mult, op1=ALU.add)
                        stt(out=cp, in0=p2, scalar=tap(2), in1=cp, op0=ALU.mult, op1=ALU.add).then_inc(mixed, 1)
                    if c % 2 == 1:
                        dve.wait_ge(mixed, i * 8 + (2 * c + 2 + 4))
                        for h in range(2):
                            f = c // 2 * 2 + h
                            dve.wait_ge(active, i * 4 + (f + 1))
                            nc.vector.tensor_tensor(cb[:, h, :], cb[:, h, :], cb[:, 2 + h, :], ALU.mult).then_inc(multiplied, 1)

                def turn(i, first):
                    for c in range(4):
                        for g in range(4 * c, 4 * c + 4) if c or not (begin and first) else ():
                            parts.cut(dve, i * 16, g)
                        if c:
                            convolve(i, c - 1, first)
                        elif not first:
                            convolve(i - 1, 3, first)

                turn(i0, True)
                with dve.Fori(i0 + 1, i1) as i:
                    turn(i, False)
                convolve(i1 - 1, 3, False)
                low_part_of(i1 - 1, 2)

    def down(part, per_turn, turns):
        final = part == 1
        KG = PART[part] // 4
        K0 = PART[0] * part
        added = sem(f"dn_added{part}")
        if final:
            rows_t, rows_got, y_out = sem("dn_rows_t"), sem("dn_rows_got"), sem("dn_y_out")
        yo = oT[:, 0:4, :]
        yrow = Carve(ffn_work)(2, 3, 256)
        parts.first = parts_sems["count"]
        parts_sems["count"] += KG * 8
        N = KG * per_turn
        with nc.Block() as block:
            @block.sync
            def _(sp):
                def load(i, g):
                    k = K0 + g % KG * 4
                    parts.load(sp, i * N, g, w_down[:, k:k + 4, ds(i * (per_turn * 256) + g // KG * 256, 256)])

                for g in range(4, N):
                    load(0, g)
                with sp.Fori(1, turns) as i:
                    for g in range(N):
                        load(i, g)
                if not final:
                    for g in range(4):
                        parts.load(sp, 8 * KG, g, w_up[:, 4 * g:4 * g + 4, 128 * PART[0]:128 * PART[0] + 256])

            @block.tensor
            def _(pe):
                if final:
                    pe.sem_inc(rows_t, 4)

                def to_rows(i, c):
                    for h in range(2):
                        pe.wait_ge(added, i * (2 * per_turn) + (2 * c + h + 1 + 4))
                        pe.wait_ge(rows_got, i * (4 * per_turn) + (4 * c + 2 * h + 2))
                        for t, (t0, n) in enumerate(TOK):
                            last = nc.tensor.transpose(bank[4 + 2 * (c % 2) + h][0:n, t * P:(t + 1) * P], yo[:, 2 * (c % 2) + h, t0:t0 + n], ident)
                        last.then_inc(rows_t, 1)

                def turn(i, first):
                    for c in range(per_turn):
                        pe.wait_ge(added, i * (2 * per_turn) + (2 * c + 2))
                        for q in range(KG):
                            g = c * KG + q
                            parts.ready(pe, i * N, g)
                            for h in range(2):
                                for kk in range(4):
                                    k = 4 * q + kk
                                    cols = slice(h * P, (h + 1) * P)
                                    last = three_passes(bank[2 * (c % 2) + h][:, 0:NT], parts.hi[:, g % 4, kk, cols], parts.lo[:, g % 4, kk, cols],
                                                        gH[:, k, :], gL[:, k, :], True, k == 0, k == 4 * KG - 1)
                            last.then_inc(parts.used, 1)
                        if final:
                            if c:
                                to_rows(i, c - 1)
                            elif not first:
                                to_rows(i - 1, per_turn - 1)

                turn(0, True)
                with pe.Fori(1, turns) as i:
                    turn(i, False)
                if final:
                    to_rows(turns - 1, per_turn - 1)

            @block.scalar
            def _(act):
                def out(i, c):
                    u = c % 2
                    act.wait_ge(y_out, i * (48 * per_turn) + (48 * c + 48))
                    for h in range(2):
                        act.wait_ge(rows_t, i * (2 * per_turn) + (2 * c + h + 1 + 4))
                        b = bank[4 + 2 * u + h]
                        nc.scalar.copy(yrow[:, u, 0:2, h * P:(h + 1) * P], b[:, 0:256].rearrange("p (a b) -> p a b", b=P)).then_inc(rows_got, 1)
                        nc.scalar.copy(yrow[0:64, u, 2, h * P:(h + 1) * P], b[0:64, 256:384]).then_inc(rows_got, 1)
                    act.wait_ge(rows_got, i * (4 * per_turn) + (4 * c + 4 + 8))
                    cols = ds(i * (256 * per_turn) + c * 256, 256)
                    for t, (t0, n) in enumerate(TOK):
                        dst = o["y_prompt"][0, t0:t0 + n, cols] if t < 2 else o["y_sample"].rearrange("b t d -> (b t) d")[:, cols]
                        act.dma_start(dst, yrow[0:n, u, t, :]).then_inc(y_out, 16)

                def turn(i, first):
                    for c in range(per_turn):
                        for g in range(c * KG, (c + 1) * KG):
                            parts.round(act, i * N, g)
                        if final and (c >= 2 or not first):
                            out(i if c >= 2 else i - 1, c - 2 if c >= 2 else per_turn + c - 2)

                if final:
                    act.sem_inc(rows_got, 8)
                    act.sem_inc(y_out, 48)
                turn(0, True)
                with act.Fori(1, turns) as i:
                    turn(i, False)
                if final:
                    out(turns - 1, per_turn - 2)
                    out(turns - 1, per_turn - 1)
                    act.wait_ge(y_out, 48 * 8 + 48)

            @block.vector
            def _(dve):
                dve.sem_inc(added, 4)

                def add(i, c):
                    parts.done(dve, i * N, (c + 1) * KG - 1)
                    for h in range(2):
                        x = xT[:, ds(i * (2 * per_turn) + (2 * c + h), 1), :].rearrange("p a t -> p (a t)")
                        dst = x
                        if final:
                            dst = yo[:, 2 * (c % 2) + h, :]
                            dve.wait_ge(rows_t, i * (2 * per_turn) + (2 * c + h + 1))
                        nc.vector.tensor_tensor(dst, x, bank[2 * (c % 2) + h][:, 0:NT], ALU.add).then_inc(added, 1)

                def turn(i, first):
                    for c in range(per_turn):
                        for g in range(c * KG, (c + 1) * KG):
                            parts.cut(dve, i * N, g)
                        if c:
                            add(i, c - 1)
                        elif not first:
                            add(i - 1, per_turn - 1)

                turn(0, True)
                with dve.Fori(1, turns) as i:
                    turn(i, False)
                add(turns - 1, per_turn - 1)

    up_and_conv(0, PART[0] // 4)
    down(0, 2, 4)
    up_and_conv(PART[0] // 4, NF // 4)
    down(1, 4, 2)


INPUTS = ["x_prompt", "x_sample", "cache_kv_cmp", "cache_kv_sel", "page_table", "cache_kv_win", "state_wkv",
          "state_shift", "state_conv", "norm1_g", "w_in", "q_gain", "k_gains", "w_cmp", "mu_shift", "w0", "w_lora_w",
          "a0", "w_lora_a", "k_k", "k_a", "r_k", "ln_x_w", "ln_x_b", "w_branch_a", "w_branch_b", "w_out", "norm2_g",
          "w_up", "conv_w", "conv_b", "w_down"]
OUTPUTS = [("y_prompt", (1, T, DM)), ("y_sample", (DB, TS, DM)),
           ("kv_cmp_prompt", (1, 1, T, 2, NKV, HD)), ("kv_cmp_sample", (1, DB, TS, 2, NKV, HD)),
           ("kv_sel_prompt", (1, 1, T, 2, NKV, HD)), ("kv_sel_sample", (1, DB, TS, 2, NKV, HD)),
           ("kv_win_prompt", (1, 1, T, 2, NKV, HD)), ("kv_win_sample", (1, DB, WIN, 2, NKV, HD)),
           ("wkv_prompt", (1, 1, NH, HD, HD)), ("wkv_sample", (1, DB, NH, HD, HD)),
           ("shift_prompt", (1, 1, SHIFT)), ("shift_sample", (1, DB, SHIFT)),
           ("conv_prompt", (1, 1, 2, 2 * DFF)), ("conv_sample", (1, DB, 2, 2 * DFF))]


def kernel(**inputs):
    import concourse.bacc as bacc
    from concourse.bass_utils import run_bass_kernel_spmd

    nc = bacc.Bacc("TRN2", target_bir_lowering=False, num_devices=1)
    arrays = {name: np.ascontiguousarray(inputs[name]) for name in INPUTS}
    arrays["shape_constants"] = shape_constants()
    a = {n: nc.dram_tensor(n, v.shape, mybir.dt.from_np(v.dtype), kind="ExternalInput").ap() for n, v in arrays.items()}
    o = {n: nc.dram_tensor("out_" + n, shape, F32, kind="ExternalOutput").ap() for n, shape in OUTPUTS}
    build_layer(nc, a, o)
    got = run_bass_kernel_spmd(nc, [arrays], core_ids=[0]).results[0]
    return tuple(got["out_" + n] for n, _ in OUTPUTS)
```
